# Optimizing a Trainium2 kernel written in Bass

```python
import jax, jax.numpy as jnp
from jax import lax
import numpy as np

D_MODEL = 2048
BATCH = 1
SEQ = 256
DEPTH = 1

CHUNK = 64
EPS = 1e-6
D_LRU = 1024
LRU_BLOCKS = 16
LRU_BLOCK = D_LRU // LRU_BLOCKS
CONV_W = 4
LRU_C = 8.0
N_HEADS = 16
N_KV = 4
Q_PER_KV = N_HEADS // N_KV
HEAD_DIM = 64
D_ATTN = N_HEADS * HEAD_DIM
D_KV = N_KV * HEAD_DIM
WINDOW = 128
WIN_CHUNKS = WINDOW // CHUNK
ROT_DIM = HEAD_DIM // 4
ROPE_THETA = 500000.0
D_IN = 2 * D_LRU + D_ATTN + 2 * D_KV
D_MIX = D_LRU + D_ATTN
N_GROUPS = 4
EXPERTS_PER_GROUP = 8
N_EXPERTS = N_GROUPS * EXPERTS_PER_GROUP
TOP_K = 2
D_EXPERT = 512
D_PLE = 256

kernel_name = "hymba_rglru_swa_hiermoe_block"

F32 = jnp.float32
NEG = -1e30

def rmsnorm(x, g):
    xf = x.astype(F32)
    y = xf * lax.rsqrt(jnp.mean(xf * xf, axis=-1, keepdims=True) + EPS) * g.astype(F32)
    return y.astype(x.dtype)

def causal_conv(x, w, b):
    c = x.shape[-1]
    y = lax.conv_general_dilated(x, w.reshape(CONV_W, 1, c).astype(x.dtype), window_strides=(1,),
                                 padding=[(CONV_W - 1, 0)], dimension_numbers=('NWC', 'WIO', 'NWC'),
                                 feature_group_count=c)
    return y + b.astype(x.dtype)

def rg_lru(xc, w_a, b_a, w_i, b_i, lam):
    bsz, s, _ = xc.shape
    xb = xc.reshape(bsz, s, LRU_BLOCKS, LRU_BLOCK)
    r = jax.nn.sigmoid(jnp.einsum('bshi,hij->bshj', xb, w_a).reshape(bsz, s, D_LRU).astype(F32) + b_a.astype(F32))
    i = jax.nn.sigmoid(jnp.einsum('bshi,hij->bshj', xb, w_i).reshape(bsz, s, D_LRU).astype(F32) + b_i.astype(F32))
    log_a = -LRU_C * r * jax.nn.softplus(-lam.astype(F32))
    a = jnp.exp(log_a)
    u = jnp.sqrt(-jnp.expm1(2.0 * log_a)) * (i * xc.astype(F32))

    def combine(left, right):
        a1, b1 = left
        a2, b2 = right
        return a1 * a2, a2 * b1 + b2

    _, h = lax.associative_scan(combine, (a, u), axis=1)
    return h.astype(xc.dtype)

def partial_rope(x, positions):
    half = ROT_DIM // 2
    inv_freq = ROPE_THETA ** (-jnp.arange(0, ROT_DIM, 2, dtype=F32) / ROT_DIM)
    ang = positions.astype(F32)[..., None] * inv_freq
    cos = jnp.cos(ang)[:, :, None, :].astype(x.dtype)
    sin = jnp.sin(ang)[:, :, None, :].astype(x.dtype)
    x1, x2, rest = x[..., :half], x[..., half:ROT_DIM], x[..., ROT_DIM:]
    return jnp.concatenate([x1 * cos - x2 * sin, x2 * cos + x1 * sin, rest], axis=-1)

def shift_chunks(t, j):
    if j == 0:
        return t
    pad = jnp.zeros_like(t[:, :j])
    return jnp.concatenate([pad, t[:, :-j]], axis=1)

def swa_sink_attention(q, k, v, sinks):
    bsz, s = q.shape[0], q.shape[1]
    nc = s // CHUNK
    qc = q.reshape(bsz, nc, CHUNK, N_KV, Q_PER_KV, HEAD_DIM)
    kc = k.reshape(bsz, nc, CHUNK, N_KV, HEAD_DIM)
    vc = v.reshape(bsz, nc, CHUNK, N_KV, HEAD_DIM)
    offs = list(range(WIN_CHUNKS - 1, -1, -1))
    kk = jnp.concatenate([shift_chunks(kc, j) for j in offs], axis=2)
    vv = jnp.concatenate([shift_chunks(vc, j) for j in offs], axis=2)
    key_off = jnp.repeat(jnp.array(offs, dtype=jnp.int32), CHUNK)
    valid = (jnp.arange(nc, dtype=jnp.int32)[:, None] - key_off[None, :]) >= 0
    valid = valid[None, :, None, None, None, :]
    scores = jnp.einsum('bnqhgd,bnkhd->bnhgqk', qc, kk).astype(F32) * (HEAD_DIM ** -0.5)
    scores = jnp.where(valid, scores, NEG)
    sink = jnp.broadcast_to(sinks.astype(F32).reshape(1, 1, N_KV, Q_PER_KV, 1, 1), scores.shape[:-1] + (1,))
    probs = jax.nn.softmax(jnp.concatenate([scores, sink], axis=-1), axis=-1)[..., :-1]
    out = jnp.einsum('bnhgqk,bnkhd->bnqhgd', probs.astype(v.dtype), vv)
    return out.reshape(bsz, s, D_ATTN)

def hier_moe(xn, w_rg, b_rg, w_re, b_re, w1, w3, w2):
    bsz, s, d = xn.shape
    t = xn.reshape(bsz * s, d)
    n = t.shape[0]
    g_probs = jax.nn.softmax((t @ w_rg).astype(F32) + b_rg.astype(F32), axis=-1)
    g_w, g_idx = lax.top_k(g_probs, 1)
    e_logits = ((t @ w_re).astype(F32) + b_re.astype(F32)).reshape(n, N_GROUPS, EXPERTS_PER_GROUP)
    e_logits = jnp.take_along_axis(e_logits, g_idx[:, :, None], axis=1)[:, 0]
    e_top, e_idx = lax.top_k(e_logits, TOP_K)
    weights = g_w * jax.nn.softmax(e_top, axis=-1)
    expert_id = g_idx * EXPERTS_PER_GROUP + e_idx
    combine = jnp.sum(jax.nn.one_hot(expert_id, N_EXPERTS, dtype=F32) * weights[..., None], axis=1)
    out = jnp.zeros((n, d), F32)
    for e in range(N_EXPERTS):
        hdn = jax.nn.silu(t @ w1[e]) * (t @ w3[e])
        out = out + combine[:, e:e + 1] * (hdn @ w2[e]).astype(F32)
    return out.reshape(bsz, s, d).astype(xn.dtype)

def setup_inputs(seed: int = 0) -> dict:
    key = jax.random.key(seed)
    ks = iter(jax.random.split(key, 40))
    nrm = lambda shape, scale: jax.random.normal(next(ks), shape, F32) * scale
    gain = lambda shape: 1.0 + 0.02 * jax.random.normal(next(ks), shape, F32)
    a0 = jax.random.uniform(next(ks), (DEPTH, D_LRU), F32, 0.9, 0.999)
    return {
        "x": nrm((BATCH, SEQ, D_MODEL), 1.0),
        "p": nrm((DEPTH, BATCH, SEQ, D_PLE), 1.0),
        "positions": jnp.broadcast_to(jnp.arange(SEQ, dtype=jnp.int32), (BATCH, SEQ)),
        "g_mix": gain((DEPTH, D_MODEL)),
        "w_in": nrm((DEPTH, D_MODEL, D_IN), D_MODEL ** -0.5),
        "conv_w": nrm((DEPTH, CONV_W, D_LRU), CONV_W ** -0.5),
        "conv_b": nrm((DEPTH, D_LRU), 0.01),
        "w_a": nrm((DEPTH, LRU_BLOCKS, LRU_BLOCK, LRU_BLOCK), LRU_BLOCK ** -0.5),
        "b_a": nrm((DEPTH, D_LRU), 0.01),
        "w_i": nrm((DEPTH, LRU_BLOCKS, LRU_BLOCK, LRU_BLOCK), LRU_BLOCK ** -0.5),
        "b_i": nrm((DEPTH, D_LRU), 0.01),
        "lam": jnp.log(a0) - jnp.log1p(-a0),
        "g_q": gain((DEPTH, HEAD_DIM)),
        "g_k": gain((DEPTH, HEAD_DIM)),
        "sinks": nrm((DEPTH, N_HEADS), 0.5),
        "g_out_lru": gain((DEPTH, D_LRU)),
        "g_out_attn": gain((DEPTH, D_ATTN)),
        "w_out": nrm((DEPTH, D_MIX, D_MODEL), D_MIX ** -0.5),
        "g_moe": gain((DEPTH, D_MODEL)),
        "w_rg": nrm((DEPTH, D_MODEL, N_GROUPS), D_MODEL ** -0.5),
        "b_rg": nrm((DEPTH, N_GROUPS), 0.01),
        "w_re": nrm((DEPTH, D_MODEL, N_EXPERTS), D_MODEL ** -0.5),
        "b_re": nrm((DEPTH, N_EXPERTS), 0.01),
        "w1": nrm((DEPTH, N_EXPERTS, D_MODEL, D_EXPERT), D_MODEL ** -0.5),
        "w3": nrm((DEPTH, N_EXPERTS, D_MODEL, D_EXPERT), D_MODEL ** -0.5),
        "w2": nrm((DEPTH, N_EXPERTS, D_EXPERT, D_MODEL), D_EXPERT ** -0.5),
        "w_ple": nrm((DEPTH, D_PLE, D_MODEL), D_PLE ** -0.5),
        "g_ple": gain((DEPTH, D_MODEL)),
        "g_pg": gain((DEPTH, D_MODEL)),
        "w_pg": nrm((DEPTH, D_MODEL, D_MODEL), D_MODEL ** -0.5),
        "b_pg": nrm((DEPTH, D_MODEL), 0.01),
    }

def reference(x, p, positions, g_mix, w_in, conv_w, conv_b, w_a, b_a, w_i, b_i, lam, g_q, g_k, sinks,
              g_out_lru, g_out_attn, w_out, g_moe, w_rg, b_rg, w_re, b_re, w1, w3, w2,
              w_ple, g_ple, g_pg, w_pg, b_pg):
    bsz, s, _ = x.shape
    h = x
    splits = [D_LRU, 2 * D_LRU, 2 * D_LRU + D_ATTN, 2 * D_LRU + D_ATTN + D_KV]
    for i in range(DEPTH):
        xn = rmsnorm(h, g_mix[i])
        z = xn @ w_in[i]
        x_lru, gate_lru, q, k, v = jnp.split(z, splits, axis=-1)
        xc = causal_conv(x_lru, conv_w[i], conv_b[i])
        y_lru = rg_lru(xc, w_a[i], b_a[i], w_i[i], b_i[i], lam[i]) * jax.nn.gelu(gate_lru)
        q = partial_rope(rmsnorm(q.reshape(bsz, s, N_HEADS, HEAD_DIM), g_q[i]), positions)
        k = partial_rope(rmsnorm(k.reshape(bsz, s, N_KV, HEAD_DIM), g_k[i]), positions)
        v = v.reshape(bsz, s, N_KV, HEAD_DIM)
        y_attn = swa_sink_attention(q, k, v, sinks[i])
        y = jnp.concatenate([rmsnorm(y_lru, g_out_lru[i]), rmsnorm(y_attn, g_out_attn[i])], axis=-1)
        h = h + y @ w_out[i]
        h = h + hier_moe(rmsnorm(h, g_moe[i]), w_rg[i], b_rg[i], w_re[i], b_re[i], w1[i], w3[i], w2[i])
        pe = rmsnorm(p[i] @ w_ple[i], g_ple[i])
        gate = jax.nn.sigmoid((rmsnorm(h, g_pg[i]) @ w_pg[i]).astype(F32) + b_pg[i].astype(F32))
        h = h + (gate * pe.astype(F32)).astype(h.dtype)
    return h


_drawn_inputs = setup_inputs


def setup_inputs(seed=0):
    import zlib

    import numpy as np

    out = dict(_drawn_inputs(seed))
    spreads = {}
    factors = {'b_a': 29.883,
     'b_i': 8.0,
     'g_k': 2.997,
     'sinks': 42.88,
     'g_out_lru': 12.336,
     'g_out_attn': 11.025,
     'b_rg': 26.94,
     'b_re': 42.716,
     'g_ple': 138.18,
     'g_pg': 67.175,
     'b_pg': 136.864,
     'g_moe': 6.461}
    for name, (base, spread) in spreads.items():
        noise = np.random.default_rng([zlib.crc32(name.encode()), seed]).standard_normal(out[name].shape)
        drawn = base * np.exp(spread * noise) if base else spread * noise
        out[name] = __import__('jax').numpy.asarray(drawn.astype(out[name].dtype))
    for name, factor in factors.items():
        out[name] = (out[name] * factor).astype(out[name].dtype)
    return out
```

```python
import math
from contextlib import ExitStack

import numpy as np

import concourse.bass as bass
from concourse import mybir

P = 128
ALU = mybir.AluOpType
ACT = mybir.ActivationFunctionType
F32 = mybir.dt.float32
I32 = mybir.dt.int32
AX = mybir.AxisListType.X

T, D = 256, 2048
NT = T // P
KD = D // P
CHUNK = 64
EPS = 1e-6
D_LRU, CB = 1024, 8
CONV_W = 4
HEADS, KV, HD = 16, 4, 64
QK = HEADS + KV
ROT = HD // 4
HALF = ROT // 2
THETA = 500000.0
GROUPS, PER_GROUP = 4, 8
NE = GROUPS * PER_GROUP
D_EXP = 512
D_PLE = 256
NEG = -1e30
NL = GROUPS + NE

RING = 12
CH = 2048
WIN_ORDER = [0, 1, 4, 5, 6, 2, 3]
FRONT_CHUNKS = 4 * len(WIN_ORDER) + 16
EXPERT_CHUNKS = 12
ROUND_CHUNKS = NE * EXPERT_CHUNKS
PLE_CHUNKS = 2
TAIL_CHUNKS = PLE_CHUNKS + 16
SLOTS = 64
ROUNDS = T // SLOTS
assert ROUND_CHUNKS % RING == 0 and 2 * EXPERT_CHUNKS % RING == 0

TWO_PI_1 = 6.28125
TWO_PI_2 = math.floor((2 * math.pi - TWO_PI_1) * 2 ** 17) / 2 ** 17
TWO_PI_3 = math.floor((2 * math.pi - TWO_PI_1 - TWO_PI_2) * 2 ** 27) / 2 ** 27
TWO_PI_4 = 2 * math.pi - TWO_PI_1 - TWO_PI_2 - TWO_PI_3
ROUND_MAGIC = 1.5 * 2 ** 23
PI_BELOW = 3.1415925


def front_uses(slot):
    return FRONT_CHUNKS // RING + (slot < FRONT_CHUNKS % RING)


def build(nc, x, p, positions, g_mix, w_in, conv_w, conv_b, w_a, b_a, w_i, b_i, lam, g_q, g_k, sinks,
          g_out_lru, g_out_attn, w_out, g_moe, w_rg, b_rg, w_re, b_re, w1, w3, w2,
          w_ple, g_ple, g_pg, w_pg, b_pg, out):
    with ExitStack() as ctx:
        def sb(name, shape, dt=F32):
            return ctx.enter_context(nc.sbuf_tensor(name, shape, dt))

        def sem(name):
            return ctx.enter_context(nc.semaphore(name))

        ring = sb("ring", [P, RING, CH])
        h = sb("h", [P, NT, D])
        hs = sb("hs", [P, NT, KD, P])
        hT = sb("hT", [P, KD, T])
        area = sb("area", [P, 15128])
        ident = sb("ident", [P, P])
        prmT = sb("prmT", [P, 80])
        gains = sb("gains", [P, 3, KD])
        gqk = sb("gqk", [P, 2, HD])
        sink_bc = sb("sink_bc", [P, HEADS])
        br_bc = sb("br_bc", [P, NL])
        wrg = sb("wrg", [P, KD, GROUPS])
        expo = sb("expo", [P, QK])
        ones_c = sb("ones_c", [P, 2])
        ss = sb("ss", [P, 8])
        rstd = sb("rstd", [P, 8])
        ssq = sb("ssq", [P, NT, QK])
        rqk = sb("rqk", [P, NT, QK])
        stat = sb("stat", [P, 6, HEADS])
        rounds_i = sb("rounds_i", [1, 1], I32)
        pos_i = sb("pos_i", [P, NT], I32)
        sp = sb("sp", [P, 6, CB])
        trig = sb("trig", [P, 2, NT, HALF])

        def part(lo, n, *dims):
            v = area[:, lo:lo + n]
            if len(dims) == 2:
                return v.rearrange("p (a b) -> p a b", a=dims[0])
            if len(dims) == 3:
                return v.rearrange("p (a b c) -> p a b c", a=dims[0], b=dims[1])
            if len(dims) == 4:
                return v.rearrange("p (a b c d) -> p a b c d", a=dims[0], b=dims[1], c=dims[2])
            return v

        xl = part(0, CB * (T + 3), CB, T + 3)
        xl_flat = part(0, CB * T, CB, T)
        xc = part(2072, CB * T, CB, T)
        t1 = part(4120, CB * T, CB, T)
        t2 = part(6168, CB * T, CB, T)
        gt = part(8216, CB * T, CB, T)
        qk = part(10264, NT * QK * HD, NT, QK, HD)
        yat = part(10264, NT * HEADS * HD, NT, HEADS, HD)
        wre = part(12312, KD * NE, KD, NE)
        v = part(12824, NT * KV * HD, NT, KV, HD)
        vs = part(13336, NT * KV * HD, NT, KV, HD)
        kT = part(13848, KV * T, KV, T)
        sqk = part(13848, QK * HD, QK, HD)
        rope = part(13848, 4 * QK * HALF, 4, QK, HALF)
        prm = part(13848, P)
        angles = part(14000, 6 * NT * HALF, 6, NT, HALF)
        hs_flat = hs[:, :, :, :].rearrange("p t k m -> p (t k m)")
        hT_flat = hT[:, :, :].rearrange("p k t -> p (k t)")
        bd = hs_flat[:, 0:2048].rearrange("p (w c j) -> p w c j", w=2, c=CB)
        S = [hs_flat[:, 0:2048].rearrange("p (h k) -> p h k", h=HEADS),
             hT_flat[:, 2048:4096].rearrange("p (h k) -> p h k", h=HEADS)]
        qT = hs_flat[:, 2048:4096].rearrange("p (j t) -> p j t", j=CB)
        PT = hT_flat[:, 0:2048].rearrange("p (h q) -> p h q", h=HEADS)
        yT = hT_flat[:, 2048:4096].rearrange("p (c t) -> p c t", c=CB)
        junk = hT[:, :, :].rearrange("p (a k) t -> p a (k t)", a=NT)
        XG = part(0, 2 * KD * SLOTS, 2, KD, SLOTS)
        H13 = part(2048, D_EXP, 4, P)
        SL = part(2560, 256, 4, SLOTS)
        HDN = part(2816, 256, 4, SLOTS)
        Y = part(3072, 2048, 2, 2, 512)
        SEL = part(5120, 512, 2, NT, 2 * SLOTS)
        G = part(5632, 512, 2, NT, P)
        before = part(6144, P)
        ones = part(6272, P)
        route = part(6400, 10 * NT * NE, 10, NT, NE)
        lg = part(7040, NT * NL, NT, NL)
        rcol = part(7120, 12 * NT, 12, NT)
        idx = part(7200, NE)
        rankm = sb("rankm", [P, NT, NE + 1])
        comb = sb("comb", [P, NT, NE + 1])
        slot_ids = sb("slot_ids", [P, 2 * SLOTS])
        pe = part(6144, NT * D, NT, D)
        gple = part(10240, D)
        bpg = part(12288, D)
        pp = part(14336, NT * D_PLE, NT, D_PLE)
        pT = part(0, 512, 2, T)
        junk2 = part(512, 8 * 512, 8, 512)
        z = part(3072, 2048, 4, 512)

        ps = ctx.enter_context(nc.psum_tensor("ps", [P, 8, 512], F32))

        x_loaded = [sem(f"x_loaded{t}") for t in range(NT)]
        prm_loaded, small_loaded, bd_loaded = sem("prm_loaded"), sem("small_loaded"), sem("bd_loaded")
        wre_loaded, end_loaded = sem("wre_loaded"), sem("end_loaded")
        loaded = [sem(f"loaded{s}") for s in range(RING)]
        tail_loaded = [sem(f"tail_loaded{s}") for s in range(RING)]
        chunks_used, tail_used = sem("chunks_used"), sem("tail_used")
        consts_ready = sem("consts_ready")
        pool_step, dve_step, act_step = sem("pool_step"), sem("dve_step"), sem("act_step")
        prm_ps, prm_ready = sem("prm_ps"), sem("prm_ready")
        ss_ready, ms_ready, rstd_ready = sem("ss_ready"), sem("ms_ready"), sem("rstd_ready")
        hs_act, hs_dve, hT_ps, hT_act, hT_dve = sem("hs_act"), sem("hs_dve"), sem("hT_ps"), sem("hT_act"), sem("hT_dve")
        xl_ready, qkv_ready, gelu_ready = sem("xl_ready"), sem("qkv_ready"), sem("gelu_ready")
        bd_zero, xl_pad, xc_ready = sem("bd_zero"), sem("xl_pad"), sem("xc_ready")
        gates_ps, gates_ready, tanh_ready, sqrt_ready = sem("gates_ps"), sem("gates_ready"), sem("tanh_ready"), sem("sqrt_ready")
        recip_done, y_lru, ysq_ready, yg_ready = sem("recip_done"), sem("y_lru"), sem("ysq_ready"), sem("yg_ready")
        lam_exp, lam_sum, lam_ln = sem("lam_exp"), sem("lam_sum"), sem("lam_ln")
        lam_ready = sem("lam_ready")
        ang_ready, trig_ready = sem("ang_ready"), sem("trig_ready")
        qsq_ready, qms_ready, qr_ready, qk_ready, sqk_free = (
            sem("qsq_ready"), sem("qms_ready"), sem("qr_ready"), sem("qk_ready"), sem("sqk_free"))
        qT_ps, qT_ready, kT_ps, kT_ready = sem("qT_ps"), sem("qT_ready"), sem("kT_ps"), sem("kT_ready")
        s_masked, scores_ps, S_ready, shifted, exp_ready = (
            sem("s_masked"), sem("scores_ps"), sem("S_ready"), sem("shifted"), sem("exp_ready"))
        sink_shifted, sink_exp = sem("sink_shifted"), sem("sink_exp")
        PT_ps, PT_act, PT_dve, pv_ps, yat_ready = sem("PT_ps"), sem("PT_act"), sem("PT_dve"), sem("pv_ps"), sem("yat_ready")
        yT_ps, yT_act, yT_dve = sem("yT_ps"), sem("yT_act"), sem("yT_dve")
        ssB_ready, ssA_ps, msAB_ready, rAB_ready = sem("ssB_ready"), sem("ssA_ps"), sem("msAB_ready"), sem("rAB_ready")
        h_ready = sem("h_ready")
        logits_ps, gmax_ready, gexp_ready, e_diff, e_exp = (
            sem("logits_ps"), sem("gmax_ready"), sem("gexp_ready"), sem("e_diff"), sem("e_exp"))
        chosen_ready, rank_ps, rounds_ready = sem("chosen_ready"), sem("rank_ps"), sem("rounds_ready")
        moe_zero, route_consts = sem("moe_zero"), sem("route_consts")
        sel_ready, gather_ps, xg_ready, h13_ready = (
            sem("sel_ready"), sem("gather_ps"), sem("xg_ready"), sem("h13_ready"))
        g_ps, g_ready, h13T_ps, silu_ready, hdn_ready = (
            sem("g_ps"), sem("g_ready"), sem("h13T_ps"), sem("silu_ready"), sem("hdn_ready"))
        y_ready, scatter_ps, acc_done, moe_done = (
            sem("y_ready"), sem("scatter_ps"), sem("acc_done"), sem("moe_done"))
        pT_ps, pT_ready, ssp_ready, msp_ready, rp_ready, pe_ready = (
            sem("pT_ps"), sem("pT_ready"), sem("ssp_ready"), sem("msp_ready"),
            sem("rp_ready"), sem("pe_ready"))
        z_ready, gate_ready, out_ready, out_stored = (
            sem("z_ready"), sem("gate_ready"), sem("out_ready"), [sem(f"out_stored{u}") for u in range(4)])

        x_v = x[0].rearrange("(t p) d -> p t d", p=P)
        out_v = out[0].rearrange("(t p) d -> p t d", p=P)
        p_v = p[0, 0].rearrange("(t p) c -> p t c", p=P)
        w_in_v = w_in[0].rearrange("(p k) n -> p k n", k=KD)
        w_out_v = w_out[0].rearrange("(c p) n -> p c n", p=P)
        w_pg_v = w_pg[0].rearrange("(p k) n -> p k n", k=KD)
        w_ple_v = w_ple[0].rearrange("(c p) n -> p c n", p=P)
        w1_v = w1[0].rearrange("e (p k) f -> e p k f", k=KD)
        w3_v = w3[0].rearrange("e (p k) f -> e p k f", k=KD)
        w2_v = w2[0].rearrange("e (p k) n -> e p k n", k=4)

        def ring4(slot):
            return ring[:, slot, :].rearrange("p (k n) -> p k n", k=4)

        block = ctx.enter_context(nc.Block())

        @block.sync
        def _(sp_q):
            for t in range(NT):
                sp_q.dma_start(h[:, t, :], x_v[:, t, :]).then_inc(x_loaded[t], 16)

            c = 0
            for g in WIN_ORDER:
                for kq in range(4):
                    if c >= RING:
                        sp_q.wait_ge(chunks_used, c - RING + 1)
                    sp_q.dma_start(ring4(c % RING), w_in_v[:, 4 * kq:4 * kq + 4, 512 * g:512 * g + 512]
                                   ).then_inc(loaded[c % RING], 16)
                    c += 1
            for n in range(4):
                for cq in range(4):
                    sp_q.wait_ge(chunks_used, c - RING + 1)
                    sp_q.dma_start(ring4(c % RING), w_out_v[:, 4 * cq:4 * cq + 4, 512 * n:512 * n + 512]
                                   ).then_inc(loaded[c % RING], 16)
                    c += 1

            def expert_round(used):
                with sp_q.Fori(0, NE // 2) as i:
                    for b in range(2):
                        e = bass.ds(i * 2 + b, 1)
                        for j in range(EXPERT_CHUNKS):
                            at = EXPERT_CHUNKS * b + j
                            slot = (FRONT_CHUNKS + at) % RING
                            sp_q.wait_ge(chunks_used, i * (2 * EXPERT_CHUNKS) + (used + at - RING + 1))
                            if j < 8:
                                src = (w1_v if j % 2 == 0 else w3_v)[e, :, 4 * (j // 2):4 * (j // 2) + 4, :]
                                src = src.rearrange("a p k f -> p (a k) f")
                                dst = ring4(slot)
                            else:
                                src = w2_v[e, :, j - 8, :].rearrange("a p n -> p (a n)")
                                dst = ring[:, slot, :]
                            sp_q.dma_start(dst, src).then_inc(loaded[slot], 16)

            expert_round(FRONT_CHUNKS)
            sp_q.wait_ge(rounds_ready, 1)
            rounds = sp_q.value_load(rounds_i[0:1, 0:1], min_val=1, max_val=ROUNDS)
            with sp_q.If(rounds > 1):
                with sp_q.Fori(1, rounds) as r:
                    expert_round(r * ROUND_CHUNKS + FRONT_CHUNKS)
                sp_q.nop()
            with sp_q.Else():
                sp_q.nop()
            for c in range(TAIL_CHUNKS):
                slot = (FRONT_CHUNKS + c) % RING
                if c < RING:
                    sp_q.wait_ge(chunks_used, rounds * ROUND_CHUNKS + (FRONT_CHUNKS + c - RING + 1))
                else:
                    sp_q.wait_ge(tail_used, c - RING + 1)
                if c < PLE_CHUNKS:
                    sp_q.dma_start(ring[:, slot, :], w_ple_v[:, c, :]).then_inc(tail_loaded[slot], 16)
                else:
                    n, kq = divmod(c - PLE_CHUNKS, 4)
                    sp_q.dma_start(ring4(slot), w_pg_v[:, 4 * kq:4 * kq + 4, 512 * n:512 * n + 512]
                                   ).then_inc(tail_loaded[slot], 16)
            for u in range(2 * 4):
                n, t = divmod(u, NT)
                sp_q.wait_ge(out_ready, u + 1)
                sp_q.dma_start(out_v[:, t, 512 * n:512 * n + 512], z[:, u % 4, :]).then_inc(out_stored[u % 4], 16)
            for u in range(4):
                sp_q.wait_ge(out_stored[u], 16 * 2)

        @block.gpsimd
        def _(pool):
            steps = [0]

            def step(ins):
                steps[0] += 1
                ins.then_inc(pool_step, 1)
                pool.wait_ge(pool_step, steps[0])

            step(pool.memset(ident[:, :], 0.0))
            pool.affine_select(out=ident[:, :], in_=ident[:, :], compare_op=ALU.not_equal, fill=1.0, base=0,
                               pattern=[[-1, P]], channel_multiplier=1).then_inc(consts_ready, 1)
            pool.memset(ones_c[:, :], 1.0)
            pool.memset(expo[:, :], -0.5).then_inc(consts_ready, 1)
            pool.memset(xl[:, :, 0:3], 0.0).then_inc(xl_pad, 1)
            pool.memset(vs[0:64, 0, :, :], 0.0).then_inc(xl_pad, 1)
            pool.wait_ge(consts_ready, 2)

            def norm_root(j):
                pool.wait_ge(ms_ready, j + 1)
                pool.tensor_tensor(rstd[:, 0:NT], ss[:, 2:2 + NT], expo[:, 0:NT], ALU.pow).then_inc(rstd_ready, 1)

            norm_root(0)
            pool.wait_ge(hT_ps, 8)
            pool.memset(bd[:, :, :, :], 0.0).then_inc(bd_zero, 1)
            pool.wait_ge(bd_zero, 1)
            for w, src in enumerate((w_a, w_i)):
                for half in range(2):
                    pool.dma_start(bd[64 * half:64 * half + 64, w, :, 64 * half:64 * half + 64],
                                   src[0, half:2 * CB:2, :, :].rearrange("c i j -> i c j")).then_inc(bd_loaded, 16)
            for t in range(NT):
                pool.wait_ge(qms_ready, t + 1)
                pool.tensor_tensor(rqk[:, t, :], ssq[:, t, :], expo[:, :], ALU.pow).then_inc(qr_ready, 1)
            pool.wait_ge(gates_ready, CB)
            pool.memset(S[0][0:64, :, 0:64], NEG).then_inc(s_masked, 1)
            pool.wait_ge(ysq_ready, 1)
            for c in range(CB):
                pool.tensor_scalar(gt[:, c, :], gt[:, c, :], prmT[:, 64 + c:65 + c], None, ALU.mult
                                   ).then_inc(yg_ready, 1)
            pool.wait_ge(msAB_ready, 1)
            pool.tensor_tensor(rstd[:, 4:8], ss[:, 4:8], expo[:, 0:4], ALU.pow).then_inc(rAB_ready, 1)
            pool.wait_ge(yat_ready, 1)
            pool.dma_start(wre, w_re[0].rearrange("(p k) e -> p k e", k=KD)).then_inc(wre_loaded, 16)
            pool.wait_ge(chunks_used, FRONT_CHUNKS)
            pool.memset(Y[:, 1, :, :], 0.0).then_inc(moe_zero, 1)
            pool.memset(G[:, 1, :, :], 0.0).then_inc(moe_zero, 1)
            step(pool.memset(ones, 1.0))
            pool.affine_select(out=before, in_=ones, compare_op=ALU.is_gt, fill=0.0, base=0,
                               pattern=[[1, P]], channel_multiplier=-1).then_inc(route_consts, 1)
            pool.iota(slot_ids[:, :].rearrange("p (a s) -> p a s", a=2), [[0, 2], [1, SLOTS]], base=0,
                      channel_multiplier=0, allow_small_or_imprecise_dtypes=True).then_inc(route_consts, 1)
            pool.iota(idx, [[1, NE]], base=0, channel_multiplier=0,
                      allow_small_or_imprecise_dtypes=True).then_inc(route_consts, 1)
            pool.memset(comb[:, :, 0:1], 0.0).then_inc(route_consts, 1)
            pool.memset(rankm[:, :, NE:NE + 1], -1.0).then_inc(route_consts, 1)
            norm_root(1)
            pool.wait_ge(rounds_ready, 1)
            pool.dma_start(gple, g_ple.partition_broadcast(P).rearrange("p a d -> p (a d)")).then_inc(end_loaded, 16)
            pool.dma_start(bpg, b_pg.partition_broadcast(P).rearrange("p a d -> p (a d)")).then_inc(end_loaded, 16)
            pool.dma_start(pp, p_v).then_inc(end_loaded, 16)
            pool.wait_ge(msp_ready, 1)
            pool.tensor_tensor(rstd[:, 4:6], ss[:, 4:6], expo[:, 0:2], ALU.pow).then_inc(rp_ready, 1)
            norm_root(2)

        @block.scalar
        def _(act):
            a_steps = [0]

            def step(ins):
                a_steps[0] += 1
                ins.then_inc(act_step, 1)
                act.wait_ge(act_step, a_steps[0])

            rows = [(conv_w[0], 32, True), (conv_b, 8, False), (b_a, 8, False), (b_i, 8, False), (lam, 8, False),
                    (g_out_lru, 8, False), (g_out_attn, 8, False)]
            at = 0
            for src, n, taps in rows:
                view = src.rearrange("j (c p) -> (j c) p", p=P)
                act.dma_start(prm[at:at + n, :], view).then_inc(prm_loaded, 16)
                at += n
            for j, g in enumerate((g_mix, g_moe, g_pg)):
                act.dma_start(gains[:, j, :], g[0].rearrange("(p k) -> p k", k=KD)).then_inc(small_loaded, 16)
            act.dma_start(gqk[:, 0, :], g_q.partition_broadcast(P).rearrange("p a d -> p (a d)")).then_inc(small_loaded, 16)
            act.dma_start(gqk[:, 1, :], g_k.partition_broadcast(P).rearrange("p a d -> p (a d)")).then_inc(small_loaded, 16)
            act.dma_start(sink_bc[:, :], sinks.partition_broadcast(P).rearrange("p a d -> p (a d)")).then_inc(small_loaded, 16)
            act.dma_start(br_bc[:, 0:GROUPS], b_rg.partition_broadcast(P).rearrange("p a d -> p (a d)")).then_inc(small_loaded, 16)
            act.dma_start(br_bc[:, GROUPS:NL], b_re.partition_broadcast(P).rearrange("p a d -> p (a d)")).then_inc(small_loaded, 16)
            act.dma_start(pos_i[:, :], positions[0].rearrange("(t p) -> p t", p=P),
                          allow_slow_non_contiguous=True).then_inc(small_loaded, 16)
            act.dma_start(wrg[:, :, :], w_rg[0].rearrange("(p k) g -> p k g", k=KD)).then_inc(small_loaded, 16)

            def norm(j, ready):
                for t in range(NT):
                    ready(t)
                    act.activation(junk[:, t, :], h[:, t, :], ACT.Square, accum_out=ss[:, t:t + 1]).then_inc(ss_ready, 1)
                act.wait_ge(rstd_ready, j + 1)
                act.activation(hs[:, 0, :, :], h[:, 0, :].rearrange("p (m k) -> p k m", k=KD), ACT.Copy,
                               scale=rstd[:, 0:1]).then_inc(hs_act, 1)
                act.wait_ge(small_loaded, 160)
                for b in range(0, 8, 2):
                    act.wait_ge(hT_ps, 8 * j + b + 1)
                    for u in range(2):
                        k = 2 * b + u
                        act.activation(hT[:, k, :], ps[:, b, T * u:T * u + T], ACT.Copy, scale=gains[:, j, k:k + 1]
                                       ).then_inc(hT_act, 1)
                    k = None

            norm(0, lambda t: act.wait_ge(x_loaded[t], 16))
            act.wait_ge(lam_sum, 1)
            act.activation(sp[:, 1, :], sp[:, 0, :], ACT.Exp).then_inc(lam_exp, 1)
            act.wait_ge(lam_sum, 2)
            act.activation(sp[:, 3, :], sp[:, 2, :], ACT.Ln).then_inc(lam_ln, 1)
            act.wait_ge(ang_ready, 1)
            act.activation(trig[:, :, :, :], angles[:, 0:2, :, :], ACT.Sin).then_inc(trig_ready, 1)
            for g in range(2):
                act.wait_ge(chunks_used, 4 * (g + 1))
                for cb in range(4):
                    ins = act.activation(xl[:, 4 * g + cb, 3:3 + T], ps[:, 4 * g + cb, 0:T], ACT.Copy)
                ins.then_inc(xl_ready, 1)
            for g in range(2):
                act.wait_ge(chunks_used, 4 * (g + 3))
                for t in range(NT):
                    ins = act.activation(qk[:, t, 8 * g:8 * g + 8, :], ps[:, 2 * g + t, :].rearrange("p (h d) -> p h d", h=8), ACT.Copy)
                ins.then_inc(qkv_ready, 1)
            act.wait_ge(chunks_used, 4 * 5)
            act.wait_ge(xl_pad, 2)
            for t in range(NT):
                act.activation(qk[:, t, HEADS:QK, :], ps[:, 4 + t, 0:256].rearrange("p (h d) -> p h d", h=KV), ACT.Copy)
                act.activation(v[:, t, :, :], ps[:, 4 + t, 256:512].rearrange("p (h d) -> p h d", h=KV), ACT.Copy)
            act.activation(vs[64:128, 0, :, :], ps[0:64, 4, 256:512].rearrange("p (h d) -> p h d", h=KV), ACT.Copy)
            act.activation(vs[0:64, 1, :, :], ps[64:128, 4, 256:512].rearrange("p (h d) -> p h d", h=KV), ACT.Copy)
            act.activation(vs[64:128, 1, :, :], ps[0:64, 5, 256:512].rearrange("p (h d) -> p h d", h=KV), ACT.Copy
                           ).then_inc(qkv_ready, 1)
            for t in range(NT):
                act.wait_ge(qkv_ready, 3)
                if t:
                    act.wait_ge(sqk_free, t)
                act.activation(sqk[:, :, :], qk[:, t, :, :], ACT.Square).then_inc(qsq_ready, 1)
            act.wait_ge(prm_ready, 1)
            for c in range(CB):
                act.wait_ge(gates_ps, c + 1)
                act.activation(t1[:, c, :], ps[:, 6 + c % 2, 0:T], ACT.Sigmoid, bias=prmT[:, 40 + c:41 + c])
                act.activation(t2[:, c, :], ps[:, 6 + c % 2, T:2 * T], ACT.Sigmoid, bias=prmT[:, 48 + c:49 + c]
                               ).then_inc(gates_ready, 1)
            act.wait_ge(gates_ready, CB)
            act.wait_ge(lam_ready, 1)
            for c in range(CB):
                ins = act.activation(t1[:, c, :], t1[:, c, :], ACT.Tanh, scale=sp[:, 5, c:c + 1])
            ins.then_inc(tanh_ready, 1)
            act.wait_ge(recip_done, 1)
            act.activation(t1[:, :, :], t1[:, :, :], ACT.Sqrt).then_inc(sqrt_ready, 1)
            act.wait_ge(chunks_used, 4 * 6)
            for cb in range(4):
                ins = act.activation(gt[:, cb, :], ps[:, cb, 0:T], ACT.Gelu_apprx_tanh)
            ins.then_inc(gelu_ready, 1)
            for t in range(NT):
                act.wait_ge(qT_ps, t + 1)
                for g in range(2):
                    ins = act.activation(qT[:, 4 * g:4 * g + 4, P * t:P * t + P],
                                         ps[:, 4 + g, :].rearrange("p (j q) -> p j q", j=4), ACT.Copy)
                ins.then_inc(qT_ready, 1)
            act.wait_ge(chunks_used, 4 * 7)
            for cb in range(4):
                ins = act.activation(gt[:, 4 + cb, :], ps[:, cb, 0:T], ACT.Gelu_apprx_tanh)
            ins.then_inc(gelu_ready, 1)
            for t in range(NT):
                base = 4 * (1 - t)
                act.wait_ge(scores_ps, t + 1)
                for b in range(4):
                    src = ps[:, base + b, :].rearrange("p (j k) -> p j k", j=4)
                    dst = S[t].rearrange("p (g j two) k -> p g two j k", g=2, two=2)[:, b // 2, b % 2, :, :]
                    if t == 0:
                        act.activation(dst[64:128], src[64:128], ACT.Copy, scale=HD ** -0.5)
                        ins = act.activation(dst[0:64, :, 64:128], src[0:64, :, 64:128], ACT.Copy, scale=HD ** -0.5)
                    else:
                        ins = act.activation(dst, src, ACT.Copy, scale=HD ** -0.5)
                ins.then_inc(S_ready, 1)
            for t in range(NT):
                act.wait_ge(shifted, t + 1)
                act.activation(S[t], S[t], ACT.Exp).then_inc(exp_ready, 1)
                act.wait_ge(sink_shifted, t + 1)
                act.activation(stat[:, 3 * t + 1, :], stat[:, 3 * t + 1, :], ACT.Exp).then_inc(sink_exp, 1)
            act.wait_ge(y_lru, 1)
            act.activation(t1[:, :, :], gt[:, :, :], ACT.Square).then_inc(ysq_ready, 1)
            for t in range(NT):
                act.wait_ge(PT_ps, t + 1)
                if t:
                    act.wait_ge(pv_ps, t)
                for b in range(2):
                    ins = act.activation(PT[:, 4 * b:4 * b + 4, :], ps[:, 4 + b, :].rearrange("p (j q) -> p j q", j=4), ACT.Copy)
                ins.then_inc(PT_act, 1)
            for t in range(NT):
                act.wait_ge(yat_ready, t + 1)
                act.activation(t2[:, 4 * t:4 * t + 4, :].rearrange("p c q -> p (c q)"),
                               yat[:, t, :, :].rearrange("p h d -> p (h d)"), ACT.Square,
                               accum_out=ss[:, 6 + t:7 + t]).then_inc(ssB_ready, 1)
            act.wait_ge(yT_ps, 1)
            for c in range(4):
                act.activation(yT[:, c, :], ps[:, 4 + c // 2, T * (c % 2):T * (c % 2) + T], ACT.Copy,
                               scale=prmT[:, 72 + c:73 + c]).then_inc(yT_act, 1)

            norm(1, lambda t: act.wait_ge(h_ready, 4))
            act.wait_ge(gmax_ready, 1)
            act.activation(lg[:, :, 0:GROUPS], lg[:, :, 0:GROUPS], ACT.Exp).then_inc(gexp_ready, 1)
            act.wait_ge(e_diff, 1)
            act.activation(rcol[:, 4, :], rcol[:, 3, :], ACT.Exp).then_inc(e_exp, 1)

            def expert_round(n0):
                with act.Fori(0, NE // 2) as i:
                    for b in range(2):
                        done = i * 2 + (n0 + b + 1)
                        act.wait_ge(chunks_used, (i * 2 + (n0 + b)) * EXPERT_CHUNKS + (FRONT_CHUNKS + 8))
                        act.activation(H13, ps[:, 0, :].rearrange("p (m k) -> p k m", k=4), ACT.Copy).then_inc(h13_ready, 1)
                        act.wait_ge(g_ps, done)
                        act.activation(G[:, b, :, :], ps[:, 6, 0:T].rearrange("p (t q) -> p t q", t=NT), ACT.Copy
                                       ).then_inc(g_ready, 1)
                        act.wait_ge(h13T_ps, done)
                        act.activation(SL, ps[:, 5, :].rearrange("p (k s) -> p k s", k=4)[:, :, 0:SLOTS], ACT.Silu
                                       ).then_inc(silu_ready, 1)
                        act.wait_ge(chunks_used, done * EXPERT_CHUNKS + FRONT_CHUNKS)
                        for u in range(2):
                            ins = act.activation(Y[:, b, u, :], ps[:, 3 + u, :], ACT.Copy)
                        ins.then_inc(y_ready, 1)

            act.wait_ge(moe_zero, 2)
            expert_round(0)
            act.wait_ge(rounds_ready, 1)
            rounds = act.value_load(rounds_i[0:1, 0:1], min_val=1, max_val=ROUNDS)
            with act.If(rounds > 1):
                with act.Fori(1, rounds) as r:
                    expert_round(r * NE)
                act.nop()
            with act.Else():
                act.nop()
            act.wait_ge(pT_ps, 1)
            act.activation(pT, ps[:, 0, :].rearrange("p (c t) -> p c t", c=2), ACT.Copy).then_inc(pT_ready, 1)
            act.wait_ge(tail_used, PLE_CHUNKS)
            for t in range(NT):
                for n in range(4):
                    ins = act.activation(junk2[:, 4 * t + n, :], ps[:, 2 * n + t, :], ACT.Square,
                                         accum_out=stat[:, t, n:n + 1])
            ins.then_inc(ssp_ready, 1)
            norm(2, lambda t: act.wait_ge(moe_done, 1))
            for u in range(2 * 4):
                act.wait_ge(z_ready, u + 1)
                act.activation(z[:, u % 4, :], z[:, u % 4, :], ACT.Sigmoid).then_inc(gate_ready, 1)

        @block.vector
        def _(dve):
            steps = [0]

            def step(ins):
                steps[0] += 1
                ins.then_inc(dve_step, 1)
                dve.wait_ge(dve_step, steps[0])

            def norm(j):
                dve.wait_ge(ss_ready, 2 * (j + 1))
                dve.tensor_scalar(ss[:, 2:2 + NT], ss[:, 0:NT], 1.0 / D, EPS, ALU.mult, ALU.add).then_inc(ms_ready, 1)
                dve.wait_ge(rstd_ready, j + 1)
                dve.tensor_scalar(hs[:, 1, :, :], h[:, 1, :].rearrange("p (m k) -> p k m", k=KD), rstd[:, 1:2], None,
                                  ALU.mult).then_inc(hs_dve, 1)
                for b in range(1, 8, 2):
                    dve.wait_ge(hT_ps, 8 * j + b + 1)
                    for u in range(2):
                        k = 2 * b + u
                        dve.tensor_scalar(hT[:, k, :], ps[:, b, T * u:T * u + T], gains[:, j, k:k + 1], None,
                                          ALU.mult).then_inc(hT_dve, 1)

            dve.wait_ge(small_loaded, 160)
            dve.wait_ge(prm_ps, 1)
            step(dve.tensor_copy(prmT[:, :], ps[:, 0, 0:80]))
            dve.tensor_scalar(sp[:, 4, :], prmT[:, 56:64], -1.0, 0.0, ALU.mult, ALU.max).then_inc(prm_ready, 1)
            dve.wait_ge(prm_ready, 1)
            step(dve.tensor_scalar(sp[:, 5, :], prmT[:, 56:64], 0.0, None, ALU.min))
            dve.scalar_tensor_tensor(out=sp[:, 0, :], in0=sp[:, 5, :], scalar=2.0, in1=prmT[:, 56:64],
                                     op0=ALU.mult, op1=ALU.subtract).then_inc(lam_sum, 1)
            norm(0)
            dve.wait_ge(lam_exp, 1)
            dve.tensor_scalar(sp[:, 2, :], sp[:, 1, :], 1.0, None, ALU.add).then_inc(lam_sum, 1)
            dve.wait_ge(lam_sum, 2)
            dve.wait_ge(lam_ln, 1)
            step(dve.tensor_scalar(sp[:, 5, :], sp[:, 2, :], 1.0, None, ALU.is_equal))
            step(dve.scalar_tensor_tensor(out=sp[:, 2, :], in0=sp[:, 2, :], scalar=-1.0, in1=sp[:, 5, :],
                                          op0=ALU.add, op1=ALU.add))
            step(dve.reciprocal(sp[:, 2, :], sp[:, 2, :]))
            step(dve.tensor_tensor(sp[:, 3, :], sp[:, 3, :], sp[:, 2, :], ALU.mult))
            step(dve.tensor_tensor(sp[:, 3, :], sp[:, 3, :], sp[:, 5, :], ALU.add))
            step(dve.tensor_tensor(sp[:, 3, :], sp[:, 3, :], sp[:, 1, :], ALU.mult))
            step(dve.tensor_tensor(sp[:, 5, :], sp[:, 3, :], sp[:, 4, :], ALU.add))
            dve.tensor_scalar(sp[:, 5, :], sp[:, 5, :], 4.0, None, ALU.mult).then_inc(lam_ready, 1)
            step(dve.tensor_copy(rstd[:, 2:4], pos_i[:, :]))
            for f in range(HALF):
                ins = dve.tensor_scalar(angles[:, 2, :, f], rstd[:, 2:4],
                                        float(np.float32(THETA) ** np.float32(-2.0 * f / ROT)), None, ALU.mult)
            step(ins)
            step(dve.tensor_scalar(angles[:, 3, :, :], angles[:, 2, :, :], 1 / (2 * math.pi), None, ALU.mult))
            step(dve.tensor_scalar(angles[:, 3, :, :], angles[:, 3, :, :], ROUND_MAGIC, None, ALU.add))
            step(dve.tensor_scalar(angles[:, 3, :, :], angles[:, 3, :, :], -ROUND_MAGIC, None, ALU.add))
            for cpi in (TWO_PI_1, TWO_PI_2, TWO_PI_3, TWO_PI_4):
                step(dve.scalar_tensor_tensor(out=angles[:, 2, :, :], in0=angles[:, 3, :, :], scalar=-cpi,
                                              in1=angles[:, 2, :, :], op0=ALU.mult, op1=ALU.add))
            step(dve.tensor_scalar(angles[:, 0, :, :], angles[:, 2, :, :], PI_BELOW, -PI_BELOW, ALU.min, ALU.max))
            step(dve.scalar_tensor_tensor(out=angles[:, 4, :, :], in0=angles[:, 0, :, :], scalar=-1.0,
                                          in1=angles[:, 0, :, :], op0=ALU.mult, op1=ALU.max))
            dve.tensor_scalar(angles[:, 1, :, :], angles[:, 4, :, :], -1.0, math.pi / 2, ALU.mult, ALU.add
                              ).then_inc(ang_ready, 1)

            dve.wait_ge(xl_pad, 1)
            dve.wait_ge(xl_ready, 2)
            for j in range(CONV_W):
                for c in range(CB):
                    tap = prmT[:, 8 * j + c:8 * j + c + 1]
                    if j == 0:
                        ins = dve.tensor_scalar(xc[:, c, :], xl[:, c, 0:T], tap, prmT[:, 32 + c:33 + c], ALU.mult, ALU.add)
                    else:
                        ins = dve.scalar_tensor_tensor(out=xc[:, c, :], in0=xl[:, c, j:j + T], scalar=tap,
                                                       in1=xc[:, c, :], op0=ALU.mult, op1=ALU.add)
                if j < CONV_W - 1:
                    step(ins)
            ins.then_inc(xc_ready, 1)

            for t in range(NT):
                dve.wait_ge(qsq_ready, t + 1)
                step(dve.tensor_reduce(ssq[:, t, :], sqk[:, :, :], AX, ALU.add))
                dve.tensor_scalar(ssq[:, t, :], ssq[:, t, :], 1.0 / HD, EPS, ALU.mult, ALU.add).then_inc(qms_ready, 1)
                dve.wait_ge(qr_ready, t + 1)
                q_ = qk[:, t, :, :]
                step(dve.tensor_tensor(q_, q_, rqk[:, t, :].unsqueeze(2).to_broadcast([P, QK, HD]), ALU.mult))
                for w, (lo, n) in enumerate(((0, HEADS), (HEADS, KV))):
                    ins = dve.tensor_tensor(qk[:, t, lo:lo + n, :], qk[:, t, lo:lo + n, :],
                                            gqk[:, w, :].unsqueeze(1).to_broadcast([P, n, HD]), ALU.mult)
                step(ins)
                if t == 0:
                    dve.wait_ge(trig_ready, 1)
                sin = trig[:, 0, t, :].unsqueeze(1).to_broadcast([P, QK, HALF])
                cos = trig[:, 1, t, :].unsqueeze(1).to_broadcast([P, QK, HALF])
                a_, b_ = qk[:, t, :, 0:HALF], qk[:, t, :, HALF:ROT]
                dve.tensor_tensor(rope[:, 0, :, :], a_, cos, ALU.mult)
                dve.tensor_tensor(rope[:, 1, :, :], b_, sin, ALU.mult)
                dve.tensor_tensor(rope[:, 2, :, :], b_, cos, ALU.mult)
                step(dve.tensor_tensor(rope[:, 3, :, :], a_, sin, ALU.mult))
                dve.tensor_tensor(a_, rope[:, 0, :, :], rope[:, 1, :, :], ALU.subtract)
                if t == 0:
                    step(dve.tensor_tensor(b_, rope[:, 2, :, :], rope[:, 3, :, :], ALU.add))
                    dve.nop().then_inc(sqk_free, 1)
                else:
                    dve.tensor_tensor(b_, rope[:, 2, :, :], rope[:, 3, :, :], ALU.add).then_inc(qk_ready, 1)

            dve.wait_ge(gates_ready, CB)
            dve.tensor_tensor(t2, t2, xc, ALU.mult)
            dve.wait_ge(tanh_ready, 1)
            step(dve.tensor_scalar(xl_flat, t1, 1.0, None, ALU.add))
            dve.reciprocal(xl_flat, xl_flat).then_inc(recip_done, 1)
            dve.wait_ge(recip_done, 1)
            dve.tensor_scalar(xc, xl_flat, 2.0, -1.0, ALU.mult, ALU.add)
            dve.wait_ge(sqrt_ready, 1)
            step(dve.scalar_tensor_tensor(out=xl_flat, in0=t1, scalar=2.0, in1=xl_flat, op0=ALU.mult, op1=ALU.mult))
            step(dve.tensor_tensor(t2, t2, xl_flat, ALU.mult))
            for c in range(CB):
                ins = dve.tensor_tensor_scan(xl_flat[:, c, :], xc[:, c, :], t2[:, c, :], 0.0, ALU.mult, ALU.add)
            step(ins)
            for t in range(NT):
                dve.wait_ge(kT_ps, t + 1)
                dve.tensor_copy(kT[:, :, P * t:P * t + P], ps[:, 6 + t, :].rearrange("p (g q) -> p g q", g=KV)
                                ).then_inc(kT_ready, 1)
            dve.wait_ge(gelu_ready, 2)
            dve.tensor_tensor(gt, gt, xl_flat, ALU.mult).then_inc(y_lru, 1)

            dve.wait_ge(s_masked, 1)
            for t in range(NT):
                dve.wait_ge(S_ready, t + 1)
                mx, sk = stat[:, 3 * t, :], stat[:, 3 * t + 1, :]
                step(dve.tensor_reduce(mx, S[t], AX, ALU.max))
                step(dve.tensor_tensor(mx, mx, sink_bc[:, :], ALU.max))
                dve.tensor_tensor(S[t], S[t], mx.unsqueeze(2).to_broadcast([P, HEADS, P]), ALU.subtract).then_inc(shifted, 1)
                dve.tensor_tensor(sk, sink_bc[:, :], mx, ALU.subtract).then_inc(sink_shifted, 1)
            for t in range(NT):
                den = stat[:, 3 * t + 2, :]
                dve.wait_ge(exp_ready, t + 1)
                step(dve.tensor_reduce(den, S[t], AX, ALU.add))
                dve.wait_ge(sink_exp, t + 1)
                step(dve.tensor_tensor(den, den, stat[:, 3 * t + 1, :], ALU.add))
                step(dve.reciprocal(den, den))
                dve.wait_ge(PT_ps, t + 1)
                if t:
                    dve.wait_ge(pv_ps, t)
                for b in range(2, 4):
                    ins = dve.tensor_copy(PT[:, 4 * b:4 * b + 4, :], ps[:, 4 + b, :].rearrange("p (j q) -> p j q", j=4))
                ins.then_inc(PT_dve, 1)
                dve.wait_ge(pv_ps, t + 1)
                for b in range(2):
                    ins = dve.tensor_tensor(yat[:, t, 8 * b:8 * b + 8, :],
                                            ps[:, 2 * t + b, :].rearrange("p (h d) -> p h d", h=8),
                                            den[:, 8 * b:8 * b + 8].unsqueeze(2).to_broadcast([P, 8, HD]), ALU.mult)
                ins.then_inc(yat_ready, 1)
            dve.wait_ge(ssA_ps, 1)
            dve.wait_ge(ssB_ready, 2)
            dve.tensor_scalar(ss[:, 4:6], ps[:, 0, 0:NT], 1.0 / D_LRU, EPS, ALU.mult, ALU.add)
            dve.tensor_scalar(ss[:, 6:8], ss[:, 6:8], 1.0 / (HEADS * HD), EPS, ALU.mult, ALU.add).then_inc(msAB_ready, 1)
            dve.wait_ge(yT_ps, 1)
            for c in range(4, CB):
                dve.tensor_scalar(yT[:, c, :], ps[:, 4 + c // 2, T * (c % 2):T * (c % 2) + T],
                                  prmT[:, 72 + c:73 + c], None, ALU.mult).then_inc(yT_dve, 1)
            dve.wait_ge(rAB_ready, 1)
            for n in range(4):
                dve.wait_ge(chunks_used, 4 * (len(WIN_ORDER) + n + 1))
                for m in range(2):
                    for t in range(NT):
                        piece = h[:, t, 512 * n:512 * n + 512]
                        ins = dve.scalar_tensor_tensor(out=piece, in0=ps[:, 4 * (n % 2) + 2 * m + t, :],
                                                       scalar=rstd[:, 4 + 2 * m + t:5 + 2 * m + t], in1=piece,
                                                       op0=ALU.mult, op1=ALU.add)
                    if m == 0:
                        step(ins)
                ins.then_inc(h_ready, 1)

            norm(1)
            gl, el = lg[:, :, 0:GROUPS], route[:, 0, :, :]
            dve.wait_ge(route_consts, 5)
            dve.wait_ge(logits_ps, 1)
            for t in range(NT):
                ins = dve.tensor_tensor(lg[:, t, :], ps[:, t, 0:NL], br_bc[:, :], ALU.add)
            step(ins)

            def col(n):
                return rcol[:, n, :]

            def wide(c, n):
                return c.unsqueeze(2).to_broadcast([P, NT, n])

            def first_of(hot, logits, top, n, s0, s1):
                step(dve.tensor_tensor(hot, logits, wide(top, n), ALU.is_equal))
                ids = idx[:, 0:n].unsqueeze(1).to_broadcast([P, NT, n])
                step(dve.scalar_tensor_tensor(out=s0, in0=hot, scalar=-1000.0, in1=ids, op0=ALU.mult, op1=ALU.add))
                step(dve.tensor_reduce(s1, s0, AX, ALU.min))
                step(dve.tensor_tensor(hot, s0, wide(s1, n), ALU.is_equal))

            ghot = route[:, 1, :, 0:GROUPS]
            step(dve.tensor_reduce(col(0), gl, AX, ALU.max))
            first_of(ghot, gl, col(0), GROUPS, route[:, 2, :, 0:GROUPS], col(1))
            dve.tensor_tensor(gl, gl, wide(col(0), GROUPS), ALU.subtract).then_inc(gmax_ready, 1)
            gh = ghot.unsqueeze(3).to_broadcast([P, NT, GROUPS, PER_GROUP])

            def by_group(a):
                return a.rearrange("p t (g e) -> p t g e", g=GROUPS)

            for t in range(NT):
                ins = dve.tensor_tensor(by_group(el)[:, t], by_group(lg[:, :, GROUPS:NL])[:, t], gh[:, t], ALU.mult)
            step(ins)
            step(dve.tensor_scalar(route[:, 3, :, 0:GROUPS], ghot, -1.0, -NEG, ALU.add, ALU.mult))
            gn = route[:, 3, :, 0:GROUPS].unsqueeze(3).to_broadcast([P, NT, GROUPS, PER_GROUP])
            for t in range(NT):
                ins = dve.tensor_tensor(by_group(el)[:, t], by_group(el)[:, t], gn[:, t], ALU.add)
            step(ins)
            hot1, hot2 = route[:, 4, :, :], route[:, 5, :, :]
            step(dve.tensor_reduce(col(1), el, AX, ALU.max))
            first_of(hot1, el, col(1), NE, route[:, 6, :, :], col(5))
            step(dve.scalar_tensor_tensor(out=el, in0=hot1, scalar=10 * NEG, in1=el, op0=ALU.mult, op1=ALU.add))
            step(dve.tensor_reduce(col(2), el, AX, ALU.max))
            first_of(hot2, el, col(2), NE, route[:, 6, :, :], col(5))
            chosen = route[:, 7, :, :]
            dve.tensor_tensor(chosen, hot1, hot2, ALU.add).then_inc(chosen_ready, 1)
            dve.tensor_tensor(col(3), col(2), col(1), ALU.subtract).then_inc(e_diff, 1)
            dve.wait_ge(gexp_ready, 1)
            step(dve.tensor_reduce(col(6), gl, AX, ALU.add))
            dve.wait_ge(e_exp, 1)
            step(dve.tensor_scalar(col(7), col(4), 1.0, None, ALU.add))
            step(dve.tensor_tensor(col(6), col(6), col(7), ALU.mult))
            step(dve.reciprocal(col(6), col(6)))
            step(dve.tensor_tensor(col(7), col(6), col(4), ALU.mult))
            step(dve.tensor_tensor(hot1, hot1, wide(col(6), NE), ALU.mult))
            step(dve.tensor_tensor(hot2, hot2, wide(col(7), NE), ALU.mult))
            dve.tensor_tensor(comb[:, :, 1:NE + 1], hot1, hot2, ALU.add)
            dve.wait_ge(chosen_ready, 1)
            dve.wait_ge(rank_ps, 1)
            step(dve.scalar_tensor_tensor(out=route[:, 8, :, :], in0=ps[:, 2, 0:NT * NE].rearrange("p (t e) -> p t e", t=NT),
                                          scalar=1.0, in1=chosen, op0=ALU.add, op1=ALU.mult))
            step(dve.tensor_scalar(rankm[:, :, 0:NE], route[:, 8, :, :], -1.0, None, ALU.add))
            most, cnt = rcol[0:1, 8, 0:1], rcol[0:1, 9, 0:1]
            step(dve.tensor_reduce(most, ps[0:1, 2, NT * NE:NT * NE + NE], AX, ALU.max))
            step(dve.tensor_scalar(cnt, most, float(SLOTS), 1.0, ALU.is_gt, ALU.add))
            for r in range(2, ROUNDS):
                step(dve.scalar_tensor_tensor(out=cnt, in0=most, scalar=float(SLOTS * r), in1=cnt,
                                              op0=ALU.is_gt, op1=ALU.add))
            dve.tensor_copy(rounds_i[:, :], cnt).then_inc(rounds_ready, 1)

            def select(b, e):
                for t in range(NT):
                    ins = dve.tensor_scalar(SEL[:, b, t, :], slot_ids[:, :], rankm[:, t, e], None, ALU.is_equal)
                ins.then_inc(sel_ready, 1)

            def spread(b):
                for u in range(2):
                    ins = dve.tensor_tensor(XG[:, b, 8 * u:8 * u + 8, :],
                                            ps[:, 1 + u, :].rearrange("p (k s) -> p k s", k=8),
                                            gains[:, 1, 8 * u:8 * u + 8].unsqueeze(2).to_broadcast([P, 8, SLOTS]), ALU.mult)
                ins.then_inc(xg_ready, 1)

            def accumulate(e, first):
                for u in range(4):
                    t, m = divmod(u, 2)
                    dve.wait_ge(scatter_ps, first + (u + 1))
                    for half in range(2):
                        n = 2 * m + half
                        piece = h[:, t, 512 * n:512 * n + 512]
                        dve.scalar_tensor_tensor(out=piece, in0=ps[:, 6 + half, :], scalar=comb[:, t, e], in1=piece,
                                                 op0=ALU.mult, op1=ALU.add).then_inc(acc_done, 1)

            def expert_round(r):
                select(0, slice(0, 1))
                dve.wait_ge(gather_ps, r * (NE + 1) + 1)
                spread(0)
                with dve.Fori(0, NE // 2) as i:
                    for b in range(2):
                        n = i * 2 + b
                        select(1 - b, bass.ds(n + 1, 1))
                        dve.wait_ge(gather_ps, r * (NE + 1) + n + 2)
                        spread(1 - b)
                        dve.wait_ge(silu_ready, r * NE + n + 1)
                        dve.tensor_tensor(HDN, SL, ps[:, 5, :].rearrange("p (k s) -> p k s", k=4)[:, :, SLOTS:2 * SLOTS],
                                          ALU.mult).then_inc(hdn_ready, 1)
                        accumulate(bass.ds(n, 1), (r * (NE + 1) + n) * 4)
                accumulate(slice(NE, NE + 1), (r * (NE + 1) + NE) * 4)

            dve.wait_ge(moe_zero, 2)
            expert_round(0)
            dve.wait_ge(rounds_ready, 1)
            rounds = dve.value_load(rounds_i[0:1, 0:1], min_val=1, max_val=ROUNDS)
            with dve.If(rounds > 1):
                with dve.Fori(1, rounds) as r:
                    dve.wait_ge(gather_ps, r * (NE + 1))
                    dve.tensor_scalar(slot_ids[:, :], slot_ids[:, :], float(SLOTS), None, ALU.add)
                    dve.drain()
                    expert_round(r)
                dve.nop()
            with dve.Else():
                dve.nop()
            dve.wait_ge(acc_done, rounds * (8 * (NE + 1)))
            dve.nop().then_inc(moe_done, 1)

            dve.wait_ge(ssp_ready, 1)
            step(dve.tensor_reduce(ss[:, 4:6], stat[:, 0:NT, 0:4], AX, ALU.add))
            dve.tensor_scalar(ss[:, 4:6], ss[:, 4:6], 1.0 / D, EPS, ALU.mult, ALU.add).then_inc(msp_ready, 1)
            dve.wait_ge(rp_ready, 1)
            dve.wait_ge(end_loaded, 48)
            for n in range(4):
                for t in range(NT):
                    dve.scalar_tensor_tensor(out=pe[:, t, 512 * n:512 * n + 512], in0=ps[:, 2 * n + t, :],
                                             scalar=rstd[:, 4 + t:5 + t], in1=gple[:, 512 * n:512 * n + 512],
                                             op0=ALU.mult, op1=ALU.mult).then_inc(pe_ready, 1)
            norm(2)

            def gate_in(u):
                n, t = divmod(u, NT)
                if t == 0:
                    dve.wait_ge(tail_used, PLE_CHUNKS + 4 * (n + 1))
                if u >= 4:
                    dve.wait_ge(out_stored[u % 4], 16)
                dve.tensor_tensor(z[:, u % 4, :], ps[:, u, :], bpg[:, 512 * n:512 * n + 512], ALU.add).then_inc(z_ready, 1)

            def gate_out(u):
                n, t = divmod(u, NT)
                dve.wait_ge(gate_ready, u + 1)
                step(dve.tensor_tensor(z[:, u % 4, :], z[:, u % 4, :], pe[:, t, 512 * n:512 * n + 512], ALU.mult))
                dve.tensor_tensor(z[:, u % 4, :], z[:, u % 4, :], h[:, t, 512 * n:512 * n + 512], ALU.add).then_inc(out_ready, 1)

            dve.wait_ge(pe_ready, 8)
            for n in range(4):
                for t in range(NT):
                    gate_in(2 * n + t)
                for t in range(NT):
                    gate_out(2 * n + t)

        @block.tensor
        def _(pe_):
            mm = pe_.matmul
            pe_.wait_ge(consts_ready, 1)
            pe_.wait_ge(prm_loaded, 16 * 7)
            pe_.transpose(ps[:, 0, 0:80], prm[0:80, :], ident[0:80, 0:80]).then_inc(prm_ps, 1)
            pe_.wait_ge(prm_ready, 1)

            def transpose_h(j):
                pe_.wait_ge(hs_act, j + 1)
                pe_.wait_ge(hs_dve, j + 1)
                for b in range(8):
                    for u in range(2):
                        for t in range(NT):
                            ins = pe_.transpose(ps[:, b, T * u + P * t:T * u + P * t + P], hs[:, t, 2 * b + u, :], ident[:, :])
                    ins.then_inc(hT_ps, 1)
                pe_.wait_ge(hT_act, 8 * (j + 1))
                pe_.wait_ge(hT_dve, 8 * (j + 1))

            transpose_h(0)

            c = 0
            for s, g in enumerate(WIN_ORDER):
                by_channel = g < 4
                bank = {0: 0, 1: 4, 2: 0, 3: 0, 4: 0, 5: 2, 6: 4}[g]
                if s == 2:
                    pe_.wait_ge(xl_ready, 1)
                if s == 4:
                    pe_.wait_ge(xl_ready, 2)
                if s == 5:
                    pe_.wait_ge(xc_ready, 1)
                    pe_.wait_ge(bd_loaded, 64)
                    for cb in range(CB):
                        if cb >= 2:
                            pe_.wait_ge(gates_ready, cb - 1)
                        for w in range(2):
                            ins = mm(ps[:, 6 + cb % 2, T * w:T * w + T], bd[:, w, cb, :], xc[:, cb, :], start=True, stop=True)
                        ins.then_inc(gates_ps, 1)
                    pe_.wait_ge(qkv_ready, 2)
                if s == 6:
                    pe_.wait_ge(qk_ready, 1)
                    pe_.wait_ge(gates_ready, CB)
                    for t in range(NT):
                        if t:
                            pe_.wait_ge(qT_ready, t)
                        for j in range(CB):
                            ins = pe_.transpose(ps[:, 4 + j // 4, P * (j % 4):P * (j % 4) + P],
                                                qk[:, t, 2 * j:2 * j + 2, :].rearrange("p h d -> p (h d)"), ident[:, :])
                        ins.then_inc(qT_ps, 1)
                        for kh in range(KV):
                            for half in range(2):
                                ins = mm(ps[64 * half:64 * half + 64, 6 + t, P * kh:P * kh + P], qk[:, t, HEADS + kh, :],
                                         ident[:, :], start=True, stop=True)
                        ins.then_inc(kT_ps, 1)
                    pe_.wait_ge(gelu_ready, 1)
                for kq in range(4):
                    slot = c % RING
                    pe_.wait_ge(loaded[slot], 16 * (c // RING + 1))
                    for kk in range(4):
                        k = 4 * kq + kk
                        if by_channel:
                            for cb in range(4):
                                ins = mm(ps[:, bank + cb, 0:T], ring4(slot)[:, kk, P * cb:P * cb + P], hT[:, k, :],
                                         start=(k == 0), stop=(k == KD - 1))
                        else:
                            for t in range(NT):
                                ins = mm(ps[:, bank + t, :], hT[:, k, P * t:P * t + P], ring4(slot)[:, kk, :],
                                         start=(k == 0), stop=(k == KD - 1))
                    ins.then_inc(chunks_used, 1)
                    c += 1

            pe_.wait_ge(qT_ready, 2)
            pe_.wait_ge(kT_ready, 2)
            pe_.wait_ge(s_masked, 1)
            for t in range(NT):
                base = 4 * (1 - t)
                if t:
                    pe_.wait_ge(gelu_ready, 2)
                for j in range(CB):
                    for q in range(2):
                        n = 2 * t + q
                        lo = max(0, CHUNK * (n - 1))
                        hi = CHUNK * (n + 1)
                        for two in range(2):
                            hh = 2 * j + two
                            at = P * (j % 4) + P - (hi - lo)
                            ins = mm(ps[64 * q:64 * q + 64, base + 2 * (j // 4) + two, at:at + hi - lo],
                                     qT[64 * two:64 * two + 64, j, CHUNK * n:CHUNK * n + CHUNK],
                                     kT[64 * two:64 * two + 64, hh // 4, lo:hi], start=True, stop=True)
                ins.then_inc(scores_ps, 1)
            for t in range(NT):
                if t == 0:
                    pe_.wait_ge(S_ready, 2)
                pe_.wait_ge(exp_ready, t + 1)
                for hh in range(HEADS):
                    ins = pe_.transpose(ps[:, 4 + hh // 4, P * (hh % 4):P * (hh % 4) + P], S[t][:, hh, :], ident[:, :])
                ins.then_inc(PT_ps, 1)
                pe_.wait_ge(PT_act, t + 1)
                pe_.wait_ge(PT_dve, t + 1)
                for hh in range(HEADS):
                    for q in range(2):
                        vals = (vs if q == 0 else v)[:, t, hh // 4, :]
                        ins = mm(ps[64 * q:64 * q + 64, 2 * t + hh // 8, HD * (hh % 8):HD * (hh % 8) + HD],
                                 PT[:, hh, 64 * q:64 * q + 64], vals, start=True, stop=True)
                ins.then_inc(pv_ps, 1)
            pe_.wait_ge(yat_ready, 2)
            for cb in range(CB):
                for t in range(NT):
                    at = T * (cb % 2) + P * t
                    ins = pe_.transpose(ps[:, 4 + cb // 2, at:at + P],
                                        yat[:, t, 2 * cb:2 * cb + 2, :].rearrange("p h d -> p (h d)"), ident[:, :])
            ins.then_inc(yT_ps, 1)
            pe_.wait_ge(ysq_ready, 1)
            for t in range(NT):
                for cb in range(CB):
                    ins = mm(ps[:, 0, t:t + 1], t1[:, cb, P * t:P * t + P], ones_c[:, 0:1], start=(cb == 0), stop=(cb == CB - 1))
            ins.then_inc(ssA_ps, 1)

            pe_.wait_ge(yg_ready, CB)
            pe_.wait_ge(msAB_ready, 1)
            for n in range(4):
                if n >= 2:
                    pe_.wait_ge(h_ready, n - 1)
                for cq in range(4):
                    slot = c % RING
                    if n == 0 and cq == 2 or n == 1 and cq == 0:
                        pe_.wait_ge(yT_act, 4)
                        pe_.wait_ge(yT_dve, 4)
                    pe_.wait_ge(loaded[slot], 16 * (c // RING + 1))
                    for kk in range(4):
                        cc = 4 * cq + kk
                        src = gt if cc < CB else yT
                        for t in range(NT):
                            ins = mm(ps[:, 4 * (n % 2) + 2 * (cq // 2) + t, :], src[:, cc % CB, P * t:P * t + P],
                                     ring4(slot)[:, kk, :], start=(cc % CB == 0), stop=(cc % CB == CB - 1))
                    ins.then_inc(chunks_used, 1)
                    c += 1

            pe_.wait_ge(h_ready, 4)
            transpose_h(1)
            pe_.wait_ge(wre_loaded, 16)
            pe_.wait_ge(small_loaded, 160)
            for t in range(NT):
                for lo, n, w in ((0, GROUPS, wrg), (GROUPS, NE, wre)):
                    for k in range(KD):
                        ins = mm(ps[:, t, lo:lo + n], hT[:, k, P * t:P * t + P], w[:, k, :],
                                 start=(k == 0), stop=(k == KD - 1))
            ins.then_inc(logits_ps, 1)
            pe_.wait_ge(chosen_ready, 1)
            pe_.wait_ge(route_consts, 5)
            mm(ps[:, 2, 0:NE], before, route[:, 7, 0, :], start=True, stop=True)
            mm(ps[:, 2, NE:2 * NE], ones, route[:, 7, 0, :], start=True, stop=False)
            mm(ps[:, 2, NE:2 * NE], before, route[:, 7, 1, :], start=False, stop=True)
            for t in range(NT):
                ins = mm(ps[0:1, 2, 2 * NE:3 * NE], ones[:, 0:1], route[:, 7, t, :], start=(t == 0), stop=(t == NT - 1))
            ins.then_inc(rank_ps, 1)

            def gather(b, count):
                pe_.wait_ge(sel_ready, count)
                for k in range(KD):
                    for t in range(NT):
                        ins = mm(ps[:, 1 + k // 8, SLOTS * (k % 8):SLOTS * (k % 8) + SLOTS], hs[:, t, k, :],
                                 SEL[:, b, t, 0:SLOTS], start=(t == 0), stop=(t == NT - 1))
                ins.then_inc(gather_ps, 1)

            def scatter(b, count):
                for u in range(4):
                    t, m = divmod(u, 2)
                    if u:
                        pe_.wait_ge(acc_done, count * 8 + 2 * u)
                    for half in range(2):
                        rows_ = slice(64 * half, 64 * half + 64)
                        ins = mm(ps[:, 6 + half, :], G[rows_, b, t, :], Y[rows_, b, m, :], start=True, stop=True)
                    ins.then_inc(scatter_ps, 1)

            def expert_round(r):
                gather(0, r * (NE + 1) + 1)
                with pe_.Fori(0, NE // 2) as i:
                    for b in range(2):
                        n = i * 2 + b

                        def arrived(j):
                            slot = (FRONT_CHUNKS + j) % RING
                            pe_.wait_ge(loaded[slot], (r * NE + n) * 16 + 16 * (front_uses(slot) + 1))
                            return slot

                        pe_.wait_ge(xg_ready, r * (NE + 1) + n + 1)
                        for kq in range(4):
                            s1, s3 = arrived(2 * kq), arrived(2 * kq + 1)
                            for kk in range(4):
                                k = 4 * kq + kk
                                for half, s in ((0, s1), (1, s3)):
                                    ins = mm(ps[64 * half:64 * half + 64, 0, :], XG[:, b, k, :], ring4(s)[:, kk, :],
                                             start=(k == 0), stop=(k == KD - 1))
                                    if kk == 3:
                                        ins.then_inc(chunks_used, 1)
                        pe_.wait_ge(sel_ready, r * (NE + 1) + n + 2)
                        for t in range(NT):
                            ins = pe_.transpose(ps[:, 6, P * t:P * t + P], SEL[:, b, t, :], ident[:, :])
                        ins.then_inc(g_ps, 1)
                        gather(1 - b, r * (NE + 1) + n + 2)
                        pe_.wait_ge(h13_ready, r * NE + n + 1)
                        for k in range(4):
                            ins = pe_.transpose(ps[:, 5, P * k:P * k + P], H13[:, k, :], ident[:, :])
                        ins.then_inc(h13T_ps, 1)
                        pe_.wait_ge(g_ready, r * NE + n + 1)
                        scatter(1 - b, r * (NE + 1) + n)
                        pe_.wait_ge(hdn_ready, r * NE + n + 1)
                        for k in range(4):
                            s = arrived(8 + k)
                            for m in range(2):
                                for half in range(2):
                                    at = 1024 * m + 512 * half
                                    ins = mm(ps[64 * half:64 * half + 64, 3 + m, :], HDN[:, k, :], ring[:, s, at:at + 512],
                                             start=(k == 0), stop=(k == 3))
                            ins.then_inc(chunks_used, 1)
                pe_.wait_ge(y_ready, r * NE + NE)
                pe_.wait_ge(acc_done, (r * (NE + 1) + NE) * 8)
                scatter(1, r * (NE + 1) + NE)

            pe_.wait_ge(moe_zero, 2)
            expert_round(0)
            pe_.wait_ge(rounds_ready, 1)
            rounds = pe_.value_load(rounds_i[0:1, 0:1], min_val=1, max_val=ROUNDS)
            with pe_.If(rounds > 1):
                with pe_.Fori(1, rounds) as r:
                    expert_round(r)
                pe_.nop()
            with pe_.Else():
                pe_.nop()

            pe_.wait_ge(moe_done, 1)
            pe_.wait_ge(end_loaded, 48)
            for cc in range(2):
                for t in range(NT):
                    ins = pe_.transpose(ps[:, 0, T * cc + P * t:T * cc + P * t + P], pp[:, t, P * cc:P * cc + P], ident[:, :])
            ins.then_inc(pT_ps, 1)
            pe_.wait_ge(pT_ready, 1)
            for c in range(PLE_CHUNKS):
                slot = (FRONT_CHUNKS + c) % RING
                pe_.wait_ge(tail_loaded[slot], 16)
                for n in range(4):
                    for t in range(NT):
                        ins = mm(ps[:, 2 * n + t, :], pT[:, c, P * t:P * t + P], ring[:, slot, 512 * n:512 * n + 512],
                                 start=(c == 0), stop=(c == PLE_CHUNKS - 1))
                ins.then_inc(tail_used, 1)
            pe_.wait_ge(pe_ready, 8)
            transpose_h(2)
            for n in range(4):
                for kq in range(4):
                    c = PLE_CHUNKS + 4 * n + kq
                    slot = (FRONT_CHUNKS + c) % RING
                    pe_.wait_ge(tail_loaded[slot], 16 * (c // RING + 1))
                    for kk in range(4):
                        k = 4 * kq + kk
                        for t in range(NT):
                            ins = mm(ps[:, 2 * n + t, :], hT[:, k, P * t:P * t + P], ring4(slot)[:, kk, :],
                                     start=(k == 0), stop=(k == KD - 1))
                    ins.then_inc(tail_used, 1)


NAMES = ["x", "p", "positions", "g_mix", "w_in", "conv_w", "conv_b", "w_a", "b_a", "w_i", "b_i", "lam", "g_q", "g_k",
         "sinks", "g_out_lru", "g_out_attn", "w_out", "g_moe", "w_rg", "b_rg", "w_re", "b_re", "w1", "w3", "w2",
         "w_ple", "g_ple", "g_pg", "w_pg", "b_pg"]


def kernel(**inputs):
    import numpy as _np
    import concourse.bacc as _bacc
    from concourse import mybir as _mybir
    from concourse.bass_utils import run_bass_kernel_spmd as _run

    nc = _bacc.Bacc("TRN2", target_bir_lowering=False, num_devices=1)
    arrays, args = {}, {}
    for name in NAMES:
        a = _np.ascontiguousarray(inputs[name])
        arrays[f"in_{name}"] = a
        args[name] = nc.dram_tensor(f"in_{name}", a.shape, _mybir.dt.from_np(a.dtype), kind="ExternalInput").ap()
    args["out"] = nc.dram_tensor("out_h", (1, T, D), _mybir.dt.float32, kind="ExternalOutput").ap()
    build(nc, **args)
    got = _run(nc, [arrays], core_ids=[0])
    return got.results[0]["out_h"]
```

```python
import math
from contextlib import ExitStack

import numpy as np

import concourse.bass as bass
from concourse import mybir

P = 128
ALU = mybir.AluOpType
ACT = mybir.ActivationFunctionType
F32 = mybir.dt.float32
I32 = mybir.dt.int32
AX = mybir.AxisListType.X

T, D = 256, 2048
NT = T // P
KD = D // P
CHUNK = 64
EPS = 1e-6
D_LRU, CB = 1024, 8
CONV_W = 4
HEADS, KV, HD = 16, 4, 64
QK = HEADS + KV
ROT = HD // 4
HALF = ROT // 2
THETA = 500000.0
GROUPS, PER_GROUP = 4, 8
NE = GROUPS * PER_GROUP
D_EXP = 512
D_PLE = 256
NEG = -1e30
NL = GROUPS + NE

RING = 12
CH = 2048
WIN_GROUPS = 7
WIN_CHUNKS = 4 * WIN_GROUPS
WOUT_A = WIN_CHUNKS
WOUT_B = WIN_CHUNKS + 8
PLE = WIN_CHUNKS + 16
FRONT_CHUNKS = PLE + 2
EXPERT_CHUNKS = 12
ROUND_CHUNKS = NE * EXPERT_CHUNKS
TAIL_CHUNKS = 16
PAIRS = NE // 2
GATHERS = 4 * (PAIRS + 1)
SCATTERS = 8 * (PAIRS + 1)
SLOTS = 64
ROUNDS = T // SLOTS
assert ROUND_CHUNKS % RING == 0 and 4 * EXPERT_CHUNKS % RING == 0 and NL <= 36

TWO_PI_1 = 6.28125
TWO_PI_2 = math.floor((2 * math.pi - TWO_PI_1) * 2 ** 17) / 2 ** 17
TWO_PI_3 = math.floor((2 * math.pi - TWO_PI_1 - TWO_PI_2) * 2 ** 27) / 2 ** 27
TWO_PI_4 = 2 * math.pi - TWO_PI_1 - TWO_PI_2 - TWO_PI_3
ROUND_MAGIC = 1.5 * 2 ** 23
PI_BELOW = 3.1415925


def front_uses(slot):
    return FRONT_CHUNKS // RING + (slot < FRONT_CHUNKS % RING)


def build(nc, x, p, positions, g_mix, w_in, conv_w, conv_b, w_a, b_a, w_i, b_i, lam, g_q, g_k, sinks,
          g_out_lru, g_out_attn, w_out, g_moe, w_rg, b_rg, w_re, b_re, w1, w3, w2,
          w_ple, g_ple, g_pg, w_pg, b_pg, out):
    with ExitStack() as ctx:
        def sb(name, shape, dt=F32):
            return ctx.enter_context(nc.sbuf_tensor(name, shape, dt))

        def sem(name):
            return ctx.enter_context(nc.semaphore(name))

        ring = sb("ring", [P, RING, CH])
        h = sb("h", [P, NT, D])
        hs = sb("hs", [P, NT, KD, P])
        hT = sb("hT", [P, KD, T])
        area = sb("area", [P, 15128])
        ident = sb("ident", [P, P])
        prmT = sb("prmT", [P, 112])
        g_moe_pk = sb("g_moe_pk", [P, KD])
        gqk = sb("gqk", [P, 2, HD])
        sink_bc = sb("sink_bc", [P, HEADS])
        br_bc = sb("br_bc", [P, NL])
        pieces = sb("pieces", [P, 2, NT, 4])
        r_ple = sb("r_ple", [P, NT])
        idx = sb("idx", [P, NE])
        expo = sb("expo", [P, QK])
        ones_c = sb("ones_c", [P, 2])
        ss = sb("ss", [P, 8])
        rstd = sb("rstd", [P, 8])
        ssq = sb("ssq", [P, NT, QK])
        rqk = sb("rqk", [P, NT, QK])
        stat = sb("stat", [P, 6, HEADS])
        rounds_i = sb("rounds_i", [1, 1], I32)
        pos_i = sb("pos_i", [P, NT], I32)
        sp = sb("sp", [P, 6, CB])
        trig = sb("trig", [P, 2, NT, HALF])

        def part(lo, n, *dims):
            v = area[:, lo:lo + n]
            if len(dims) == 2:
                return v.rearrange("p (a b) -> p a b", a=dims[0])
            if len(dims) == 3:
                return v.rearrange("p (a b c) -> p a b c", a=dims[0], b=dims[1])
            if len(dims) == 4:
                return v.rearrange("p (a b c d) -> p a b c d", a=dims[0], b=dims[1], c=dims[2])
            return v

        xl = part(0, CB * (T + 3), CB, T + 3)
        xl_flat = part(0, CB * T, CB, T)
        xc = part(2072, CB * T, CB, T)
        t1 = part(4120, CB * T, CB, T)
        t2 = part(6168, CB * T, CB, T)
        gt = part(8216, CB * T, CB, T)
        qk = part(10264, NT * QK * HD, NT, QK, HD)
        yat = part(10264, NT * HEADS * HD, NT, HEADS, HD)
        v = part(12824, NT * KV * HD, NT, KV, HD)
        vs = part(13336, NT * KV * HD, NT, KV, HD)
        kT = part(13848, KV * T, KV, T)
        sqk = [part(0, QK * HD, QK, HD), part(6168, QK * HD, QK, HD)]
        junkB = part(2072, 2048, 2, 1024)
        rope = part(13848, 4 * QK * HALF, 4, QK, HALF)
        prm = part(13848, P)
        angles = part(14000, 6 * NT * HALF, 6, NT, HALF)
        hs_flat = hs[:, :, :, :].rearrange("p t k m -> p (t k m)")
        hT_flat = hT[:, :, :].rearrange("p k t -> p (k t)")
        hs_t = hs[:, :, :, :].rearrange("p t k m -> p t (k m)")
        junkH = hs_flat.rearrange("p (a n) -> p a n", a=8)
        bd = hs_flat[:, 0:2048].rearrange("p (w c j) -> p w c j", w=2, c=CB)
        S = [hs_flat[:, 0:2048].rearrange("p (h k) -> p h k", h=HEADS),
             hT_flat[:, 2048:4096].rearrange("p (h k) -> p h k", h=HEADS)]
        qT = hs_flat[:, 2048:4096].rearrange("p (j t) -> p j t", j=CB)
        PT = hT_flat[:, 0:2048].rearrange("p (h q) -> p h q", h=HEADS)
        yT = hT_flat[:, 2048:4096].rearrange("p (c t) -> p c t", c=CB)
        junk = hT[:, :, :].rearrange("p (a k) t -> p a (k t)", a=NT)
        XG = part(0, 2 * KD * P, 2, KD, P)
        Y = part(4096, 2 * D, 2, D)
        H13 = part(8192, D_EXP, 4, P)
        SL = part(8704, 256, 4, SLOTS)
        HDN = part(8960, 256, 4, SLOTS)
        SEL = part(9216, 512, 2, NT, P)
        SELW = part(9728, 256, NT, P)
        G = part(9984, 512, 2, NT, P)
        pe = part(10496, NT * D, NT, D)
        before = part(14592, P)
        ones = part(14720, P)
        pp = part(0, NT * D_PLE, NT, D_PLE)
        pT = part(512, 512, 2, T)
        wr = part(2048, KD * NL, KD, NL)
        gple = part(4096, D)
        junkP = part(6144, 2048, 4, 512)
        junkP2 = part(8192, 2048, 4, 512)
        route = hT_flat[:, 0:640].rearrange("p (a t e) -> p a t e", a=10, t=NT)
        lg = hT_flat[:, 640:640 + NT * NL].rearrange("p (t n) -> p t n", t=NT)
        rcol = hT_flat[:, 720:744].rearrange("p (a t) -> p a t", t=NT)
        lT = hT_flat[:, 1024:1024 + T]
        rankm = sb("rankm", [P, NT, NE + 2])
        comb = sb("comb", [P, NT, NE])
        slot_ids = sb("slot_ids", [P, SLOTS])
        bpg = part(0, D)
        z = part(4096, 2048, 4, 512)

        ps = ctx.enter_context(nc.psum_tensor("ps", [P, 8, 512], F32))

        x_loaded = [sem(f"x_loaded{t}") for t in range(NT)]
        prm_loaded, small_loaded, bd_loaded = sem("prm_loaded"), sem("small_loaded"), sem("bd_loaded")
        wr_loaded, ple_loaded, bpg_loaded = sem("wr_loaded"), sem("ple_loaded"), sem("bpg_loaded")
        loaded = [sem(f"loaded{s}") for s in range(RING)]
        tail_loaded = [sem(f"tail_loaded{s}") for s in range(RING)]
        chunks_used, tail_used = sem("chunks_used"), sem("tail_used")
        consts_ready = sem("consts_ready")
        pool_step, dve_step, act_step = sem("pool_step"), sem("dve_step"), sem("act_step")
        prm_ps, prm_ready = sem("prm_ps"), sem("prm_ready")
        ss_ready, ms_ready, rstd_ready = sem("ss_ready"), sem("ms_ready"), sem("rstd_ready")
        hs_act, hs_dve, hT_ps, hT_act, hT_dve = sem("hs_act"), sem("hs_dve"), sem("hT_ps"), sem("hT_act"), sem("hT_dve")
        xl_ready, qkv_ready, gelu_ready = sem("xl_ready"), sem("qkv_ready"), sem("gelu_ready")
        bd_zero, xl_pad, xc_ready = sem("bd_zero"), sem("xl_pad"), sem("xc_ready")
        gates_ps, gates_ready, tanh_ready, sqrt_ready = sem("gates_ps"), sem("gates_ready"), sem("tanh_ready"), sem("sqrt_ready")
        recip_done, y_lru, ysq_ready, yg_ready = sem("recip_done"), sem("y_lru"), sem("ysq_ready"), sem("yg_ready")
        lam_exp, lam_sum, lam_ln = sem("lam_exp"), sem("lam_sum"), sem("lam_ln")
        lam_ready = sem("lam_ready")
        ang_ready, trig_ready = sem("ang_ready"), sem("trig_ready")
        qsq_ready, qms_ready, qr_ready, qk_ready = (
            sem("qsq_ready"), sem("qms_ready"), sem("qr_ready"), sem("qk_ready"))
        qT_ps, qT_ready, kT_ps, kT_ready = sem("qT_ps"), sem("qT_ready"), sem("kT_ps"), sem("kT_ready")
        s_masked, scores_ps, S_ready, shifted, exp_ready = (
            sem("s_masked"), sem("scores_ps"), sem("S_ready"), sem("shifted"), sem("exp_ready"))
        sink_shifted, sink_exp = sem("sink_shifted"), sem("sink_exp")
        PT_ps, PT_act, PT_dve, pv_ps, yat_ready = sem("PT_ps"), sem("PT_act"), sem("PT_dve"), sem("pv_ps"), sem("yat_ready")
        yT_ps, yT_act, yT_dve = sem("yT_ps"), sem("yT_act"), sem("yT_dve")
        ssA_ps, msA_ready, rA_ready = sem("ssA_ps"), sem("msA_ready"), sem("rA_ready")
        ssB_ready, msB_ready, rB_ready = sem("ssB_ready"), sem("msB_ready"), sem("rB_ready")
        hA_ready, ss1_ready = sem("hA_ready"), sem("ss1_ready")
        h_ready = sem("h_ready")
        lT_ps, lT_ready = sem("lT_ps"), sem("lT_ready")
        logits_ps, gmax_ready, gexp_ready, e_diff, e_exp = (
            sem("logits_ps"), sem("gmax_ready"), sem("gexp_ready"), sem("e_diff"), sem("e_exp"))
        chosen_ready, rank_ps, rounds_ready = sem("chosen_ready"), sem("rank_ps"), sem("rounds_ready")
        route_consts = sem("route_consts")
        sel_ready, gather_ps, xg_ready, h13_ready = (
            sem("sel_ready"), sem("gather_ps"), sem("xg_ready"), sem("h13_ready"))
        selw_ready, g_ps, g_ready, h13T_ps, silu_ready, hdn_ready = (
            sem("selw_ready"), sem("g_ps"), sem("g_ready"), sem("h13T_ps"), sem("silu_ready"), sem("hdn_ready"))
        y_ready, scatter_ps, acc_done, moe_done = (
            sem("y_ready"), sem("scatter_ps"), sem("acc_done"), sem("moe_done"))
        pT_ps, pT_ready, ple_ps, pe_raw, msp_ready, rp_ready, pe_ready = (
            sem("pT_ps"), sem("pT_ready"), sem("ple_ps"), sem("pe_raw"), sem("msp_ready"),
            sem("rp_ready"), sem("pe_ready"))
        z_ready, gate_ready, out_ready, out_stored = (
            sem("z_ready"), sem("gate_ready"), sem("out_ready"), [sem(f"out_stored{u}") for u in range(4)])

        x_v = x[0].rearrange("(t p) d -> p t d", p=P)
        out_v = out[0].rearrange("(t p) d -> p t d", p=P)
        p_v = p[0, 0].rearrange("(t p) c -> p t c", p=P)
        w_in_v = w_in[0].rearrange("(k p) n -> p k n", p=P)
        w_out_v = w_out[0].rearrange("(c p) n -> p c n", p=P)
        w_pg_v = w_pg[0].rearrange("(k p) n -> p k n", p=P)
        w_ple_v = w_ple[0].rearrange("(c p) n -> p c n", p=P)
        w1_v = w1[0].rearrange("e (p k) f -> e p k f", k=KD)
        w3_v = w3[0].rearrange("e (p k) f -> e p k f", k=KD)
        w2_v = w2[0].rearrange("e (p k) n -> e p k n", k=4)

        def gain(j, k):
            return g_moe_pk[:, k:k + 1] if j == 1 else prmT[:, (80, 0, 96)[j] + k:(80, 0, 96)[j] + k + 1]

        def ring4(slot):
            return ring[:, slot, :].rearrange("p (k n) -> p k n", k=4)

        block = ctx.enter_context(nc.Block())

        @block.sync
        def _(sp_q):
            for t in range(NT):
                sp_q.dma_start(h[:, t, :], x_v[:, t, :]).then_inc(x_loaded[t], 16)

            def front_chunk(c, src, flat=False):
                if c >= RING:
                    sp_q.wait_ge(chunks_used, c - RING + 1)
                slot = c % RING
                sp_q.dma_start(ring[:, slot, :] if flat else ring4(slot), src).then_inc(loaded[slot], 16)

            for g in range(WIN_GROUPS):
                for kq in range(4):
                    if 4 * g + kq == 2:
                        sp_q.wait_ge(prm_loaded, 16 * 9)
                        sp_q.wait_ge(small_loaded, 16 * 7)
                    front_chunk(4 * g + kq, w_in_v[:, 4 * kq:4 * kq + 4, 512 * g:512 * g + 512])
            for c in range(16):
                part_, n, cq = c // 8, c // 2 % 4, c % 2
                rows4 = 8 * part_ + 4 * cq
                front_chunk(WOUT_A + c, w_out_v[:, rows4:rows4 + 4, 512 * n:512 * n + 512])
            for c in range(2):
                front_chunk(PLE + c, w_ple_v[:, c, :], flat=True)

            def expert_round(used):
                with sp_q.Fori(0, NE) as e:
                    at_e = e * EXPERT_CHUNKS
                    for j in range(EXPERT_CHUNKS):
                        slot = (FRONT_CHUNKS + j) % RING
                        sp_q.wait_ge(chunks_used, at_e + (used + j - RING + 1))
                        if j < 8:
                            src = (w1_v if j % 2 == 0 else w3_v)[bass.ds(e, 1), :, 4 * (j // 2):4 * (j // 2) + 4, :]
                            src = src.rearrange("a p k f -> p (a k) f")
                            dst = ring4(slot)
                        else:
                            src = w2_v[bass.ds(e, 1), :, j - 8, :].rearrange("a p n -> p (a n)")
                            dst = ring[:, slot, :]
                        sp_q.dma_start(dst, src).then_inc(loaded[slot], 16)

            expert_round(FRONT_CHUNKS)
            sp_q.wait_ge(rounds_ready, 1)
            rounds = sp_q.value_load(rounds_i[0:1, 0:1], min_val=1, max_val=ROUNDS)
            with sp_q.If(rounds > 1):
                with sp_q.Fori(1, rounds) as r:
                    expert_round(r * ROUND_CHUNKS + FRONT_CHUNKS)
                sp_q.nop()
            with sp_q.Else():
                sp_q.nop()
            for c in range(TAIL_CHUNKS):
                slot = (FRONT_CHUNKS + c) % RING
                if c < RING:
                    sp_q.wait_ge(chunks_used, rounds * ROUND_CHUNKS + (FRONT_CHUNKS + c - RING + 1))
                else:
                    sp_q.wait_ge(tail_used, c - RING + 1)
                n, kq = divmod(c, 4)
                sp_q.dma_start(ring4(slot), w_pg_v[:, 4 * kq:4 * kq + 4, 512 * n:512 * n + 512]
                               ).then_inc(tail_loaded[slot], 16)
            for u in range(2 * 4):
                n, t = divmod(u, NT)
                sp_q.wait_ge(out_ready, u + 1)
                sp_q.dma_start(out_v[:, t, 512 * n:512 * n + 512], z[:, u % 4, :]).then_inc(out_stored[u % 4], 16)
            for u in range(4):
                sp_q.wait_ge(out_stored[u], 16 * 2)

        @block.gpsimd
        def _(pool):
            steps = [0]

            def step(ins):
                steps[0] += 1
                ins.then_inc(pool_step, 1)
                pool.wait_ge(pool_step, steps[0])

            step(pool.memset(ident[:, :], 0.0))
            pool.affine_select(out=ident[:, :], in_=ident[:, :], compare_op=ALU.not_equal, fill=1.0, base=0,
                               pattern=[[-1, P]], channel_multiplier=1).then_inc(consts_ready, 1)
            pool.memset(ones_c[:, :], 1.0)
            pool.memset(expo[:, :], -0.5).then_inc(consts_ready, 1)
            pool.memset(xl[:, :, 0:3], 0.0).then_inc(xl_pad, 1)
            pool.memset(vs[0:64, 0, :, :], 0.0).then_inc(xl_pad, 1)
            pool.wait_ge(consts_ready, 2)

            def norm_root(j):
                pool.wait_ge(ms_ready, j + 1)
                pool.tensor_tensor(rstd[:, 0:NT], ss[:, 2:2 + NT], expo[:, 0:NT], ALU.pow).then_inc(rstd_ready, 1)

            norm_root(0)
            pool.wait_ge(hs_dve, 1)
            pool.wait_ge(hT_ps, 8)
            pool.memset(bd[:, :, :, :], 0.0).then_inc(bd_zero, 1)
            pool.wait_ge(bd_zero, 1)
            for w, src in enumerate((w_a, w_i)):
                for half in range(2):
                    pool.dma_start(bd[64 * half:64 * half + 64, w, :, 64 * half:64 * half + 64],
                                   src[0, half:2 * CB:2, :, :].rearrange("c i j -> i c j")).then_inc(bd_loaded, 16)
            pool.wait_ge(gates_ready, CB)
            pool.memset(S[0][0:64, :, 0:64], NEG).then_inc(s_masked, 1)
            pool.wait_ge(ysq_ready, 1)
            for c in range(CB):
                pool.tensor_scalar(gt[:, c, :], gt[:, c, :], prmT[:, 64 + c:65 + c], None, ALU.mult
                                   ).then_inc(yg_ready, 1)
            pool.wait_ge(msA_ready, 1)
            pool.tensor_tensor(rstd[:, 4:6], ss[:, 4:6], expo[:, 0:2], ALU.pow).then_inc(rA_ready, 1)
            for t in range(NT):
                pool.wait_ge(qms_ready, t + 1)
                pool.tensor_tensor(rqk[:, t, :], ssq[:, t, :], expo[:, :], ALU.pow).then_inc(qr_ready, 1)
            pool.wait_ge(ssB_ready, 2)
            pool.dma_start(wr[:, :, 0:GROUPS], w_rg[0].rearrange("(p k) g -> p k g", k=KD)).then_inc(wr_loaded, 16)
            pool.dma_start(wr[:, :, GROUPS:NL], w_re[0].rearrange("(p k) e -> p k e", k=KD)).then_inc(wr_loaded, 16)
            pool.dma_start(pp, p_v).then_inc(ple_loaded, 16)
            pool.dma_start(gple, g_ple.partition_broadcast(P).rearrange("p a d -> p (a d)")).then_inc(ple_loaded, 16)
            pool.wait_ge(msB_ready, 1)
            pool.tensor_tensor(rstd[:, 6:8], ss[:, 6:8], expo[:, 0:2], ALU.pow).then_inc(rB_ready, 1)
            step(pool.memset(ones, 1.0))
            pool.affine_select(out=before, in_=ones, compare_op=ALU.is_gt, fill=0.0, base=0,
                               pattern=[[1, P]], channel_multiplier=-1).then_inc(route_consts, 1)
            pool.iota(slot_ids[:, :], [[1, SLOTS]], base=0, channel_multiplier=0,
                      allow_small_or_imprecise_dtypes=True).then_inc(route_consts, 1)
            pool.iota(idx[:, :], [[1, NE]], base=0, channel_multiplier=0,
                      allow_small_or_imprecise_dtypes=True).then_inc(route_consts, 1)
            pool.memset(rankm[:, :, NE:NE + 2], -1.0).then_inc(route_consts, 1)
            norm_root(1)
            pool.wait_ge(chunks_used, PLE)
            pool.memset(G[:, 1, :, :], 0.0).then_inc(g_ready, 1)
            pool.wait_ge(pe_raw, 4)
            pool.memset(Y[:, 1, :], 0.0).then_inc(y_ready, 1)
            pool.wait_ge(pe_raw, 8)
            pool.wait_ge(ple_loaded, 32)
            for t in range(NT):
                pool.tensor_tensor(pe[:, t, :], pe[:, t, :], gple, ALU.mult).then_inc(pe_ready, 1)
            pool.wait_ge(msp_ready, 1)
            pool.tensor_tensor(r_ple[:, :], ss[:, 4:6], expo[:, 0:2], ALU.pow).then_inc(rp_ready, 1)
            pool.wait_ge(moe_done, 1)
            pool.dma_start(bpg, b_pg.partition_broadcast(P).rearrange("p a d -> p (a d)")).then_inc(bpg_loaded, 16)
            norm_root(2)

        @block.scalar
        def _(act):
            a_steps = [0]

            def step(ins):
                a_steps[0] += 1
                ins.then_inc(act_step, 1)
                act.wait_ge(act_step, a_steps[0])

            rows = [(conv_w[0], 32, True), (conv_b, 8, False), (b_a, 8, False), (b_i, 8, False), (lam, 8, False),
                    (g_out_lru, 8, False), (g_out_attn, 8, False), (g_mix, 16, False), (g_pg, 16, False)]
            at = 0
            for src, n, taps in rows:
                view = src.rearrange("j (c p) -> (j c) p", p=P)
                act.dma_start(prm[at:at + n, :], view).then_inc(prm_loaded, 16)
                at += n
            act.dma_start(g_moe_pk[:, :], g_moe[0].rearrange("(p k) -> p k", k=KD)).then_inc(small_loaded, 16)
            act.dma_start(gqk[:, 0, :], g_q.partition_broadcast(P).rearrange("p a d -> p (a d)")).then_inc(small_loaded, 16)
            act.dma_start(gqk[:, 1, :], g_k.partition_broadcast(P).rearrange("p a d -> p (a d)")).then_inc(small_loaded, 16)
            act.dma_start(sink_bc[:, :], sinks.partition_broadcast(P).rearrange("p a d -> p (a d)")).then_inc(small_loaded, 16)
            act.dma_start(br_bc[:, 0:GROUPS], b_rg.partition_broadcast(P).rearrange("p a d -> p (a d)")).then_inc(small_loaded, 16)
            act.dma_start(br_bc[:, GROUPS:NL], b_re.partition_broadcast(P).rearrange("p a d -> p (a d)")).then_inc(small_loaded, 16)
            act.dma_start(pos_i[:, :], positions[0].rearrange("(t p) -> p t", p=P),
                          allow_slow_non_contiguous=True).then_inc(small_loaded, 16)

            def copy_hT(j):
                for b in range(0, 8, 2):
                    act.wait_ge(hT_ps, 8 * j + b + 1)
                    for u in range(2):
                        k = 2 * b + u
                        act.activation(hT[:, k, :], ps[:, b, T * u:T * u + T], ACT.Copy, scale=gain(j, k)
                                       ).then_inc(hT_act, 1)

            act.wait_ge(x_loaded[0], 16)
            act.activation(junk[:, 0, :], h[:, 0, :], ACT.Square, accum_out=ss[:, 0:1]).then_inc(ss_ready, 1)
            act.wait_ge(rstd_ready, 1)
            act.activation(hs_t[:, 0, :], h[:, 0, :], ACT.Copy, scale=rstd[:, 0:1]).then_inc(hs_act, 1)
            act.wait_ge(prm_ready, 1)
            copy_hT(0)
            act.wait_ge(lam_sum, 1)
            act.activation(sp[:, 1, :], sp[:, 0, :], ACT.Exp).then_inc(lam_exp, 1)
            act.wait_ge(lam_sum, 2)
            act.activation(sp[:, 3, :], sp[:, 2, :], ACT.Ln).then_inc(lam_ln, 1)
            act.wait_ge(ang_ready, 1)
            act.activation(trig[:, :, :, :], angles[:, 0:2, :, :], ACT.Sin).then_inc(trig_ready, 1)
            for g in range(2):
                act.wait_ge(chunks_used, 4 * (g + 1))
                for cb in range(4):
                    ins = act.activation(xl[:, 4 * g + cb, 3:3 + T], ps[:, 4 * g + cb, 0:T], ACT.Copy)
                ins.then_inc(xl_ready, 1)
            for g in range(2):
                act.wait_ge(chunks_used, 4 * (g + 3))
                for cb in range(4):
                    ins = act.activation(gt[:, 4 * g + cb, :], ps[:, 4 * g + cb, 0:T], ACT.Gelu_apprx_tanh)
                ins.then_inc(gelu_ready, 1)
            for c in range(CB):
                act.wait_ge(gates_ps, c + 1)
                act.activation(t1[:, c, :], ps[:, c % 2, 0:T], ACT.Sigmoid, bias=prmT[:, 40 + c:41 + c])
                act.activation(t2[:, c, :], ps[:, c % 2, T:2 * T], ACT.Sigmoid, bias=prmT[:, 48 + c:49 + c]
                               ).then_inc(gates_ready, 1)
            act.wait_ge(gates_ready, CB)
            act.wait_ge(lam_ready, 1)
            for c in range(CB):
                ins = act.activation(t1[:, c, :], t1[:, c, :], ACT.Tanh, scale=sp[:, 5, c:c + 1])
            ins.then_inc(tanh_ready, 1)
            act.wait_ge(recip_done, 1)
            act.activation(t1[:, :, :], t1[:, :, :], ACT.Sqrt).then_inc(sqrt_ready, 1)

            def copy_q(g):
                act.wait_ge(chunks_used, 4 * (g + 5))
                for t in range(NT):
                    ins = act.activation(qk[:, t, 8 * g:8 * g + 8, :],
                                         ps[:, 2 + 2 * g + t, :].rearrange("p (h d) -> p h d", h=8), ACT.Copy)
                ins.then_inc(qkv_ready, 1)

            copy_q(0)
            act.wait_ge(y_lru, 1)
            act.activation(t1[:, :, :], gt[:, :, :], ACT.Square).then_inc(ysq_ready, 1)
            copy_q(1)
            act.wait_ge(chunks_used, 4 * 7)
            act.wait_ge(xl_pad, 2)

            def kv_of(rows_, t, lo):
                return ps[rows_, 6 + t, lo:lo + 256].rearrange("p (h d) -> p h d", h=KV)

            for t in range(NT):
                ins = act.activation(qk[:, t, HEADS:QK, :], kv_of(slice(0, P), t, 0), ACT.Copy)
            ins.then_inc(qkv_ready, 1)
            act.wait_ge(qkv_ready, 3)
            for t in range(NT):
                act.activation(sqk[t], qk[:, t, :, :], ACT.Square).then_inc(qsq_ready, 1)
            for t in range(NT):
                act.activation(v[:, t, :, :], kv_of(slice(0, P), t, 256), ACT.Copy)
            act.activation(vs[64:128, 0, :, :], kv_of(slice(0, 64), 0, 256), ACT.Copy)
            act.activation(vs[0:64, 1, :, :], kv_of(slice(64, 128), 0, 256), ACT.Copy)
            act.activation(vs[64:128, 1, :, :], kv_of(slice(0, 64), 1, 256), ACT.Copy).then_inc(qkv_ready, 1)
            for t in range(NT):
                act.wait_ge(qT_ps, t + 1)
                for g in range(2):
                    ins = act.activation(qT[:, 4 * g:4 * g + 4, P * t:P * t + P],
                                         ps[:, 4 + g, :].rearrange("p (j q) -> p j q", j=4), ACT.Copy)
                ins.then_inc(qT_ready, 1)
            for t in range(NT):
                act.wait_ge(scores_ps, t + 1)
                for b in range(4):
                    src = ps[:, 4 + b, :].rearrange("p (j k) -> p j k", j=4)
                    dst = S[t].rearrange("p (g j two) k -> p g two j k", g=2, two=2)[:, b // 2, b % 2, :, :]
                    if t == 0:
                        act.activation(dst[64:128], src[64:128], ACT.Copy, scale=HD ** -0.5)
                        ins = act.activation(dst[0:64, :, 64:128], src[0:64, :, 64:128], ACT.Copy, scale=HD ** -0.5)
                    else:
                        ins = act.activation(dst, src, ACT.Copy, scale=HD ** -0.5)
                ins.then_inc(S_ready, 1)
                act.wait_ge(shifted, t + 1)
                act.activation(S[t], S[t], ACT.Exp).then_inc(exp_ready, 1)
                act.wait_ge(sink_shifted, t + 1)
                act.activation(stat[:, 3 * t + 1, :], stat[:, 3 * t + 1, :], ACT.Exp).then_inc(sink_exp, 1)
            for t in range(NT):
                act.wait_ge(PT_ps, t + 1)
                if t:
                    act.wait_ge(pv_ps, t)
                for b in range(2):
                    ins = act.activation(PT[:, 4 * b:4 * b + 4, :], ps[:, 4 + b, :].rearrange("p (j q) -> p j q", j=4), ACT.Copy)
                ins.then_inc(PT_act, 1)
            for t in range(NT):
                act.wait_ge(yat_ready, t + 1)
                act.activation(junkB[:, t, :],
                               yat[:, t, :, :].rearrange("p h d -> p (h d)"), ACT.Square,
                               accum_out=ss[:, 6 + t:7 + t]).then_inc(ssB_ready, 1)
            act.wait_ge(yT_ps, 1)
            for c in range(4):
                act.activation(yT[:, c, :], ps[:, 4 + c // 2, T * (c % 2):T * (c % 2) + T], ACT.Copy,
                               scale=prmT[:, 72 + c:73 + c]).then_inc(yT_act, 1)

            for n in range(4):
                act.wait_ge(h_ready, n + 1)
                for t in range(NT):
                    ins = act.activation(junkH[:, 2 * n + t, :],
                                         h[:, t, 512 * n:512 * n + 512], ACT.Square, accum_out=pieces[:, 0, t, n:n + 1])
            ins.then_inc(ss1_ready, 1)
            act.wait_ge(rstd_ready, 2)
            act.activation(hs[:, 0, :, :], h[:, 0, :].rearrange("p (m k) -> p k m", k=KD), ACT.Copy,
                           scale=rstd[:, 0:1]).then_inc(hs_act, 1)
            act.wait_ge(small_loaded, 16 * 7)
            copy_hT(1)
            act.wait_ge(lT_ps, 1)
            act.activation(lT[0:NL, :], ps[0:NL, 0, 0:T], ACT.Copy).then_inc(lT_ready, 1)
            act.wait_ge(pT_ps, 1)
            act.activation(pT, ps[:, 3, :].rearrange("p (c t) -> p c t", c=2), ACT.Copy).then_inc(pT_ready, 1)

            def copy_ple(half):
                act.wait_ge(ple_ps, half + 1)
                for u in range(4):
                    n, t = 2 * half + u // 2, u % 2
                    act.activation(pe[:, t, 512 * n:512 * n + 512], ps[:, 4 + u, :], ACT.Copy)
                    act.activation(junkP[:, u, :] if half == 0 else junkP2[:, u, :], ps[:, 4 + u, :], ACT.Square,
                                   accum_out=pieces[:, 1, t, n:n + 1]).then_inc(pe_raw, 1)

            copy_ple(0)
            act.wait_ge(gmax_ready, 1)
            act.activation(lg[:, :, 0:GROUPS], lg[:, :, 0:GROUPS], ACT.Exp).then_inc(gexp_ready, 1)
            act.wait_ge(e_diff, 1)
            act.activation(rcol[:, 4, :], rcol[:, 3, :], ACT.Exp).then_inc(e_exp, 1)

            copy_ple(1)

            def expert_round(n0, p0):
                with act.Fori(0, PAIRS // 2) as i:
                    for b in range(2):
                        for e in range(2):
                            n = i * 4 + (n0 + 2 * b + e)
                            act.wait_ge(chunks_used, n * EXPERT_CHUNKS + (FRONT_CHUNKS + 8))
                            act.activation(H13, ps[:, 0, :].rearrange("p (m k) -> p k m", k=4), ACT.Copy).then_inc(h13_ready, 1)
                            act.wait_ge(h13T_ps, n + 1)
                            act.activation(SL, ps[:, 5, :].rearrange("p (k s) -> p k s", k=4)[:, :, 0:SLOTS], ACT.Silu
                                           ).then_inc(silu_ready, 1)
                            if e == 1:
                                act.wait_ge(g_ps, i * 2 + (p0 + b + 1))
                                act.activation(G[:, b, :, :], ps[:, 6, 0:T].rearrange("p (t q) -> p t q", t=NT), ACT.Copy
                                               ).then_inc(g_ready, 1)
                            act.wait_ge(chunks_used, n * EXPERT_CHUNKS + (FRONT_CHUNKS + EXPERT_CHUNKS))
                            for m in range(2):
                                for half in range(2):
                                    ins = act.activation(Y[64 * e:64 * e + 64, b, 512 * (2 * m + half):512 * (2 * m + half) + 512],
                                                         ps[64 * half:64 * half + 64, 3 + m, :], ACT.Copy)
                            ins.then_inc(y_ready, 1)

            act.wait_ge(pe_ready, NT)
            expert_round(0, 0)
            act.wait_ge(rounds_ready, 1)
            rounds = act.value_load(rounds_i[0:1, 0:1], min_val=1, max_val=ROUNDS)
            with act.If(rounds > 1):
                with act.Fori(1, rounds) as r:
                    expert_round(r * NE, r * PAIRS)
                act.nop()
            with act.Else():
                act.nop()
            copy_hT(2)
            act.wait_ge(moe_done, 1)
            for t in range(NT):
                act.activation(hs_t[:, t, :], h[:, t, :], ACT.Square, accum_out=ss[:, t:t + 1]).then_inc(ss_ready, 1)
            for u in range(2 * 4):
                act.wait_ge(z_ready, u + 1)
                act.activation(z[:, u % 4, :], z[:, u % 4, :], ACT.Sigmoid).then_inc(gate_ready, 1)

        @block.vector
        def _(dve):
            steps = [0]

            def step(ins):
                steps[0] += 1
                ins.then_inc(dve_step, 1)
                dve.wait_ge(dve_step, steps[0])

            def copy_hT(j):
                for b in range(1, 8, 2):
                    dve.wait_ge(hT_ps, 8 * j + b + 1)
                    for u in range(2):
                        k = 2 * b + u
                        dve.tensor_scalar(hT[:, k, :], ps[:, b, T * u:T * u + T], gain(j, k), None,
                                          ALU.mult).then_inc(hT_dve, 1)

            def mean_squares(j):
                dve.tensor_scalar(ss[:, 2:2 + NT], ss[:, 0:NT], 1.0 / D, EPS, ALU.mult, ALU.add).then_inc(ms_ready, 1)
                dve.wait_ge(rstd_ready, j + 1)

            dve.wait_ge(x_loaded[1], 16)
            step(dve.tensor_tensor_reduce(out=junk[:, 1, :], in0=h[:, 1, :], in1=h[:, 1, :], scale=1.0, scalar=0.0,
                                          op0=ALU.mult, op1=ALU.add, accum_out=ss[:, 1:2]))
            dve.wait_ge(ss_ready, 1)
            mean_squares(0)
            dve.tensor_scalar(hs_t[:, 1, :], h[:, 1, :], rstd[:, 1:2], None, ALU.mult).then_inc(hs_dve, 1)
            dve.wait_ge(prm_ps, 1)
            step(dve.tensor_copy(prmT[:, :], ps[:, 0, 0:112]))
            dve.tensor_scalar(sp[:, 4, :], prmT[:, 56:64], -1.0, 0.0, ALU.mult, ALU.max).then_inc(prm_ready, 1)
            dve.wait_ge(prm_ready, 1)
            step(dve.tensor_scalar(sp[:, 5, :], prmT[:, 56:64], 0.0, None, ALU.min))
            dve.scalar_tensor_tensor(out=sp[:, 0, :], in0=sp[:, 5, :], scalar=2.0, in1=prmT[:, 56:64],
                                     op0=ALU.mult, op1=ALU.subtract).then_inc(lam_sum, 1)
            copy_hT(0)
            dve.wait_ge(lam_exp, 1)
            dve.tensor_scalar(sp[:, 2, :], sp[:, 1, :], 1.0, None, ALU.add).then_inc(lam_sum, 1)
            dve.wait_ge(lam_sum, 2)
            dve.wait_ge(lam_ln, 1)
            step(dve.tensor_scalar(sp[:, 5, :], sp[:, 2, :], 1.0, None, ALU.is_equal))
            step(dve.scalar_tensor_tensor(out=sp[:, 2, :], in0=sp[:, 2, :], scalar=-1.0, in1=sp[:, 5, :],
                                          op0=ALU.add, op1=ALU.add))
            step(dve.reciprocal(sp[:, 2, :], sp[:, 2, :]))
            step(dve.tensor_tensor(sp[:, 3, :], sp[:, 3, :], sp[:, 2, :], ALU.mult))
            step(dve.tensor_tensor(sp[:, 3, :], sp[:, 3, :], sp[:, 5, :], ALU.add))
            step(dve.tensor_tensor(sp[:, 3, :], sp[:, 3, :], sp[:, 1, :], ALU.mult))
            step(dve.tensor_tensor(sp[:, 5, :], sp[:, 3, :], sp[:, 4, :], ALU.add))
            dve.tensor_scalar(sp[:, 5, :], sp[:, 5, :], 4.0, None, ALU.mult).then_inc(lam_ready, 1)
            dve.wait_ge(small_loaded, 16 * 7)
            step(dve.tensor_copy(rstd[:, 2:4], pos_i[:, :]))
            for f in range(HALF):
                ins = dve.tensor_scalar(angles[:, 2, :, f], rstd[:, 2:4],
                                        float(np.float32(THETA) ** np.float32(-2.0 * f / ROT)), None, ALU.mult)
            step(ins)
            step(dve.tensor_scalar(angles[:, 3, :, :], angles[:, 2, :, :], 1 / (2 * math.pi), None, ALU.mult))
            step(dve.tensor_scalar(angles[:, 3, :, :], angles[:, 3, :, :], ROUND_MAGIC, None, ALU.add))
            step(dve.tensor_scalar(angles[:, 3, :, :], angles[:, 3, :, :], -ROUND_MAGIC, None, ALU.add))
            for cpi in (TWO_PI_1, TWO_PI_2, TWO_PI_3, TWO_PI_4):
                step(dve.scalar_tensor_tensor(out=angles[:, 2, :, :], in0=angles[:, 3, :, :], scalar=-cpi,
                                              in1=angles[:, 2, :, :], op0=ALU.mult, op1=ALU.add))
            step(dve.tensor_scalar(angles[:, 0, :, :], angles[:, 2, :, :], PI_BELOW, -PI_BELOW, ALU.min, ALU.max))
            step(dve.scalar_tensor_tensor(out=angles[:, 4, :, :], in0=angles[:, 0, :, :], scalar=-1.0,
                                          in1=angles[:, 0, :, :], op0=ALU.mult, op1=ALU.max))
            dve.tensor_scalar(angles[:, 1, :, :], angles[:, 4, :, :], -1.0, math.pi / 2, ALU.mult, ALU.add
                              ).then_inc(ang_ready, 1)

            dve.wait_ge(xl_pad, 1)
            dve.wait_ge(xl_ready, 2)
            for j in range(CONV_W):
                for c in range(CB):
                    tap = prmT[:, 8 * j + c:8 * j + c + 1]
                    if j == 0:
                        ins = dve.tensor_scalar(xc[:, c, :], xl[:, c, 0:T], tap, prmT[:, 32 + c:33 + c], ALU.mult, ALU.add)
                    else:
                        ins = dve.scalar_tensor_tensor(out=xc[:, c, :], in0=xl[:, c, j:j + T], scalar=tap,
                                                       in1=xc[:, c, :], op0=ALU.mult, op1=ALU.add)
                if j < CONV_W - 1:
                    step(ins)
            ins.then_inc(xc_ready, 1)

            dve.wait_ge(gates_ready, CB)
            dve.tensor_tensor(t2, t2, xc, ALU.mult)
            dve.wait_ge(tanh_ready, 1)
            step(dve.tensor_scalar(xl_flat, t1, 1.0, None, ALU.add))
            dve.reciprocal(xl_flat, xl_flat).then_inc(recip_done, 1)
            dve.wait_ge(recip_done, 1)
            dve.tensor_scalar(xc, xl_flat, 2.0, -1.0, ALU.mult, ALU.add)
            dve.wait_ge(sqrt_ready, 1)
            step(dve.scalar_tensor_tensor(out=xl_flat, in0=t1, scalar=2.0, in1=xl_flat, op0=ALU.mult, op1=ALU.mult))
            step(dve.tensor_tensor(t2, t2, xl_flat, ALU.mult))
            for c in range(CB):
                ins = dve.tensor_tensor_scan(xl_flat[:, c, :], xc[:, c, :], t2[:, c, :], 0.0, ALU.mult, ALU.add)
            step(ins)
            dve.tensor_tensor(gt, gt, xl_flat, ALU.mult).then_inc(y_lru, 1)
            dve.wait_ge(ssA_ps, 1)
            dve.tensor_scalar(ss[:, 4:6], ps[:, 0, 0:NT], 1.0 / D_LRU, EPS, ALU.mult, ALU.add).then_inc(msA_ready, 1)

            for t in range(NT):
                dve.wait_ge(qsq_ready, t + 1)
                step(dve.tensor_reduce(ssq[:, t, :], sqk[t], AX, ALU.add))
                dve.tensor_scalar(ssq[:, t, :], ssq[:, t, :], 1.0 / HD, EPS, ALU.mult, ALU.add).then_inc(qms_ready, 1)
                dve.wait_ge(qr_ready, t + 1)
                q_ = qk[:, t, :, :]
                step(dve.tensor_tensor(q_, q_, rqk[:, t, :].unsqueeze(2).to_broadcast([P, QK, HD]), ALU.mult))
                for w, (lo, n) in enumerate(((0, HEADS), (HEADS, KV))):
                    ins = dve.tensor_tensor(qk[:, t, lo:lo + n, :], qk[:, t, lo:lo + n, :],
                                            gqk[:, w, :].unsqueeze(1).to_broadcast([P, n, HD]), ALU.mult)
                step(ins)
                if t == 0:
                    dve.wait_ge(trig_ready, 1)
                sin = trig[:, 0, t, :].unsqueeze(1).to_broadcast([P, QK, HALF])
                cos = trig[:, 1, t, :].unsqueeze(1).to_broadcast([P, QK, HALF])
                a_, b_ = qk[:, t, :, 0:HALF], qk[:, t, :, HALF:ROT]
                dve.tensor_tensor(rope[:, 0, :, :], a_, cos, ALU.mult)
                dve.tensor_tensor(rope[:, 1, :, :], b_, sin, ALU.mult)
                dve.tensor_tensor(rope[:, 2, :, :], b_, cos, ALU.mult)
                step(dve.tensor_tensor(rope[:, 3, :, :], a_, sin, ALU.mult))
                dve.tensor_tensor(a_, rope[:, 0, :, :], rope[:, 1, :, :], ALU.subtract)
                dve.tensor_tensor(b_, rope[:, 2, :, :], rope[:, 3, :, :], ALU.add).then_inc(qk_ready, 1)
                dve.wait_ge(qk_ready, t + 1)

            def add_w_out(part_, n, ready):
                dve.wait_ge(chunks_used, (WOUT_A, WOUT_B)[part_] + 2 * (n + 1))
                for t in range(NT):
                    piece = h[:, t, 512 * n:512 * n + 512]
                    ins = dve.scalar_tensor_tensor(out=piece, in0=ps[:, 2 * ((n + 1) % 2) + t, :],
                                                   scalar=rstd[:, 4 + 2 * part_ + t:5 + 2 * part_ + t], in1=piece,
                                                   op0=ALU.mult, op1=ALU.add)
                ins.then_inc(ready, 1)

            dve.wait_ge(rA_ready, 1)
            dve.wait_ge(hs_act, 1)
            add_w_out(0, 0, hA_ready)
            for t in range(NT):
                dve.wait_ge(kT_ps, t + 1)
                dve.tensor_copy(kT[:, :, P * t:P * t + P], ps[:, 6 + t, :].rearrange("p (g q) -> p g q", g=KV)
                                ).then_inc(kT_ready, 1)
            add_w_out(0, 1, hA_ready)
            dve.wait_ge(s_masked, 1)
            for t in range(NT):
                dve.wait_ge(S_ready, t + 1)
                mx, sk = stat[:, 3 * t, :], stat[:, 3 * t + 1, :]
                step(dve.tensor_reduce(mx, S[t], AX, ALU.max))
                step(dve.tensor_tensor(mx, mx, sink_bc[:, :], ALU.max))
                dve.tensor_tensor(S[t], S[t], mx.unsqueeze(2).to_broadcast([P, HEADS, P]), ALU.subtract).then_inc(shifted, 1)
                dve.tensor_tensor(sk, sink_bc[:, :], mx, ALU.subtract).then_inc(sink_shifted, 1)
                add_w_out(0, 2 + t, hA_ready)
            for t in range(NT):
                den = stat[:, 3 * t + 2, :]
                dve.wait_ge(exp_ready, t + 1)
                step(dve.tensor_reduce(den, S[t], AX, ALU.add))
                dve.wait_ge(sink_exp, t + 1)
                step(dve.tensor_tensor(den, den, stat[:, 3 * t + 1, :], ALU.add))
                step(dve.reciprocal(den, den))
                dve.wait_ge(PT_ps, t + 1)
                if t:
                    dve.wait_ge(pv_ps, t)
                for b in range(2, 4):
                    ins = dve.tensor_copy(PT[:, 4 * b:4 * b + 4, :], ps[:, 4 + b, :].rearrange("p (j q) -> p j q", j=4))
                ins.then_inc(PT_dve, 1)
                dve.wait_ge(pv_ps, t + 1)
                for b in range(2):
                    ins = dve.tensor_tensor(yat[:, t, 8 * b:8 * b + 8, :],
                                            ps[:, 2 * (1 - t) + b, :].rearrange("p (h d) -> p h d", h=8),
                                            den[:, 8 * b:8 * b + 8].unsqueeze(2).to_broadcast([P, 8, HD]), ALU.mult)
                ins.then_inc(yat_ready, 1)
            dve.wait_ge(yT_ps, 1)
            for c in range(4, CB):
                dve.tensor_scalar(yT[:, c, :], ps[:, 4 + c // 2, T * (c % 2):T * (c % 2) + T],
                                  prmT[:, 72 + c:73 + c], None, ALU.mult).then_inc(yT_dve, 1)
            dve.wait_ge(ssB_ready, 2)
            dve.tensor_scalar(ss[:, 6:8], ss[:, 6:8], 1.0 / (HEADS * HD), EPS, ALU.mult, ALU.add).then_inc(msB_ready, 1)
            dve.wait_ge(rB_ready, 1)
            dve.wait_ge(hA_ready, 4)
            for n in range(4):
                add_w_out(1, n, h_ready)

            dve.wait_ge(ss1_ready, 1)
            step(dve.tensor_reduce(ss[:, 0:NT], pieces[:, 0, :, :], AX, ALU.add))
            mean_squares(1)
            dve.tensor_scalar(hs[:, 1, :, :], h[:, 1, :].rearrange("p (m k) -> p k m", k=KD), rstd[:, 1:2], None,
                              ALU.mult).then_inc(hs_dve, 1)
            copy_hT(1)
            gl, el = lg[:, :, 0:GROUPS], route[:, 0, :, :]
            dve.wait_ge(route_consts, 4)
            dve.wait_ge(logits_ps, 1)
            for t in range(NT):
                ins = dve.tensor_tensor(lg[:, t, :], ps[:, 1, 64 * t:64 * t + NL], br_bc[:, :], ALU.add)
            step(ins)

            def col(n):
                return rcol[:, n, :]

            def wide(c, n):
                return c.unsqueeze(2).to_broadcast([P, NT, n])

            def first_of(hot, logits, top, n, s0, s1):
                step(dve.tensor_tensor(hot, logits, wide(top, n), ALU.is_equal))
                ids = idx[:, 0:n].unsqueeze(1).to_broadcast([P, NT, n])
                step(dve.scalar_tensor_tensor(out=s0, in0=hot, scalar=-1000.0, in1=ids, op0=ALU.mult, op1=ALU.add))
                step(dve.tensor_reduce(s1, s0, AX, ALU.min))
                step(dve.tensor_tensor(hot, s0, wide(s1, n), ALU.is_equal))

            ghot = route[:, 1, :, 0:GROUPS]
            step(dve.tensor_reduce(col(0), gl, AX, ALU.max))
            first_of(ghot, gl, col(0), GROUPS, route[:, 2, :, 0:GROUPS], col(1))
            dve.tensor_tensor(gl, gl, wide(col(0), GROUPS), ALU.subtract).then_inc(gmax_ready, 1)
            gh = ghot.unsqueeze(3).to_broadcast([P, NT, GROUPS, PER_GROUP])

            def by_group(a):
                return a.rearrange("p t (g e) -> p t g e", g=GROUPS)

            for t in range(NT):
                ins = dve.tensor_tensor(by_group(el)[:, t], by_group(lg[:, :, GROUPS:NL])[:, t], gh[:, t], ALU.mult)
            step(ins)
            step(dve.tensor_scalar(route[:, 3, :, 0:GROUPS], ghot, -1.0, -NEG, ALU.add, ALU.mult))
            gn = route[:, 3, :, 0:GROUPS].unsqueeze(3).to_broadcast([P, NT, GROUPS, PER_GROUP])
            for t in range(NT):
                ins = dve.tensor_tensor(by_group(el)[:, t], by_group(el)[:, t], gn[:, t], ALU.add)
            step(ins)
            hot1, hot2 = route[:, 4, :, :], route[:, 5, :, :]
            step(dve.tensor_reduce(col(1), el, AX, ALU.max))
            first_of(hot1, el, col(1), NE, route[:, 6, :, :], col(5))
            step(dve.scalar_tensor_tensor(out=el, in0=hot1, scalar=10 * NEG, in1=el, op0=ALU.mult, op1=ALU.add))
            step(dve.tensor_reduce(col(2), el, AX, ALU.max))
            first_of(hot2, el, col(2), NE, route[:, 6, :, :], col(5))
            chosen = route[:, 7, :, :]
            dve.tensor_tensor(chosen, hot1, hot2, ALU.add).then_inc(chosen_ready, 1)
            dve.tensor_tensor(col(3), col(2), col(1), ALU.subtract).then_inc(e_diff, 1)
            dve.wait_ge(gexp_ready, 1)
            step(dve.tensor_reduce(col(6), gl, AX, ALU.add))
            dve.wait_ge(e_exp, 1)
            step(dve.tensor_scalar(col(7), col(4), 1.0, None, ALU.add))
            step(dve.tensor_tensor(col(6), col(6), col(7), ALU.mult))
            step(dve.reciprocal(col(6), col(6)))
            step(dve.tensor_tensor(col(7), col(6), col(4), ALU.mult))
            step(dve.tensor_tensor(hot1, hot1, wide(col(6), NE), ALU.mult))
            step(dve.tensor_tensor(hot2, hot2, wide(col(7), NE), ALU.mult))
            dve.tensor_tensor(comb[:, :, :], hot1, hot2, ALU.add)
            dve.wait_ge(chosen_ready, 1)
            dve.wait_ge(rank_ps, 1)
            step(dve.scalar_tensor_tensor(out=route[:, 8, :, :], in0=ps[:, 2, 0:NT * NE].rearrange("p (t e) -> p t e", t=NT),
                                          scalar=1.0, in1=chosen, op0=ALU.add, op1=ALU.mult))
            step(dve.tensor_scalar(rankm[:, :, 0:NE], route[:, 8, :, :], -1.0, None, ALU.add))
            most, cnt = rcol[0:1, 8, 0:1], rcol[0:1, 9, 0:1]
            step(dve.tensor_reduce(most, ps[0:1, 2, NT * NE:NT * NE + NE], AX, ALU.max))
            step(dve.tensor_scalar(cnt, most, float(SLOTS), 1.0, ALU.is_gt, ALU.add))
            for r in range(2, ROUNDS):
                step(dve.scalar_tensor_tensor(out=cnt, in0=most, scalar=float(SLOTS * r), in1=cnt,
                                              op0=ALU.is_gt, op1=ALU.add))
            dve.tensor_copy(rounds_i[:, :], cnt).then_inc(rounds_ready, 1)

            dve.wait_ge(pe_raw, 8)
            step(dve.tensor_reduce(ss[:, 4:6], pieces[:, 1, :, :], AX, ALU.add))
            dve.tensor_scalar(ss[:, 4:6], ss[:, 4:6], 1.0 / D, EPS, ALU.mult, ALU.add).then_inc(msp_ready, 1)

            def select(b, first):
                for e in range(2):
                    for t in range(NT):
                        ins = dve.tensor_scalar(SEL[:, b, t, SLOTS * e:SLOTS * e + SLOTS], slot_ids[:, :],
                                                rankm[:, t, first(e)], None, ALU.is_equal)
                ins.then_inc(sel_ready, 1)

            def spread(b, q, count):
                dve.wait_ge(gather_ps, count + 1)
                dve.tensor_tensor(XG[:, b, 4 * q:4 * q + 4, :], ps[:, 1 + q % 2, :].rearrange("p (k s) -> p k s", k=4),
                                  g_moe_pk[:, 4 * q:4 * q + 4].unsqueeze(2).to_broadcast([P, 4, P]), ALU.mult
                                  ).then_inc(xg_ready, 1)

            def accumulate(u, count):
                t, n = divmod(u, 4)
                dve.wait_ge(scatter_ps, count + (u + 1))
                piece = h[:, t, 512 * n:512 * n + 512]
                dve.tensor_tensor(piece, ps[:, 6 + u % 2, :], piece, ALU.add).then_inc(acc_done, 1)

            def expert_round(r):
                select(0, lambda e: slice(e, e + 1))
                for q in range(4):
                    spread(0, q, r * GATHERS + q)
                with dve.Fori(0, PAIRS // 2) as i:
                    for b in range(2):
                        pair = i * 2 + b
                        quarters = r * GATHERS + (pair + 1) * 4
                        units = r * SCATTERS + pair * 8
                        select(1 - b, lambda e: bass.ds(pair * 2 + (2 + e), 1))
                        accumulate(0, units)
                        for e in range(2):
                            for t in range(NT):
                                col_e = bass.ds(pair * 2 + e, 1)
                                ins = dve.tensor_scalar(SELW[:, t, SLOTS * e:SLOTS * e + SLOTS], slot_ids[:, :],
                                                        rankm[:, t, col_e], comb[:, t, col_e], ALU.is_equal, ALU.mult)
                        ins.then_inc(selw_ready, 1)
                        for e in range(2):
                            for u in range(1 if e == 0 else 4, 4 * e + 4):
                                accumulate(u, units)
                            spread(1 - b, 2 * e, quarters + 2 * e)
                            dve.wait_ge(silu_ready, r * NE + pair * 2 + (e + 1))
                            dve.tensor_tensor(HDN, SL, ps[:, 5, :].rearrange("p (k s) -> p k s", k=4)[:, :, SLOTS:2 * SLOTS],
                                              ALU.mult).then_inc(hdn_ready, 1)
                            spread(1 - b, 2 * e + 1, quarters + (2 * e + 1))
                for u in range(8):
                    accumulate(u, r * SCATTERS + PAIRS * 8)

            expert_round(0)
            dve.wait_ge(rounds_ready, 1)
            rounds = dve.value_load(rounds_i[0:1, 0:1], min_val=1, max_val=ROUNDS)
            with dve.If(rounds > 1):
                with dve.Fori(1, rounds) as r:
                    dve.tensor_scalar(slot_ids[:, :], slot_ids[:, :], float(SLOTS), None, ALU.add)
                    dve.memset(G[:, 1, :, :], 0.0).then_inc(g_ready, 1)
                    dve.wait_ge(g_ready, r * (PAIRS + 1) + 1)
                    expert_round(r)
                dve.nop()
            with dve.Else():
                dve.nop()
            dve.wait_ge(acc_done, rounds * SCATTERS)
            dve.nop().then_inc(moe_done, 1)

            copy_hT(2)
            dve.wait_ge(ss_ready, 3)
            mean_squares(2)
            dve.wait_ge(rp_ready, 1)
            dve.wait_ge(bpg_loaded, 16)

            def gate_in(u):
                n, t = divmod(u, NT)
                if t == 0:
                    dve.wait_ge(tail_used, 4 * (n + 1))
                if u >= 4:
                    dve.wait_ge(out_stored[u % 4], 16)
                dve.scalar_tensor_tensor(out=z[:, u % 4, :], in0=ps[:, u, :], scalar=rstd[:, t:t + 1],
                                         in1=bpg[:, 512 * n:512 * n + 512], op0=ALU.mult, op1=ALU.add).then_inc(z_ready, 1)

            def gate_out(u):
                n, t = divmod(u, NT)
                dve.wait_ge(gate_ready, u + 1)
                step(dve.scalar_tensor_tensor(out=z[:, u % 4, :], in0=z[:, u % 4, :], scalar=r_ple[:, t:t + 1],
                                              in1=pe[:, t, 512 * n:512 * n + 512], op0=ALU.mult, op1=ALU.mult))
                dve.tensor_tensor(z[:, u % 4, :], z[:, u % 4, :], h[:, t, 512 * n:512 * n + 512], ALU.add).then_inc(out_ready, 1)

            for n in range(4):
                for t in range(NT):
                    gate_in(2 * n + t)
                for t in range(NT):
                    gate_out(2 * n + t)

        @block.tensor
        def _(pe_):
            mm = pe_.matmul
            pe_.wait_ge(consts_ready, 1)
            pe_.wait_ge(prm_loaded, 16 * 9)
            pe_.transpose(ps[:, 0, 0:112], prm[0:112, :], ident[0:112, 0:112]).then_inc(prm_ps, 1)

            def transpose_h(source):
                for b in range(8):
                    for u in range(2):
                        for t in range(NT):
                            ins = pe_.transpose(ps[:, b, T * u + P * t:T * u + P * t + P], source(t, 2 * b + u), ident[:, :])
                    ins.then_inc(hT_ps, 1)

            def copied(j, blocks):
                pe_.wait_ge(hT_act, 8 * j + 2 * blocks)
                pe_.wait_ge(hT_dve, 8 * j + 2 * blocks)

            pe_.wait_ge(hs_act, 1)
            pe_.wait_ge(hs_dve, 1)
            pe_.wait_ge(prm_ready, 1)
            transpose_h(lambda t, k: hs_t[:, t, P * k:P * k + P])

            def chunk(c):
                pe_.wait_ge(loaded[c % RING], 16 * (c // RING + 1))
                return ring4(c % RING)

            for g in range(WIN_GROUPS):
                bank = (0, 4, 0, 4, 2, 4, 6)[g]
                if g == 2 or g == 3:
                    pe_.wait_ge(xl_ready, g - 1)
                if g == 4:
                    pe_.wait_ge(gelu_ready, 1)
                    pe_.wait_ge(xc_ready, 1)
                    pe_.wait_ge(bd_loaded, 64)
                    for cb in range(CB):
                        if cb >= 2:
                            pe_.wait_ge(gates_ready, cb - 1)
                        for w in range(2):
                            ins = mm(ps[:, cb % 2, T * w:T * w + T], bd[:, w, cb, :], xc[:, cb, :], start=True, stop=True)
                        ins.then_inc(gates_ps, 1)
                if g == 5:
                    pe_.wait_ge(gelu_ready, 2)
                for kq in range(4):
                    if g == 0:
                        copied(0, max(2, kq + 1))
                    w = chunk(4 * g + kq)
                    for kk in range(4):
                        k = 4 * kq + kk
                        if g < 4:
                            for cb in range(4):
                                ins = mm(ps[:, bank + cb, 0:T], w[:, kk, P * cb:P * cb + P], hT[:, k, :],
                                         start=(k == 0), stop=(k == KD - 1))
                        else:
                            for t in range(NT):
                                ins = mm(ps[:, bank + t, :], hT[:, k, P * t:P * t + P], w[:, kk, :],
                                         start=(k == 0), stop=(k == KD - 1))
                    ins.then_inc(chunks_used, 1)

            def w_out_columns(part_, n):
                for cq in range(2):
                    w = chunk((WOUT_A, WOUT_B)[part_] + 2 * n + cq)
                    for kk in range(4):
                        cc = 4 * cq + kk
                        for t in range(NT):
                            ins = mm(ps[:, 2 * ((n + 1) % 2) + t, :], (gt, yT)[part_][:, cc, P * t:P * t + P], w[:, kk, :],
                                     start=(cc == 0), stop=(cc == CB - 1))
                    ins.then_inc(chunks_used, 1)

            pe_.wait_ge(ysq_ready, 1)
            pe_.wait_ge(gates_ready, CB)
            for t in range(NT):
                for cb in range(CB):
                    ins = mm(ps[:, 0, t:t + 1], t1[:, cb, P * t:P * t + P], ones_c[:, 0:1], start=(cb == 0), stop=(cb == CB - 1))
            ins.then_inc(ssA_ps, 1)
            pe_.wait_ge(yg_ready, CB)
            pe_.wait_ge(qkv_ready, 1)
            w_out_columns(0, 0)
            pe_.wait_ge(qk_ready, NT)
            pe_.wait_ge(qkv_ready, 4)
            for t in range(NT):
                if t:
                    pe_.wait_ge(qT_ready, t)
                for j in range(CB):
                    ins = pe_.transpose(ps[:, 4 + j // 4, P * (j % 4):P * (j % 4) + P],
                                        qk[:, t, 2 * j:2 * j + 2, :].rearrange("p h d -> p (h d)"), ident[:, :])
                ins.then_inc(qT_ps, 1)
                for kh in range(KV):
                    for half in range(2):
                        ins = mm(ps[64 * half:64 * half + 64, 6 + t, P * kh:P * kh + P], qk[:, t, HEADS + kh, :],
                                 ident[:, :], start=True, stop=True)
                ins.then_inc(kT_ps, 1)
            pe_.wait_ge(msA_ready, 1)
            w_out_columns(0, 1)
            pe_.wait_ge(qT_ready, 2)
            pe_.wait_ge(kT_ready, 2)
            for t in range(NT):
                if t:
                    pe_.wait_ge(S_ready, t)
                for j in range(CB):
                    for q in range(2):
                        n = 2 * t + q
                        lo = max(0, CHUNK * (n - 1))
                        hi = CHUNK * (n + 1)
                        for two in range(2):
                            hh = 2 * j + two
                            at = P * (j % 4) + P - (hi - lo)
                            ins = mm(ps[64 * q:64 * q + 64, 4 + 2 * (j // 4) + two, at:at + hi - lo],
                                     qT[64 * two:64 * two + 64, j, CHUNK * n:CHUNK * n + CHUNK],
                                     kT[64 * two:64 * two + 64, hh // 4, lo:hi], start=True, stop=True)
                ins.then_inc(scores_ps, 1)
                pe_.wait_ge(hA_ready, t + 1)
                w_out_columns(0, 2 + t)
            pe_.wait_ge(S_ready, 2)
            for t in range(NT):
                pe_.wait_ge(exp_ready, t + 1)
                for hh in range(HEADS):
                    ins = pe_.transpose(ps[:, 4 + hh // 4, P * (hh % 4):P * (hh % 4) + P], S[t][:, hh, :], ident[:, :])
                ins.then_inc(PT_ps, 1)
                pe_.wait_ge(PT_act, t + 1)
                pe_.wait_ge(PT_dve, t + 1)
                pe_.wait_ge(hA_ready, 3 + t)
                for hh in range(HEADS):
                    for q in range(2):
                        vals = (vs if q == 0 else v)[:, t, hh // 4, :]
                        ins = mm(ps[64 * q:64 * q + 64, 2 * (1 - t) + hh // 8, HD * (hh % 8):HD * (hh % 8) + HD],
                                 PT[:, hh, 64 * q:64 * q + 64], vals, start=True, stop=True)
                ins.then_inc(pv_ps, 1)
            pe_.wait_ge(yat_ready, 2)
            for cb in range(CB):
                for t in range(NT):
                    at = T * (cb % 2) + P * t
                    ins = pe_.transpose(ps[:, 4 + cb // 2, at:at + P],
                                        yat[:, t, 2 * cb:2 * cb + 2, :].rearrange("p h d -> p (h d)"), ident[:, :])
            ins.then_inc(yT_ps, 1)
            pe_.wait_ge(yT_act, 4)
            pe_.wait_ge(yT_dve, 4)
            for n in range(4):
                if n >= 2:
                    pe_.wait_ge(h_ready, n - 1)
                w_out_columns(1, n)

            pe_.wait_ge(hs_act, 2)
            pe_.wait_ge(hs_dve, 2)
            transpose_h(lambda t, k: hs[:, t, k, :])
            pe_.wait_ge(wr_loaded, 32)
            for kq in range(4):
                copied(1, max(1, kq + 1))
                for k in range(4 * kq, 4 * kq + 4):
                    ins = mm(ps[0:NL, 0, 0:T], wr[:, k, :], hT[:, k, :], start=(k == 0), stop=(k == KD - 1))
            ins.then_inc(lT_ps, 1)
            pe_.wait_ge(ple_loaded, 32)
            for cc in range(2):
                for t in range(NT):
                    ins = pe_.transpose(ps[:, 3, T * cc + P * t:T * cc + P * t + P], pp[:, t, P * cc:P * cc + P], ident[:, :])
            ins.then_inc(pT_ps, 1)
            pe_.wait_ge(lT_ready, 1)
            for t in range(NT):
                ins = pe_.transpose(ps[:, 1, 64 * t:64 * t + NL], lT[0:NL, P * t:P * t + P], ident[0:NL, 0:NL])
            ins.then_inc(logits_ps, 1)
            pe_.wait_ge(pT_ready, 1)
            for cc in range(2):
                chunk(PLE + cc)
            for half in range(2):
                if half:
                    pe_.wait_ge(pe_raw, 4)
                for u in range(4):
                    n, t = 2 * half + u // 2, u % 2
                    for cc in range(2):
                        ins = mm(ps[:, 4 + u, :], pT[:, cc, P * t:P * t + P],
                                 ring[:, (PLE + cc) % RING, 512 * n:512 * n + 512], start=(cc == 0), stop=(cc == 1))
                ins.then_inc(ple_ps, 1)
            pe_.wait_ge(chosen_ready, 1)
            pe_.wait_ge(route_consts, 4)
            mm(ps[:, 2, 0:NE], before, route[:, 7, 0, :], start=True, stop=True)
            mm(ps[:, 2, NE:2 * NE], ones, route[:, 7, 0, :], start=True, stop=False)
            mm(ps[:, 2, NE:2 * NE], before, route[:, 7, 1, :], start=False, stop=True)
            for t in range(NT):
                ins = mm(ps[0:1, 2, 2 * NE:3 * NE], ones[:, 0:1], route[:, 7, t, :], start=(t == 0), stop=(t == NT - 1))
            ins.then_inc(rank_ps, 1)
            pe_.wait_ge(ple_ps, 2)
            pe_.nop().then_inc(chunks_used, 2)
            pe_.wait_ge(pe_raw, 8)

            def gather(b, q, count):
                for k in range(4 * q, 4 * q + 4):
                    for t in range(NT):
                        ins = mm(ps[:, 1 + q % 2, P * (k % 4):P * (k % 4) + P], hs[:, t, k, :], SEL[:, b, t, :],
                                 start=(t == 0), stop=(t == NT - 1))
                ins.then_inc(gather_ps, 1)

            def scatter(b, u, count):
                t, n = divmod(u, 4)
                if u >= 2:
                    pe_.wait_ge(acc_done, count + (u - 1))
                mm(ps[:, 6 + u % 2, :], G[:, b, t, :], Y[:, b, 512 * n:512 * n + 512], start=True, stop=True
                   ).then_inc(scatter_ps, 1)

            def expert_round(r):
                pe_.wait_ge(sel_ready, r * (PAIRS + 1) + 1)
                for q in range(4):
                    if q >= 2:
                        pe_.wait_ge(xg_ready, r * GATHERS + (q - 1))
                    gather(0, q, r * GATHERS + q)
                with pe_.Fori(0, PAIRS // 2) as i:
                    for b in range(2):
                        pair = i * 2 + b
                        quarters = r * GATHERS + pair * 4
                        units = r * SCATTERS + pair * 8
                        pe_.wait_ge(xg_ready, quarters + 4)
                        pe_.wait_ge(g_ready, r * (PAIRS + 1) + pair + 1)
                        pe_.wait_ge(y_ready, r * NE + pair * 2 + 1)
                        for e in range(2):
                            n = r * NE + pair * 2 + e

                            def arrived(j):
                                slot = (FRONT_CHUNKS + j) % RING
                                pe_.wait_ge(loaded[slot], n * 16 + 16 * (front_uses(slot) + 1))
                                return slot

                            for kq in range(4):
                                s1, s3 = arrived(2 * kq), arrived(2 * kq + 1)
                                for kk in range(4):
                                    k = 4 * kq + kk
                                    for half, s in ((0, s1), (1, s3)):
                                        ins = mm(ps[64 * half:64 * half + 64, 0, :], XG[:, b, k, SLOTS * e:SLOTS * e + SLOTS],
                                                 ring4(s)[:, kk, :], start=(k == 0), stop=(k == KD - 1))
                                        if kk == 3:
                                            ins.then_inc(chunks_used, 1)
                                scatter(1 - b, 4 * e + kq, units)
                            if e == 0:
                                pe_.wait_ge(sel_ready, r * (PAIRS + 1) + pair + 2)
                            else:
                                pe_.wait_ge(xg_ready, quarters + 5)
                            gather(1 - b, 2 * e, quarters)
                            pe_.wait_ge(h13_ready, n + 1)
                            for k in range(4):
                                ins = pe_.transpose(ps[:, 5, P * k:P * k + P], H13[:, k, :], ident[:, :])
                            ins.then_inc(h13T_ps, 1)
                            if e == 1:
                                pe_.wait_ge(xg_ready, quarters + 6)
                            gather(1 - b, 2 * e + 1, quarters)
                            if e == 1:
                                pe_.wait_ge(selw_ready, r * PAIRS + pair + 1)
                                pe_.wait_ge(acc_done, units + 7)
                                for t in range(NT):
                                    ins = pe_.transpose(ps[:, 6, P * t:P * t + P], SELW[:, t, :], ident[:, :])
                                ins.then_inc(g_ps, 1)
                                pe_.wait_ge(y_ready, n + 1)
                            pe_.wait_ge(hdn_ready, n + 1)
                            for k in range(4):
                                s = arrived(8 + k)
                                for m in range(2):
                                    for half in range(2):
                                        at = 1024 * m + 512 * half
                                        ins = mm(ps[64 * half:64 * half + 64, 3 + m, :], HDN[:, k, :], ring[:, s, at:at + 512],
                                                 start=(k == 0), stop=(k == 3))
                                ins.then_inc(chunks_used, 1)
                pe_.wait_ge(g_ready, r * (PAIRS + 1) + (PAIRS + 1))
                pe_.wait_ge(y_ready, r * NE + (NE + 1))
                pe_.wait_ge(xg_ready, r * GATHERS + GATHERS)
                for u in range(8):
                    scatter(1, u, r * SCATTERS + PAIRS * 8)

            expert_round(0)
            pe_.wait_ge(rounds_ready, 1)
            rounds = pe_.value_load(rounds_i[0:1, 0:1], min_val=1, max_val=ROUNDS)
            with pe_.If(rounds > 1):
                with pe_.Fori(1, rounds) as r:
                    expert_round(r)
                pe_.nop()
            with pe_.Else():
                pe_.nop()

            pe_.wait_ge(moe_done, 1)
            transpose_h(lambda t, k: h[:, t, P * k:P * k + P])
            for n in range(4):
                for kq in range(4):
                    c = 4 * n + kq
                    slot = (FRONT_CHUNKS + c) % RING
                    if n == 0:
                        copied(2, kq + 1)
                    elif kq == 0:
                        copied(2, 4)
                    pe_.wait_ge(tail_loaded[slot], 16 * (c // RING + 1))
                    for kk in range(4):
                        k = 4 * kq + kk
                        for t in range(NT):
                            ins = mm(ps[:, 2 * n + t, :], hT[:, k, P * t:P * t + P], ring4(slot)[:, kk, :],
                                     start=(k == 0), stop=(k == KD - 1))
                    ins.then_inc(tail_used, 1)


NAMES = ["x", "p", "positions", "g_mix", "w_in", "conv_w", "conv_b", "w_a", "b_a", "w_i", "b_i", "lam", "g_q", "g_k",
         "sinks", "g_out_lru", "g_out_attn", "w_out", "g_moe", "w_rg", "b_rg", "w_re", "b_re", "w1", "w3", "w2",
         "w_ple", "g_ple", "g_pg", "w_pg", "b_pg"]


def kernel(**inputs):
    import numpy as _np
    import concourse.bacc as _bacc
    from concourse import mybir as _mybir
    from concourse.bass_utils import run_bass_kernel_spmd as _run

    nc = _bacc.Bacc("TRN2", target_bir_lowering=False, num_devices=1)
    arrays, args = {}, {}
    for name in NAMES:
        a = _np.ascontiguousarray(inputs[name])
        arrays[f"in_{name}"] = a
        args[name] = nc.dram_tensor(f"in_{name}", a.shape, _mybir.dt.from_np(a.dtype), kind="ExternalInput").ap()
    args["out"] = nc.dram_tensor("out_h", (1, T, D), _mybir.dt.float32, kind="ExternalOutput").ap()
    build(nc, **args)
    got = _run(nc, [arrays], core_ids=[0])
    return got.results[0]["out_h"]
```

```python
import math
from contextlib import ExitStack

import numpy as np

import concourse.bass as bass
from concourse import mybir

P = 128
ALU = mybir.AluOpType
ACT = mybir.ActivationFunctionType
F32 = mybir.dt.float32
I32 = mybir.dt.int32
AX = mybir.AxisListType.X

T, D = 256, 2048
NT = T // P
KD = D // P
CHUNK = 64
EPS = 1e-6
D_LRU, CB = 1024, 8
CONV_W = 4
HEADS, KV, HD = 16, 4, 64
QK = HEADS + KV
ROT = HD // 4
HALF = ROT // 2
THETA = 500000.0
GROUPS, PER_GROUP = 4, 8
NE = GROUPS * PER_GROUP
D_EXP = 512
D_PLE = 256
NEG = -1e30
NL = GROUPS + NE

RING = 12
CH = 2048
WIN_GROUPS = (4, 5, 6, 0, 1, 2, 3)
WIN_CHUNKS = 4 * len(WIN_GROUPS)
BLOCKS_FROM = 4 * 3
WOUT_B = WIN_CHUNKS
WOUT_A = WIN_CHUNKS + 8
PLE = WIN_CHUNKS + 16
FRONT_CHUNKS = PLE + 2
EXPERT_CHUNKS = 12
ROUND_CHUNKS = NE * EXPERT_CHUNKS
TAIL_CHUNKS = 16
PAIRS = NE // 2
GATHERS = 4 * (PAIRS + 1)
SCATTERS = 8 * (PAIRS + 1)
SLOTS = 64
ROUNDS = T // SLOTS
assert ROUND_CHUNKS % RING == 0 and 4 * EXPERT_CHUNKS % RING == 0 and NL <= 36

TWO_PI_1 = 6.28125
TWO_PI_2 = math.floor((2 * math.pi - TWO_PI_1) * 2 ** 17) / 2 ** 17
TWO_PI_3 = math.floor((2 * math.pi - TWO_PI_1 - TWO_PI_2) * 2 ** 27) / 2 ** 27
TWO_PI_4 = 2 * math.pi - TWO_PI_1 - TWO_PI_2 - TWO_PI_3
ROUND_MAGIC = 1.5 * 2 ** 23
PI_BELOW = 3.1415925


AHEAD = 2


def slot_of(j, ahead=AHEAD):
    return (FRONT_CHUNKS - ahead + j) % RING


def build(nc, x, p, positions, g_mix, w_in, conv_w, conv_b, w_a, b_a, w_i, b_i, lam, g_q, g_k, sinks,
          g_out_lru, g_out_attn, w_out, g_moe, w_rg, b_rg, w_re, b_re, w1, w3, w2,
          w_ple, g_ple, g_pg, w_pg, b_pg, out):
    with ExitStack() as ctx:
        def sb(name, shape, dt=F32):
            return ctx.enter_context(nc.sbuf_tensor(name, shape, dt))

        def sem(name):
            return ctx.enter_context(nc.semaphore(name))

        ring = sb("ring", [P, RING, CH])
        h = sb("h", [P, NT, D])
        hs = sb("hs", [P, NT, KD, P])
        hT = sb("hT", [P, KD, T])
        area = sb("area", [P, 15128])
        ident = sb("ident", [P, P])
        prmT = sb("prmT", [P, 112])
        g_moe_pk = sb("g_moe_pk", [P, KD])
        gqk = sb("gqk", [P, 2, HD])
        sink_bc = sb("sink_bc", [P, HEADS])
        br_bc = sb("br_bc", [P, NL])
        pieces = sb("pieces", [P, 2, NT, 4])
        r_ple = sb("r_ple", [P, NT])
        idx = sb("idx", [P, NE])
        expo = sb("expo", [P, QK])
        ones_c = sb("ones_c", [P, 2])
        ss = sb("ss", [P, 8])
        rstd = sb("rstd", [P, 8])
        ssq = sb("ssq", [P, NT, QK])
        rqk = sb("rqk", [P, NT, QK])
        stat = sb("stat", [P, 6, HEADS])
        rounds_i = sb("rounds_i", [1, 1], I32)
        pos_i = sb("pos_i", [P, NT], I32)
        sp = sb("sp", [P, 6, CB])
        trig = sb("trig", [P, 2, NT, HALF])

        def part(lo, n, *dims):
            v = area[:, lo:lo + n]
            if len(dims) == 2:
                return v.rearrange("p (a b) -> p a b", a=dims[0])
            if len(dims) == 3:
                return v.rearrange("p (a b c) -> p a b c", a=dims[0], b=dims[1])
            if len(dims) == 4:
                return v.rearrange("p (a b c d) -> p a b c d", a=dims[0], b=dims[1], c=dims[2])
            return v

        xl = part(0, CB * (T + 3), CB, T + 3)
        xl_flat = part(0, CB * T, CB, T)
        xc = part(2072, CB * T, CB, T)
        t1 = part(4120, CB * T, CB, T)
        t2 = part(6168, CB * T, CB, T)
        gt = part(8216, CB * T, CB, T)
        qk = part(10264, NT * QK * HD, NT, QK, HD)
        yat = part(10264, NT * HEADS * HD, NT, HEADS, HD)
        v = part(12824, NT * KV * HD, NT, KV, HD)
        vs = part(13336, NT * KV * HD, NT, KV, HD)
        kT = part(13848, KV * T, KV, T)
        sqk = [part(4120, QK * HD, QK, HD), part(6168, QK * HD, QK, HD)]
        junkB = part(4120, 2048, 2, 1024)
        ysum = part(2072, T)
        rope = part(13848, 4 * QK * HALF, 4, QK, HALF)
        prm = part(13848, P)
        angles = part(14000, 6 * NT * HALF, 6, NT, HALF)
        hs_flat = hs[:, :, :, :].rearrange("p t k m -> p (t k m)")
        hT_flat = hT[:, :, :].rearrange("p k t -> p (k t)")
        hs_t = hs[:, :, :, :].rearrange("p t k m -> p t (k m)")
        bd = hs_flat[:, 0:2048].rearrange("p (w c j) -> p w c j", w=2, c=CB)
        S = [part(4120, HEADS * P, HEADS, P), part(6168, HEADS * P, HEADS, P)]
        qT = hs_flat[:, 2048:4096].rearrange("p (j t) -> p j t", j=CB)
        PT = hs_flat[:, 2048:4096].rearrange("p (h q) -> p h q", h=HEADS)
        yT = hs_flat[:, 2048:4096].rearrange("p (c t) -> p c t", c=CB)
        junk = hT[:, :, :].rearrange("p (a k) t -> p a (k t)", a=NT)
        XG = part(0, 2 * KD * P, 2, KD, P)
        Y = part(4096, 2 * D, 2, D)
        H13 = part(8192, D_EXP, 4, P)
        SL = part(8704, 256, 4, SLOTS)
        HDN = part(8960, 256, 4, SLOTS)
        SEL = part(9216, 512, 2, NT, P)
        SELW = part(9728, 256, NT, P)
        G = part(9984, 512, 2, NT, P)
        pe = part(10496, NT * D, NT, D)
        before = part(14592, P)
        ones = part(14720, P)
        pp = part(0, NT * D_PLE, NT, D_PLE)
        pT = part(512, 512, 2, T)
        wr = part(2048, KD * NL, KD, NL)
        gple = part(4096, D)
        junkP = part(6144, 2048, 4, 512)
        route = part(2624, 640, 10, NT, NE)
        lg = part(3264, NT * NL, NT, NL)
        rcol = part(3344, 24, 12, NT)
        rankm = sb("rankm", [P, NT, NE + 2])
        comb = sb("comb", [P, NT, NE])
        slot_ids = sb("slot_ids", [P, SLOTS])
        bpg = part(0, D)
        z = part(4096, 2048, 4, 512)

        ps = ctx.enter_context(nc.psum_tensor("ps", [P, 8, 512], F32))

        x_loaded = [sem(f"x_loaded{t}") for t in range(NT)]
        prm_loaded, small_loaded, bd_loaded = sem("prm_loaded"), sem("small_loaded"), sem("bd_loaded")
        wr_loaded, ple_loaded, bpg_loaded = sem("wr_loaded"), sem("ple_loaded"), sem("bpg_loaded")
        loaded = [sem(f"loaded{s}") for s in range(RING)]
        ahead_loaded = [sem(f"ahead_loaded{j}") for j in range(AHEAD)]
        tail_loaded = [sem(f"tail_loaded{s}") for s in range(RING)]
        chunks_used, tail_used = sem("chunks_used"), sem("tail_used")
        consts_ready = sem("consts_ready")
        pool_step, dve_step, act_step = sem("pool_step"), sem("dve_step"), sem("act_step")
        prm_ps, prm_ready = sem("prm_ps"), sem("prm_ready")
        ss_ready, ms_ready, rstd_ready = sem("ss_ready"), sem("ms_ready"), sem("rstd_ready")
        hs_act, hs_dve, hT_ps, hT_act, hT_dve = sem("hs_act"), sem("hs_dve"), sem("hT_ps"), sem("hT_act"), sem("hT_dve")
        qkv_ready, block_ps, block_copied = sem("qkv_ready"), sem("block_ps"), sem("block_copied")
        bd_zero, xl_pad, xc_ready = sem("bd_zero"), sem("xl_pad"), sem("xc_ready")
        gates_ps, gates_ready, tanh_ready, sqrt_ready = sem("gates_ps"), sem("gates_ready"), sem("tanh_ready"), sem("sqrt_ready")
        recip_done, y_lru, ysq_ready, yg_ready = sem("recip_done"), sem("y_lru"), sem("ysq_ready"), sem("yg_ready")
        lam_exp, lam_sum, lam_ln = sem("lam_exp"), sem("lam_sum"), sem("lam_ln")
        lam_ready = sem("lam_ready")
        ang_ready, trig_ready = sem("ang_ready"), sem("trig_ready")
        qsq_ready, qms_ready, qr_ready, qk_ready = (
            sem("qsq_ready"), sem("qms_ready"), sem("qr_ready"), sem("qk_ready"))
        qT_ps, qT_ready, kT_ps, kT_ready = sem("qT_ps"), sem("qT_ready"), sem("kT_ps"), sem("kT_ready")
        s_masked, scores_ps, S_ready, shifted, exp_ready = (
            sem("s_masked"), sem("scores_ps"), sem("S_ready"), sem("shifted"), sem("exp_ready"))
        sink_shifted, sink_exp = sem("sink_shifted"), sem("sink_exp")
        PT_ps, PT_act, PT_dve, pv_ps, yat_ready = sem("PT_ps"), sem("PT_act"), sem("PT_dve"), sem("pv_ps"), sem("yat_ready")
        yT_ps, yT_act, yT_dve = sem("yT_ps"), sem("yT_act"), sem("yT_dve")
        ssA_ps, msA_ready, rA_ready = sem("ssA_ps"), sem("msA_ready"), sem("rA_ready")
        ssB_ready, msB_ready, rB_ready = sem("ssB_ready"), sem("msB_ready"), sem("rB_ready")
        hB_ready, ss1_ready, A_ps = sem("hB_ready"), sem("ss1_ready"), sem("A_ps")
        ysum_ready, gate_ps = sem("ysum_ready"), sem("gate_ps")
        xnT_ps, xnT_act, xnT_dve = sem("xnT_ps"), sem("xnT_act"), sem("xnT_dve")
        h_ready = sem("h_ready")
        logits_ps, gmax_ready, gexp_ready, e_diff, e_exp = (
            sem("logits_ps"), sem("gmax_ready"), sem("gexp_ready"), sem("e_diff"), sem("e_exp"))
        chosen_ready, rank_ps, rounds_ready = sem("chosen_ready"), sem("rank_ps"), sem("rounds_ready")
        route_consts = sem("route_consts")
        sel_ready, gather_ps, xg_ready, h13_ready = (
            sem("sel_ready"), sem("gather_ps"), sem("xg_ready"), sem("h13_ready"))
        selw_ready, g_ps, g_ready, h13T_ps, silu_ready, hdn_ready = (
            sem("selw_ready"), sem("g_ps"), sem("g_ready"), sem("h13T_ps"), sem("silu_ready"), sem("hdn_ready"))
        y_ready, scatter_ps, acc_done, moe_done = (
            sem("y_ready"), sem("scatter_ps"), sem("acc_done"), sem("moe_done"))
        pT_ps, pT_ready, ple_ps, pe_raw, msp_ready, rp_ready, pe_ready = (
            sem("pT_ps"), sem("pT_ready"), sem("ple_ps"), sem("pe_raw"), sem("msp_ready"),
            sem("rp_ready"), sem("pe_ready"))
        z_ready, gate_ready, out_ready, out_stored = (
            sem("z_ready"), sem("gate_ready"), sem("out_ready"), [sem(f"out_stored{u}") for u in range(4)])

        x_v = x[0].rearrange("(t p) d -> p t d", p=P)
        out_v = out[0].rearrange("(t p) d -> p t d", p=P)
        p_v = p[0, 0].rearrange("(t p) c -> p t c", p=P)
        w_in_v = w_in[0].rearrange("(k p) n -> p k n", p=P)
        w_out_v = w_out[0].rearrange("(c p) n -> p c n", p=P)
        w_pg_v = w_pg[0].rearrange("(k p) n -> p k n", p=P)
        w_ple_v = w_ple[0].rearrange("(c p) n -> p c n", p=P)
        w1_v = w1[0].rearrange("e (p k) f -> e p k f", k=KD)
        w3_v = w3[0].rearrange("e (p k) f -> e p k f", k=KD)
        w2_v = w2[0].rearrange("e (p k) n -> e p k n", k=4)

        def gain(j, k):
            return prmT[:, (80, 96)[j] + k:(80, 96)[j] + k + 1]

        def h_by_k(t):
            return h[:, t, :].rearrange("p (m k) -> p k m", k=KD)

        B_BANKS = (2, 6, 4, 0)
        A_BANKS = ((3, 6, 7, 2), (4, 5, 0, 1))
        XN_BANKS = (2, 3, 6, 7)
        LAST_BANKS = (6, 7, 3, 4)
        PLE_BANKS = (5, 1, 6, 7, 3, 4, 0, 5)

        def ring4(slot):
            return ring[:, slot, :].rearrange("p (k n) -> p k n", k=4)

        block = ctx.enter_context(nc.Block())

        @block.sync
        def _(sp_q):
            for t in range(NT):
                sp_q.dma_start(h[:, t, :], x_v[:, t, :]).then_inc(x_loaded[t], 16)

            def front_chunk(c, src, flat=False):
                if c >= RING:
                    sp_q.wait_ge(chunks_used, c - RING + 1)
                slot = c % RING
                sp_q.dma_start(ring[:, slot, :] if flat else ring4(slot), src).then_inc(loaded[slot], 16)

            for g, cols in enumerate(WIN_GROUPS):
                for kq in range(4):
                    if g == 0 and kq == 0:
                        sp_q.wait_ge(prm_loaded, 16 * 9)
                    front_chunk(4 * g + kq, w_in_v[:, 4 * kq:4 * kq + 4, 512 * cols:512 * cols + 512])
            for c in range(16):
                part_, n, cq = c // 8, c // 2 % 4, c % 2
                rows4 = 8 * (1 - part_) + 4 * cq
                front_chunk(WOUT_B + c, w_out_v[:, rows4:rows4 + 4, 512 * n:512 * n + 512])
            for c in range(2):
                front_chunk(PLE + c, w_ple_v[:, c, :], flat=True)

            def expert_chunk(e, j, dst, signal):
                if j < 8:
                    src = (w1_v if j % 2 == 0 else w3_v)[bass.ds(e, 1), :, 4 * (j // 2):4 * (j // 2) + 4, :]
                    src = src.rearrange("a p k f -> p (a k) f")
                    dst = dst.rearrange("p (k n) -> p k n", k=4)
                else:
                    src = w2_v[bass.ds(e, 1), :, j - 8, :].rearrange("a p n -> p (a n)")
                sp_q.dma_start(dst, src).then_inc(signal, 16)

            for j in range(EXPERT_CHUNKS):
                if j == EXPERT_CHUNKS - 2:
                    sp_q.wait_ge(logits_ps, NT)
                    for a in range(AHEAD):
                        expert_chunk(1, a, hT_flat[:, CH * a:CH * a + CH], ahead_loaded[a])
                sp_q.wait_ge(chunks_used, FRONT_CHUNKS + j - RING + 1)
                expert_chunk(0, j, ring[:, slot_of(j, 0), :], loaded[slot_of(j, 0)])
            for c in range(EXPERT_CHUNKS):
                e, j = (1, AHEAD + c) if c < EXPERT_CHUNKS - AHEAD else (2, c - (EXPERT_CHUNKS - AHEAD))
                sp_q.wait_ge(chunks_used, FRONT_CHUNKS + c + 1)
                expert_chunk(e, j, ring[:, slot_of(j), :], loaded[slot_of(j)])
            for j in range(AHEAD, EXPERT_CHUNKS):
                sp_q.wait_ge(chunks_used, FRONT_CHUNKS + EXPERT_CHUNKS + j + 1)
                expert_chunk(2, j, ring[:, slot_of(j), :], loaded[slot_of(j)])

            def experts(first, used):
                with sp_q.Fori(first, NE) as e:
                    for j in range(EXPERT_CHUNKS):
                        sp_q.wait_ge(chunks_used, e * EXPERT_CHUNKS + (used + j - RING + 1))
                        expert_chunk(e, j, ring[:, slot_of(j), :], loaded[slot_of(j)])

            experts(3, FRONT_CHUNKS)
            sp_q.wait_ge(rounds_ready, 1)
            rounds = sp_q.value_load(rounds_i[0:1, 0:1], min_val=1, max_val=ROUNDS)
            with sp_q.If(rounds > 1):
                with sp_q.Fori(1, rounds) as r:
                    experts(0, r * ROUND_CHUNKS + FRONT_CHUNKS)
                sp_q.nop()
            with sp_q.Else():
                sp_q.nop()
            for c in range(TAIL_CHUNKS):
                slot = slot_of(c)
                if c < RING:
                    sp_q.wait_ge(chunks_used, rounds * ROUND_CHUNKS + (FRONT_CHUNKS + c - RING + 1))
                else:
                    sp_q.wait_ge(tail_used, c - RING + 1)
                n, kq = divmod(c, 4)
                sp_q.dma_start(ring4(slot), w_pg_v[:, 4 * kq:4 * kq + 4, 512 * n:512 * n + 512]
                               ).then_inc(tail_loaded[slot], 16)
            for u in range(2 * 4):
                n, t = divmod(u, NT)
                sp_q.wait_ge(out_ready, u + 1)
                sp_q.dma_start(out_v[:, t, 512 * n:512 * n + 512], z[:, u % 4, :]).then_inc(out_stored[u % 4], 16)
            for u in range(4):
                sp_q.wait_ge(out_stored[u], 16 * 2)

        @block.gpsimd
        def _(pool):
            steps = [0]

            def step(ins):
                steps[0] += 1
                ins.then_inc(pool_step, 1)
                pool.wait_ge(pool_step, steps[0])

            step(pool.memset(ident[:, :], 0.0))
            pool.affine_select(out=ident[:, :], in_=ident[:, :], compare_op=ALU.not_equal, fill=1.0, base=0,
                               pattern=[[-1, P]], channel_multiplier=1).then_inc(consts_ready, 1)
            pool.memset(ones_c[:, :], 1.0)
            pool.memset(expo[:, :], -0.5).then_inc(consts_ready, 1)
            pool.memset(xl[:, :, 0:3], 0.0).then_inc(xl_pad, 1)
            pool.memset(vs[0:64, 0, :, :], 0.0).then_inc(xl_pad, 1)
            pool.wait_ge(consts_ready, 2)

            def norm_root(j, lo=0, n=NT):
                pool.wait_ge(ms_ready, j + 1)
                pool.tensor_tensor(rstd[:, lo:lo + n], ss[:, 2 + lo:2 + lo + n], expo[:, 0:n], ALU.pow
                                   ).then_inc(rstd_ready, 1)

            norm_root(0)
            pool.wait_ge(hs_dve, 1)
            pool.wait_ge(hT_ps, 8)
            pool.memset(bd[:, :, :, :], 0.0).then_inc(bd_zero, 1)
            pool.wait_ge(bd_zero, 1)
            for w, src in enumerate((w_a, w_i)):
                for half in range(2):
                    pool.dma_start(bd[64 * half:64 * half + 64, w, :, 64 * half:64 * half + 64],
                                   src[0, half:2 * CB:2, :, :].rearrange("c i j -> i c j")).then_inc(bd_loaded, 16)
            for t in range(NT):
                pool.wait_ge(qms_ready, t + 1)
                pool.tensor_tensor(rqk[:, t, :], ssq[:, t, :], expo[:, :], ALU.pow).then_inc(qr_ready, 1)
            pool.memset(S[0][0:64, :, 0:64], NEG).then_inc(s_masked, 1)
            pool.wait_ge(msB_ready, 1)
            pool.tensor_tensor(rstd[:, 6:8], ss[:, 6:8], expo[:, 0:2], ALU.pow).then_inc(rB_ready, 1)
            pool.wait_ge(ysq_ready, 1)
            for c in range(CB):
                pool.tensor_scalar(gt[:, c, :], gt[:, c, :], prmT[:, 64 + c:65 + c], None, ALU.mult
                                   ).then_inc(yg_ready, 1)
            pool.wait_ge(msA_ready, 1)
            pool.tensor_tensor(rstd[:, 4:6], ss[:, 4:6], expo[:, 0:2], ALU.pow).then_inc(rA_ready, 1)
            pool.dma_start(wr[:, :, 0:GROUPS], w_rg[0].rearrange("(p k) g -> p k g", k=KD)).then_inc(wr_loaded, 16)
            pool.dma_start(wr[:, :, GROUPS:NL], w_re[0].rearrange("(p k) e -> p k e", k=KD)).then_inc(wr_loaded, 16)
            pool.dma_start(pp, p_v).then_inc(ple_loaded, 16)
            pool.dma_start(gple, g_ple.partition_broadcast(P).rearrange("p a d -> p (a d)")).then_inc(ple_loaded, 16)
            step(pool.memset(ones, 1.0))
            pool.affine_select(out=before, in_=ones, compare_op=ALU.is_gt, fill=0.0, base=0,
                               pattern=[[1, P]], channel_multiplier=-1).then_inc(route_consts, 1)
            pool.iota(slot_ids[:, :], [[1, SLOTS]], base=0, channel_multiplier=0,
                      allow_small_or_imprecise_dtypes=True).then_inc(route_consts, 1)
            pool.iota(idx[:, :], [[1, NE]], base=0, channel_multiplier=0,
                      allow_small_or_imprecise_dtypes=True).then_inc(route_consts, 1)
            pool.memset(rankm[:, :, NE:NE + 2], -1.0).then_inc(route_consts, 1)
            for t in range(NT):
                norm_root(1 + t, t, 1)
            pool.wait_ge(chunks_used, PLE)
            pool.memset(G[:, 1, :, :], 0.0).then_inc(g_ready, 1)
            pool.wait_ge(pe_raw, 8)
            pool.memset(Y[:, 1, :], 0.0).then_inc(y_ready, 4)
            pool.wait_ge(ple_loaded, 32)
            pool.wait_ge(xg_ready, 4)
            for n in range(4):
                for t in range(NT):
                    piece = pe[:, t, 512 * n:512 * n + 512]
                    pool.tensor_tensor(piece, piece, gple[:, 512 * n:512 * n + 512], ALU.mult).then_inc(pe_ready, 1)
            pool.wait_ge(msp_ready, 1)
            pool.tensor_tensor(r_ple[:, :], ss[:, 4:6], expo[:, 0:2], ALU.pow).then_inc(rp_ready, 1)
            pool.wait_ge(moe_done, 1)
            pool.dma_start(bpg, b_pg.partition_broadcast(P).rearrange("p a d -> p (a d)")).then_inc(bpg_loaded, 16)
            norm_root(3)

        @block.scalar
        def _(act):
            a_steps = [0]

            def step(ins):
                a_steps[0] += 1
                ins.then_inc(act_step, 1)
                act.wait_ge(act_step, a_steps[0])

            rows = [(conv_w[0], 32), (conv_b, 8), (b_a, 8), (b_i, 8), (lam, 8),
                    (g_out_lru, 8), (g_out_attn, 8), (g_mix, 16), (g_pg, 16)]
            at = 0
            for src, n in rows:
                view = src.rearrange("j (c p) -> (j c) p", p=P)
                act.dma_start(prm[at:at + n, :], view).then_inc(prm_loaded, 16)
                at += n
            def copy_hT(j):
                for b in range(0, 8, 2):
                    act.wait_ge(hT_ps, 8 * j + b + 1)
                    for u in range(2):
                        k = 2 * b + u
                        act.activation(hT[:, k, :], ps[:, b, T * u:T * u + T], ACT.Copy, scale=gain(j, k)
                                       ).then_inc(hT_act, 1)

            act.wait_ge(x_loaded[0], 16)
            act.activation(junk[:, 0, :], h[:, 0, :], ACT.Square, accum_out=ss[:, 0:1]).then_inc(ss_ready, 1)
            act.wait_ge(rstd_ready, 1)
            act.activation(hs_t[:, 0, :], h[:, 0, :], ACT.Copy, scale=rstd[:, 0:1]).then_inc(hs_act, 1)
            act.wait_ge(prm_ready, 1)
            copy_hT(0)
            act.dma_start(g_moe_pk[:, :], g_moe[0].rearrange("(p k) -> p k", k=KD)).then_inc(small_loaded, 16)
            act.dma_start(gqk[:, 0, :], g_q.partition_broadcast(P).rearrange("p a d -> p (a d)")).then_inc(small_loaded, 16)
            act.dma_start(gqk[:, 1, :], g_k.partition_broadcast(P).rearrange("p a d -> p (a d)")).then_inc(small_loaded, 16)
            act.dma_start(sink_bc[:, :], sinks.partition_broadcast(P).rearrange("p a d -> p (a d)")).then_inc(small_loaded, 16)
            act.dma_start(br_bc[:, 0:GROUPS], b_rg.partition_broadcast(P).rearrange("p a d -> p (a d)")).then_inc(small_loaded, 16)
            act.dma_start(br_bc[:, GROUPS:NL], b_re.partition_broadcast(P).rearrange("p a d -> p (a d)")).then_inc(small_loaded, 16)
            act.dma_start(pos_i[:, :], positions[0].rearrange("(t p) -> p t", p=P),
                          allow_slow_non_contiguous=True).then_inc(small_loaded, 16)
            act.wait_ge(lam_sum, 1)
            act.activation(sp[:, 1, :], sp[:, 0, :], ACT.Exp).then_inc(lam_exp, 1)
            act.wait_ge(lam_sum, 2)
            act.activation(sp[:, 3, :], sp[:, 2, :], ACT.Ln).then_inc(lam_ln, 1)
            act.wait_ge(ang_ready, 1)
            act.activation(trig[:, :, :, :], angles[:, 0:2, :, :], ACT.Sin).then_inc(trig_ready, 1)

            for g in range(2):
                act.wait_ge(chunks_used, 4 * (g + 1))
                for t in range(NT):
                    ins = act.activation(qk[:, t, 8 * g:8 * g + 8, :],
                                         ps[:, 2 + 2 * g + t, :].rearrange("p (h d) -> p h d", h=8), ACT.Copy)
                ins.then_inc(qkv_ready, 1)
            act.wait_ge(chunks_used, 4 * 3)
            act.wait_ge(xl_pad, 2)

            def kv_of(rows_, t, lo):
                return ps[rows_, 6 + t, lo:lo + 256].rearrange("p (h d) -> p h d", h=KV)

            for t in range(NT):
                ins = act.activation(qk[:, t, HEADS:QK, :], kv_of(slice(0, P), t, 0), ACT.Copy)
            ins.then_inc(qkv_ready, 1)
            act.wait_ge(qkv_ready, 3)
            for t in range(NT):
                act.activation(sqk[t], qk[:, t, :, :], ACT.Square).then_inc(qsq_ready, 1)
            for t in range(NT):
                act.activation(v[:, t, :, :], kv_of(slice(0, P), t, 256), ACT.Copy)
            act.activation(vs[64:128, 0, :, :], kv_of(slice(0, 64), 0, 256), ACT.Copy)
            act.activation(vs[0:64, 1, :, :], kv_of(slice(64, 128), 0, 256), ACT.Copy)
            act.activation(vs[64:128, 1, :, :], kv_of(slice(0, 64), 1, 256), ACT.Copy).then_inc(qkv_ready, 1)

            def copy_block(c):
                g, cb = divmod(c, 4)
                if cb < 3:
                    act.wait_ge(block_ps, 3 * g + cb + 1)
                else:
                    act.wait_ge(chunks_used, BLOCKS_FROM + 4 * (g + 1))
                if c < CB:
                    ins = act.activation(xl[:, c, 3:3 + T], ps[:, c % 2, 0:T], ACT.Copy)
                else:
                    ins = act.activation(gt[:, c - CB, :], ps[:, c % 2, 0:T], ACT.Gelu_apprx_tanh)
                ins.then_inc(block_copied, 1)

            def copy_qT(t):
                act.wait_ge(qT_ps, t + 1)
                for g in range(2):
                    ins = act.activation(qT[:, 4 * g:4 * g + 4, P * t:P * t + P],
                                         ps[:, 4 + g, :].rearrange("p (j q) -> p j q", j=4), ACT.Copy)
                ins.then_inc(qT_ready, 1)

            def copy_scores(t):
                act.wait_ge(scores_ps, t + 1)
                for b in range(4):
                    src = ps[:, 4 + b, :].rearrange("p (j k) -> p j k", j=4)
                    dst = S[t].rearrange("p (g j two) k -> p g two j k", g=2, two=2)[:, b // 2, b % 2, :, :]
                    if t == 0:
                        act.activation(dst[64:128], src[64:128], ACT.Copy, scale=HD ** -0.5)
                        ins = act.activation(dst[0:64, :, 64:128], src[0:64, :, 64:128], ACT.Copy, scale=HD ** -0.5)
                    else:
                        ins = act.activation(dst, src, ACT.Copy, scale=HD ** -0.5)
                ins.then_inc(S_ready, 1)

            def exponentials(t):
                act.wait_ge(shifted, t + 1)
                act.activation(S[t], S[t], ACT.Exp).then_inc(exp_ready, 1)
                act.wait_ge(sink_shifted, t + 1)
                act.activation(stat[:, 3 * t + 1, :], stat[:, 3 * t + 1, :], ACT.Exp).then_inc(sink_exp, 1)

            def copy_PT(t):
                act.wait_ge(PT_ps, t + 1)
                if t:
                    act.wait_ge(pv_ps, t)
                for b in range(2):
                    ins = act.activation(PT[:, 4 * b:4 * b + 4, :], ps[:, 4 + b, :].rearrange("p (j q) -> p j q", j=4), ACT.Copy)
                ins.then_inc(PT_act, 1)

            copy_block(0)
            copy_block(1)
            copy_block(2)
            copy_qT(0)
            copy_block(3)
            copy_qT(1)
            copy_block(4)
            copy_scores(0)
            copy_block(5)
            copy_scores(1)
            copy_block(6)
            exponentials(0)
            copy_block(7)
            exponentials(1)
            copy_block(8)
            copy_PT(0)
            copy_block(9)
            copy_block(10)
            copy_PT(1)
            copy_block(11)
            copy_block(12)
            for t in range(NT):
                act.wait_ge(yat_ready, t + 1)
                act.activation(junkB[:, t, :],
                               yat[:, t, :, :].rearrange("p h d -> p (h d)"), ACT.Square,
                               accum_out=ss[:, 6 + t:7 + t]).then_inc(ssB_ready, 1)
            act.wait_ge(yT_ps, 1)
            for c in range(4):
                act.activation(yT[:, c, :], ps[:, 4 + c // 2, T * (c % 2):T * (c % 2) + T], ACT.Copy,
                               scale=prmT[:, 72 + c:73 + c]).then_inc(yT_act, 1)
            copy_block(13)
            act.wait_ge(ssB_ready, 2)
            for c in range(CB):
                act.wait_ge(gates_ps, c + 1)
                act.activation(t1[:, c, :], ps[:, 4 + c % 4, 0:T], ACT.Sigmoid, bias=prmT[:, 40 + c:41 + c])
                act.activation(t2[:, c, :], ps[:, 4 + c % 4, T:2 * T], ACT.Sigmoid, bias=prmT[:, 48 + c:49 + c]
                               ).then_inc(gates_ready, 1)
            act.wait_ge(gates_ready, CB)
            act.wait_ge(lam_ready, 1)
            for c in range(CB):
                ins = act.activation(t1[:, c, :], t1[:, c, :], ACT.Tanh, scale=sp[:, 5, c:c + 1])
            ins.then_inc(tanh_ready, 1)
            copy_block(14)
            copy_block(15)
            act.wait_ge(recip_done, 1)
            act.activation(t1[:, :, :], t1[:, :, :], ACT.Sqrt).then_inc(sqrt_ready, 1)

            act.wait_ge(y_lru, 1)
            act.activation(t1[:, :, :], gt[:, :, :], ACT.Square).then_inc(ysq_ready, 1)

            def squares(t, n):
                act.wait_ge(h_ready, 4 * t + n + 1)
                act.activation(hs_t[:, t, 512 * n:512 * n + 512],
                               h[:, t, 512 * n:512 * n + 512], ACT.Square, accum_out=pieces[:, 0, t, n:n + 1]
                               ).then_inc(ss1_ready, 1)

            def scale_half(t):
                act.wait_ge(ss1_ready, 4 * (t + 1))
                act.wait_ge(rstd_ready, 2 + t)
                act.activation(hs[:, t, 0:8, :], h_by_k(t)[:, 0:8, :], ACT.Copy, scale=rstd[:, t:t + 1]).then_inc(hs_act, 1)

            def copy_xnT(t):
                for b in (0, 2):
                    act.wait_ge(xnT_ps, 4 * t + b + 1)
                    for k in range(4 * b, 4 * b + 4):
                        act.activation(hT[:, k, P * t:P * t + P], ps[:, XN_BANKS[b], P * (k % 4):P * (k % 4) + P], ACT.Copy,
                                       scale=g_moe_pk[:, k:k + 1]).then_inc(xnT_act, 1)

            for n in range(4):
                squares(0, n)
            scale_half(0)
            squares(1, 0)
            squares(1, 1)
            act.wait_ge(small_loaded, 16 * 7)
            copy_xnT(0)
            act.wait_ge(pT_ps, 1)
            act.activation(pT, ps[:, 1, :].rearrange("p (c t) -> p c t", c=2), ACT.Copy).then_inc(pT_ready, 1)
            squares(1, 2)
            squares(1, 3)
            scale_half(1)
            copy_xnT(1)
            def copy_ple(u):
                act.wait_ge(ple_ps, u + 1)
                if u >= 4:
                    act.wait_ge(pe_raw, u - 3)
                n, t = divmod(u, NT)
                act.activation(pe[:, t, 512 * n:512 * n + 512], ps[:, PLE_BANKS[u], :], ACT.Copy)
                act.activation(junkP[:, u % 4, :], ps[:, PLE_BANKS[u], :], ACT.Square,
                               accum_out=pieces[:, 1, t, n:n + 1]).then_inc(pe_raw, 1)

            for u in range(5):
                copy_ple(u)
            act.wait_ge(gmax_ready, 1)
            act.activation(lg[:, :, 0:GROUPS], lg[:, :, 0:GROUPS], ACT.Exp).then_inc(gexp_ready, 1)
            act.wait_ge(e_diff, 1)
            act.activation(rcol[:, 4, :], rcol[:, 3, :], ACT.Exp).then_inc(e_exp, 1)

            for u in range(5, 8):
                copy_ple(u)

            def expert_round(n0, p0):
                with act.Fori(0, PAIRS // 2) as i:
                    for b in range(2):
                        for e in range(2):
                            n = i * 4 + (n0 + 2 * b + e)
                            act.wait_ge(chunks_used, n * EXPERT_CHUNKS + (FRONT_CHUNKS + 8))
                            act.activation(H13, ps[:, 0, :].rearrange("p (m k) -> p k m", k=4), ACT.Copy).then_inc(h13_ready, 1)
                            act.wait_ge(h13T_ps, n + 1)
                            act.activation(SL, ps[:, 5, :].rearrange("p (k s) -> p k s", k=4)[:, :, 0:SLOTS], ACT.Silu
                                           ).then_inc(silu_ready, 1)
                            if e == 1:
                                act.wait_ge(g_ps, i * 2 + (p0 + b + 1))
                                act.activation(G[:, b, :, :], ps[:, 6, 0:T].rearrange("p (t q) -> p t q", t=NT), ACT.Copy
                                               ).then_inc(g_ready, 1)
                            act.wait_ge(chunks_used, n * EXPERT_CHUNKS + (FRONT_CHUNKS + EXPERT_CHUNKS))
                            for m in range(2):
                                for half in range(2):
                                    at = 1024 * m + 512 * half
                                    act.activation(Y[64 * e:64 * e + 64, b, at:at + 512],
                                                   ps[64 * half:64 * half + 64, 3 + m, :], ACT.Copy).then_inc(y_ready, 1)

            act.wait_ge(pe_ready, 8)
            expert_round(0, 0)
            act.wait_ge(rounds_ready, 1)
            rounds = act.value_load(rounds_i[0:1, 0:1], min_val=1, max_val=ROUNDS)
            with act.If(rounds > 1):
                with act.Fori(1, rounds) as r:
                    expert_round(r * NE, r * PAIRS)
                act.nop()
            with act.Else():
                act.nop()
            copy_hT(1)
            act.wait_ge(moe_done, 1)
            for t in range(NT):
                act.activation(hs_t[:, t, :], h[:, t, :], ACT.Square, accum_out=ss[:, t:t + 1]).then_inc(ss_ready, 1)
            for u in range(2 * 4):
                act.wait_ge(z_ready, u + 1)
                act.activation(z[:, u % 4, :], z[:, u % 4, :], ACT.Sigmoid).then_inc(gate_ready, 1)

        @block.vector
        def _(dve):
            steps = [0]

            def step(ins):
                steps[0] += 1
                ins.then_inc(dve_step, 1)
                dve.wait_ge(dve_step, steps[0])

            def copy_hT(j):
                for b in range(1, 8, 2):
                    dve.wait_ge(hT_ps, 8 * j + b + 1)
                    for u in range(2):
                        k = 2 * b + u
                        dve.tensor_scalar(hT[:, k, :], ps[:, b, T * u:T * u + T], gain(j, k), None,
                                          ALU.mult).then_inc(hT_dve, 1)

            def mean_squares(j, lo=0, n=NT):
                dve.tensor_scalar(ss[:, 2 + lo:2 + lo + n], ss[:, lo:lo + n], 1.0 / D, EPS, ALU.mult, ALU.add
                                  ).then_inc(ms_ready, 1)
                dve.wait_ge(rstd_ready, j + 1)

            dve.wait_ge(x_loaded[1], 16)
            step(dve.tensor_tensor_reduce(out=junk[:, 1, :], in0=h[:, 1, :], in1=h[:, 1, :], scale=1.0, scalar=0.0,
                                          op0=ALU.mult, op1=ALU.add, accum_out=ss[:, 1:2]))
            dve.wait_ge(ss_ready, 1)
            mean_squares(0)
            dve.tensor_scalar(hs_t[:, 1, :], h[:, 1, :], rstd[:, 1:2], None, ALU.mult).then_inc(hs_dve, 1)
            dve.wait_ge(prm_ps, 1)
            step(dve.tensor_copy(prmT[:, :], ps[:, 0, 0:112]))
            dve.tensor_scalar(sp[:, 4, :], prmT[:, 56:64], -1.0, 0.0, ALU.mult, ALU.max).then_inc(prm_ready, 1)
            dve.wait_ge(prm_ready, 1)
            step(dve.tensor_scalar(sp[:, 5, :], prmT[:, 56:64], 0.0, None, ALU.min))
            dve.scalar_tensor_tensor(out=sp[:, 0, :], in0=sp[:, 5, :], scalar=2.0, in1=prmT[:, 56:64],
                                     op0=ALU.mult, op1=ALU.subtract).then_inc(lam_sum, 1)
            copy_hT(0)
            dve.wait_ge(lam_exp, 1)
            dve.tensor_scalar(sp[:, 2, :], sp[:, 1, :], 1.0, None, ALU.add).then_inc(lam_sum, 1)
            dve.wait_ge(lam_sum, 2)
            dve.wait_ge(lam_ln, 1)
            step(dve.tensor_scalar(sp[:, 5, :], sp[:, 2, :], 1.0, None, ALU.is_equal))
            step(dve.scalar_tensor_tensor(out=sp[:, 2, :], in0=sp[:, 2, :], scalar=-1.0, in1=sp[:, 5, :],
                                          op0=ALU.add, op1=ALU.add))
            step(dve.reciprocal(sp[:, 2, :], sp[:, 2, :]))
            step(dve.tensor_tensor(sp[:, 3, :], sp[:, 3, :], sp[:, 2, :], ALU.mult))
            step(dve.tensor_tensor(sp[:, 3, :], sp[:, 3, :], sp[:, 5, :], ALU.add))
            step(dve.tensor_tensor(sp[:, 3, :], sp[:, 3, :], sp[:, 1, :], ALU.mult))
            step(dve.tensor_tensor(sp[:, 5, :], sp[:, 3, :], sp[:, 4, :], ALU.add))
            dve.tensor_scalar(sp[:, 5, :], sp[:, 5, :], 4.0, None, ALU.mult).then_inc(lam_ready, 1)
            dve.wait_ge(small_loaded, 16 * 7)
            step(dve.tensor_copy(rstd[:, 2:4], pos_i[:, :]))
            for f in range(HALF):
                ins = dve.tensor_scalar(angles[:, 2, :, f], rstd[:, 2:4],
                                        float(np.float32(THETA) ** np.float32(-2.0 * f / ROT)), None, ALU.mult)
            step(ins)
            step(dve.tensor_scalar(angles[:, 3, :, :], angles[:, 2, :, :], 1 / (2 * math.pi), None, ALU.mult))
            step(dve.tensor_scalar(angles[:, 3, :, :], angles[:, 3, :, :], ROUND_MAGIC, None, ALU.add))
            step(dve.tensor_scalar(angles[:, 3, :, :], angles[:, 3, :, :], -ROUND_MAGIC, None, ALU.add))
            for cpi in (TWO_PI_1, TWO_PI_2, TWO_PI_3, TWO_PI_4):
                step(dve.scalar_tensor_tensor(out=angles[:, 2, :, :], in0=angles[:, 3, :, :], scalar=-cpi,
                                              in1=angles[:, 2, :, :], op0=ALU.mult, op1=ALU.add))
            step(dve.tensor_scalar(angles[:, 0, :, :], angles[:, 2, :, :], PI_BELOW, -PI_BELOW, ALU.min, ALU.max))
            step(dve.scalar_tensor_tensor(out=angles[:, 4, :, :], in0=angles[:, 0, :, :], scalar=-1.0,
                                          in1=angles[:, 0, :, :], op0=ALU.mult, op1=ALU.max))
            dve.tensor_scalar(angles[:, 1, :, :], angles[:, 4, :, :], -1.0, math.pi / 2, ALU.mult, ALU.add
                              ).then_inc(ang_ready, 1)

            for t in range(NT):
                dve.wait_ge(qsq_ready, t + 1)
                step(dve.tensor_reduce(ssq[:, t, :], sqk[t], AX, ALU.add))
                dve.tensor_scalar(ssq[:, t, :], ssq[:, t, :], 1.0 / HD, EPS, ALU.mult, ALU.add).then_inc(qms_ready, 1)
                dve.wait_ge(qr_ready, t + 1)
                q_ = qk[:, t, :, :]
                step(dve.tensor_tensor(q_, q_, rqk[:, t, :].unsqueeze(2).to_broadcast([P, QK, HD]), ALU.mult))
                for w, (lo, n) in enumerate(((0, HEADS), (HEADS, KV))):
                    ins = dve.tensor_tensor(qk[:, t, lo:lo + n, :], qk[:, t, lo:lo + n, :],
                                            gqk[:, w, :].unsqueeze(1).to_broadcast([P, n, HD]), ALU.mult)
                step(ins)
                if t == 0:
                    dve.wait_ge(trig_ready, 1)
                sin = trig[:, 0, t, :].unsqueeze(1).to_broadcast([P, QK, HALF])
                cos = trig[:, 1, t, :].unsqueeze(1).to_broadcast([P, QK, HALF])
                a_, b_ = qk[:, t, :, 0:HALF], qk[:, t, :, HALF:ROT]
                dve.tensor_tensor(rope[:, 0, :, :], a_, cos, ALU.mult)
                dve.tensor_tensor(rope[:, 1, :, :], b_, sin, ALU.mult)
                dve.tensor_tensor(rope[:, 2, :, :], b_, cos, ALU.mult)
                step(dve.tensor_tensor(rope[:, 3, :, :], a_, sin, ALU.mult))
                dve.tensor_tensor(a_, rope[:, 0, :, :], rope[:, 1, :, :], ALU.subtract)
                dve.tensor_tensor(b_, rope[:, 2, :, :], rope[:, 3, :, :], ALU.add).then_inc(qk_ready, 1)
                dve.wait_ge(qk_ready, t + 1)

            for t in range(NT):
                dve.wait_ge(kT_ps, t + 1)
                dve.tensor_copy(kT[:, :, P * t:P * t + P], ps[:, 6 + t, :].rearrange("p (g q) -> p g q", g=KV)
                                ).then_inc(kT_ready, 1)
            def convolution(half):
                if half == 0:
                    dve.wait_ge(xl_pad, 1)
                dve.wait_ge(block_copied, 4 * (half + 1))
                for j in range(CONV_W):
                    for c in range(4 * half, 4 * half + 4):
                        tap = prmT[:, 8 * j + c:8 * j + c + 1]
                        if j == 0:
                            ins = dve.tensor_scalar(xc[:, c, :], xl[:, c, 0:T], tap, prmT[:, 32 + c:33 + c], ALU.mult, ALU.add)
                        else:
                            ins = dve.scalar_tensor_tensor(out=xc[:, c, :], in0=xl[:, c, j:j + T], scalar=tap,
                                                           in1=xc[:, c, :], op0=ALU.mult, op1=ALU.add)
                    if j < CONV_W - 1:
                        step(ins)
                ins.then_inc(xc_ready, 1)

            dve.wait_ge(s_masked, 1)
            for t in range(NT):
                dve.wait_ge(S_ready, t + 1)
                mx, sk = stat[:, 3 * t, :], stat[:, 3 * t + 1, :]
                step(dve.tensor_reduce(mx, S[t], AX, ALU.max))
                step(dve.tensor_tensor(mx, mx, sink_bc[:, :], ALU.max))
                dve.tensor_tensor(S[t], S[t], mx.unsqueeze(2).to_broadcast([P, HEADS, P]), ALU.subtract).then_inc(shifted, 1)
                dve.tensor_tensor(sk, sink_bc[:, :], mx, ALU.subtract).then_inc(sink_shifted, 1)
                convolution(t)
            for t in range(NT):
                den = stat[:, 3 * t + 2, :]
                dve.wait_ge(exp_ready, t + 1)
                step(dve.tensor_reduce(den, S[t], AX, ALU.add))
                dve.wait_ge(sink_exp, t + 1)
                step(dve.tensor_tensor(den, den, stat[:, 3 * t + 1, :], ALU.add))
                step(dve.reciprocal(den, den))
                dve.wait_ge(PT_ps, t + 1)
                if t:
                    dve.wait_ge(pv_ps, t)
                for b in range(2, 4):
                    ins = dve.tensor_copy(PT[:, 4 * b:4 * b + 4, :], ps[:, 4 + b, :].rearrange("p (j q) -> p j q", j=4))
                ins.then_inc(PT_dve, 1)
                dve.wait_ge(pv_ps, t + 1)
                for b in range(2):
                    ins = dve.tensor_tensor(yat[:, t, 8 * b:8 * b + 8, :],
                                            ps[:, 2 + b, :].rearrange("p (h d) -> p h d", h=8),
                                            den[:, 8 * b:8 * b + 8].unsqueeze(2).to_broadcast([P, 8, HD]), ALU.mult)
                ins.then_inc(yat_ready, 1)
            dve.wait_ge(yT_ps, 1)
            for c in range(4, CB):
                dve.tensor_scalar(yT[:, c, :], ps[:, 4 + c // 2, T * (c % 2):T * (c % 2) + T],
                                  prmT[:, 72 + c:73 + c], None, ALU.mult).then_inc(yT_dve, 1)
            dve.wait_ge(ssB_ready, 2)
            dve.tensor_scalar(ss[:, 6:8], ss[:, 6:8], 1.0 / (HEADS * HD), EPS, ALU.mult, ALU.add).then_inc(msB_ready, 1)

            dve.wait_ge(gates_ready, CB)
            dve.tensor_tensor(t2, t2, xc, ALU.mult)
            dve.wait_ge(tanh_ready, 1)
            step(dve.tensor_scalar(xl_flat, t1, 1.0, None, ALU.add))
            dve.reciprocal(xl_flat, xl_flat).then_inc(recip_done, 1)
            dve.wait_ge(recip_done, 1)
            dve.tensor_scalar(xc, xl_flat, 2.0, -1.0, ALU.mult, ALU.add)
            dve.wait_ge(sqrt_ready, 1)
            step(dve.scalar_tensor_tensor(out=xl_flat, in0=t1, scalar=2.0, in1=xl_flat, op0=ALU.mult, op1=ALU.mult))
            step(dve.tensor_tensor(t2, t2, xl_flat, ALU.mult))
            for c in range(CB):
                ins = dve.tensor_tensor_scan(xl_flat[:, c, :], xc[:, c, :], t2[:, c, :], 0.0, ALU.mult, ALU.add)
            step(ins)
            dve.wait_ge(block_copied, 2 * CB)
            dve.tensor_tensor(gt, gt, xl_flat, ALU.mult).then_inc(y_lru, 1)

            def add_w_out(bank, scale, t, n):
                piece = h[:, t, 512 * n:512 * n + 512]
                return dve.scalar_tensor_tensor(out=piece, in0=ps[:, bank, :], scalar=rstd[:, scale + t:scale + t + 1],
                                                in1=piece, op0=ALU.mult, op1=ALU.add)

            dve.wait_ge(rB_ready, 1)
            dve.wait_ge(hs_act, 1)
            for n in range(4):
                if n == 1:
                    dve.wait_ge(ysq_ready, 1)
                    dve.tensor_reduce(ysum, t1.rearrange("p c t -> p t c"), AX, ALU.add).then_inc(ysum_ready, 1)
                if n == 3:
                    dve.wait_ge(ssA_ps, 1)
                    dve.tensor_scalar(ss[:, 4:6], ps[:, 2, 0:NT], 1.0 / D_LRU, EPS, ALU.mult, ALU.add).then_inc(msA_ready, 1)
                dve.wait_ge(chunks_used, WOUT_B + 2 * (n + 1))
                for t in range(NT):
                    ins = add_w_out(B_BANKS[n] + t, 6, t, n)
                ins.then_inc(hB_ready, 1)

            dve.wait_ge(rA_ready, 1)
            dve.wait_ge(hB_ready, 4)

            def add_A(t, n):
                if t == 0:
                    dve.wait_ge(A_ps, n + 1)
                else:
                    dve.wait_ge(chunks_used, WOUT_A + 2 * (n + 1))
                add_w_out(A_BANKS[t][n], 4, t, n).then_inc(h_ready, 1)

            def scale_half(t):
                dve.wait_ge(ss1_ready, 4 * (t + 1))
                step(dve.tensor_reduce(ss[:, t:t + 1], pieces[:, 0, t, :], AX, ALU.add))
                mean_squares(1 + t, t, 1)
                dve.tensor_scalar(hs[:, t, 8:KD, :], h_by_k(t)[:, 8:KD, :], rstd[:, t:t + 1], None, ALU.mult
                                  ).then_inc(hs_dve, 1)

            def copy_xnT(t):
                for b in (1, 3):
                    dve.wait_ge(xnT_ps, 4 * t + b + 1)
                    dve.tensor_tensor(hT[:, 4 * b:4 * b + 4, P * t:P * t + P],
                                      ps[:, XN_BANKS[b], :].rearrange("p (k m) -> p k m", k=4),
                                      g_moe_pk[:, 4 * b:4 * b + 4].unsqueeze(2).to_broadcast([P, 4, P]), ALU.mult
                                      ).then_inc(xnT_dve, 1)

            for n in range(4):
                add_A(0, n)
            scale_half(0)
            add_A(1, 0)
            add_A(1, 1)
            copy_xnT(0)
            add_A(1, 2)
            add_A(1, 3)
            scale_half(1)
            copy_xnT(1)
            gl, el = lg[:, :, 0:GROUPS], route[:, 0, :, :]
            dve.wait_ge(route_consts, 4)
            dve.wait_ge(logits_ps, 2)
            for t in range(NT):
                ins = dve.tensor_tensor(lg[:, t, :], ps[:, 4 * (1 - t), 0:NL], br_bc[:, :], ALU.add)
            step(ins)

            def col(n):
                return rcol[:, n, :]

            def wide(c, n):
                return c.unsqueeze(2).to_broadcast([P, NT, n])

            def first_of(hot, logits, top, n, s0, s1):
                step(dve.tensor_tensor(hot, logits, wide(top, n), ALU.is_equal))
                ids = idx[:, 0:n].unsqueeze(1).to_broadcast([P, NT, n])
                step(dve.scalar_tensor_tensor(out=s0, in0=hot, scalar=-1000.0, in1=ids, op0=ALU.mult, op1=ALU.add))
                step(dve.tensor_reduce(s1, s0, AX, ALU.min))
                step(dve.tensor_tensor(hot, s0, wide(s1, n), ALU.is_equal))

            ghot = route[:, 1, :, 0:GROUPS]
            step(dve.tensor_reduce(col(0), gl, AX, ALU.max))
            first_of(ghot, gl, col(0), GROUPS, route[:, 2, :, 0:GROUPS], col(1))
            dve.tensor_tensor(gl, gl, wide(col(0), GROUPS), ALU.subtract).then_inc(gmax_ready, 1)
            gh = ghot.unsqueeze(3).to_broadcast([P, NT, GROUPS, PER_GROUP])

            def by_group(a):
                return a.rearrange("p t (g e) -> p t g e", g=GROUPS)

            for t in range(NT):
                ins = dve.tensor_tensor(by_group(el)[:, t], by_group(lg[:, :, GROUPS:NL])[:, t], gh[:, t], ALU.mult)
            step(ins)
            step(dve.tensor_scalar(route[:, 3, :, 0:GROUPS], ghot, -1.0, -NEG, ALU.add, ALU.mult))
            gn = route[:, 3, :, 0:GROUPS].unsqueeze(3).to_broadcast([P, NT, GROUPS, PER_GROUP])
            for t in range(NT):
                ins = dve.tensor_tensor(by_group(el)[:, t], by_group(el)[:, t], gn[:, t], ALU.add)
            step(ins)
            hot1, hot2 = route[:, 4, :, :], route[:, 5, :, :]
            step(dve.tensor_reduce(col(1), el, AX, ALU.max))
            first_of(hot1, el, col(1), NE, route[:, 6, :, :], col(5))
            step(dve.scalar_tensor_tensor(out=el, in0=hot1, scalar=10 * NEG, in1=el, op0=ALU.mult, op1=ALU.add))
            step(dve.tensor_reduce(col(2), el, AX, ALU.max))
            first_of(hot2, el, col(2), NE, route[:, 6, :, :], col(5))
            chosen = route[:, 7, :, :]
            dve.tensor_tensor(chosen, hot1, hot2, ALU.add).then_inc(chosen_ready, 1)
            dve.tensor_tensor(col(3), col(2), col(1), ALU.subtract).then_inc(e_diff, 1)
            dve.wait_ge(chosen_ready, 1)
            dve.wait_ge(rank_ps, 1)
            step(dve.scalar_tensor_tensor(out=route[:, 8, :, :], in0=ps[:, 2, 0:NT * NE].rearrange("p (t e) -> p t e", t=NT),
                                          scalar=1.0, in1=chosen, op0=ALU.add, op1=ALU.mult))
            dve.tensor_scalar(rankm[:, :, 0:NE], route[:, 8, :, :], -1.0, None, ALU.add)
            most = rcol[0:1, 8, 0:1]
            step(dve.tensor_reduce(most, ps[0:1, 2, NT * NE:NT * NE + NE], AX, ALU.max))
            def select(b, first):
                for e in range(2):
                    for t in range(NT):
                        ins = dve.tensor_scalar(SEL[:, b, t, SLOTS * e:SLOTS * e + SLOTS], slot_ids[:, :],
                                                rankm[:, t, first(e)], None, ALU.is_equal)
                ins.then_inc(sel_ready, 1)

            def spread(b, q, count):
                dve.wait_ge(gather_ps, count + 1)
                dve.tensor_tensor(XG[:, b, 4 * q:4 * q + 4, :], ps[:, 1 + q % 2, :].rearrange("p (k s) -> p k s", k=4),
                                  g_moe_pk[:, 4 * q:4 * q + 4].unsqueeze(2).to_broadcast([P, 4, P]), ALU.mult
                                  ).then_inc(xg_ready, 1)

            def accumulate(u, count, banks=(6, 7)):
                t, n = divmod(u, 4)
                dve.wait_ge(scatter_ps, count + (u + 1))
                piece = h[:, t, 512 * n:512 * n + 512]
                dve.tensor_tensor(piece, ps[:, banks[u % len(banks)], :], piece, ALU.add).then_inc(acc_done, 1)

            def first_pair(r):
                select(0, lambda e: slice(e, e + 1))
                for q in range(4):
                    spread(0, q, r * GATHERS + q)

            def expert_round(r):
                with dve.Fori(0, PAIRS // 2) as i:
                    for b in range(2):
                        pair = i * 2 + b
                        quarters = r * GATHERS + (pair + 1) * 4
                        units = r * SCATTERS + pair * 8
                        select(1 - b, lambda e: bass.ds(pair * 2 + (2 + e), 1))
                        accumulate(0, units)
                        for e in range(2):
                            for t in range(NT):
                                col_e = bass.ds(pair * 2 + e, 1)
                                ins = dve.tensor_scalar(SELW[:, t, SLOTS * e:SLOTS * e + SLOTS], slot_ids[:, :],
                                                        rankm[:, t, col_e], comb[:, t, col_e], ALU.is_equal, ALU.mult)
                        ins.then_inc(selw_ready, 1)
                        for e in range(2):
                            for u in range(1 if e == 0 else 4, 4 * e + 4):
                                accumulate(u, units)
                            spread(1 - b, 2 * e, quarters + 2 * e)
                            dve.wait_ge(silu_ready, r * NE + pair * 2 + (e + 1))
                            dve.tensor_tensor(HDN, SL, ps[:, 5, :].rearrange("p (k s) -> p k s", k=4)[:, :, SLOTS:2 * SLOTS],
                                              ALU.mult).then_inc(hdn_ready, 1)
                            spread(1 - b, 2 * e + 1, quarters + (2 * e + 1))
                for u in range(8):
                    accumulate(u, r * SCATTERS + PAIRS * 8, LAST_BANKS)

            first_pair(0)
            dve.wait_ge(gexp_ready, 1)
            step(dve.tensor_reduce(col(6), gl, AX, ALU.add))
            dve.wait_ge(e_exp, 1)
            step(dve.tensor_scalar(col(7), col(4), 1.0, None, ALU.add))
            step(dve.tensor_tensor(col(6), col(6), col(7), ALU.mult))
            step(dve.reciprocal(col(6), col(6)))
            step(dve.tensor_tensor(col(7), col(6), col(4), ALU.mult))
            step(dve.tensor_tensor(hot1, hot1, wide(col(6), NE), ALU.mult))
            step(dve.tensor_tensor(hot2, hot2, wide(col(7), NE), ALU.mult))
            dve.tensor_tensor(comb[:, :, :], hot1, hot2, ALU.add)
            cnt = rcol[0:1, 9, 0:1]
            step(dve.tensor_scalar(cnt, most, float(SLOTS), 1.0, ALU.is_gt, ALU.add))
            for r in range(2, ROUNDS):
                step(dve.scalar_tensor_tensor(out=cnt, in0=most, scalar=float(SLOTS * r), in1=cnt,
                                              op0=ALU.is_gt, op1=ALU.add))
            dve.tensor_copy(rounds_i[:, :], cnt).then_inc(rounds_ready, 1)

            dve.wait_ge(pe_raw, 8)
            step(dve.tensor_reduce(ss[:, 4:6], pieces[:, 1, :, :], AX, ALU.add))
            dve.tensor_scalar(ss[:, 4:6], ss[:, 4:6], 1.0 / D, EPS, ALU.mult, ALU.add).then_inc(msp_ready, 1)

            expert_round(0)
            dve.wait_ge(rounds_ready, 1)
            rounds = dve.value_load(rounds_i[0:1, 0:1], min_val=1, max_val=ROUNDS)
            with dve.If(rounds > 1):
                with dve.Fori(1, rounds) as r:
                    dve.tensor_scalar(slot_ids[:, :], slot_ids[:, :], float(SLOTS), None, ALU.add)
                    dve.memset(G[:, 1, :, :], 0.0).then_inc(g_ready, 1)
                    dve.wait_ge(g_ready, r * (PAIRS + 1) + 1)
                    first_pair(r)
                    expert_round(r)
                dve.nop()
            with dve.Else():
                dve.nop()
            dve.wait_ge(acc_done, rounds * SCATTERS)
            dve.nop().then_inc(moe_done, 1)

            copy_hT(1)
            dve.wait_ge(ss_ready, 3)
            mean_squares(3)
            dve.wait_ge(rp_ready, 1)
            dve.wait_ge(bpg_loaded, 16)

            def gate_in(u):
                n, t = divmod(u, NT)
                if n == 3 and t == 0:
                    dve.wait_ge(gate_ps, 1)
                else:
                    dve.wait_ge(tail_used, 4 * (n + 1))
                if u >= 4:
                    dve.wait_ge(out_stored[u % 4], 16)
                dve.scalar_tensor_tensor(out=z[:, u % 4, :], in0=ps[:, u, :], scalar=rstd[:, t:t + 1],
                                         in1=bpg[:, 512 * n:512 * n + 512], op0=ALU.mult, op1=ALU.add).then_inc(z_ready, 1)

            def gate_out(u):
                n, t = divmod(u, NT)
                dve.wait_ge(gate_ready, u + 1)
                step(dve.scalar_tensor_tensor(out=z[:, u % 4, :], in0=z[:, u % 4, :], scalar=r_ple[:, t:t + 1],
                                              in1=pe[:, t, 512 * n:512 * n + 512], op0=ALU.mult, op1=ALU.mult))
                dve.tensor_tensor(z[:, u % 4, :], z[:, u % 4, :], h[:, t, 512 * n:512 * n + 512], ALU.add).then_inc(out_ready, 1)

            for n in range(3):
                for t in range(NT):
                    gate_in(2 * n + t)
                for t in range(NT):
                    gate_out(2 * n + t)
            for t in range(NT):
                gate_in(6 + t)
                gate_out(6 + t)

        @block.tensor
        def _(pe_):
            mm = pe_.matmul
            pe_.wait_ge(consts_ready, 1)
            pe_.wait_ge(prm_loaded, 16 * 9)
            pe_.transpose(ps[:, 0, 0:112], prm[0:112, :], ident[0:112, 0:112]).then_inc(prm_ps, 1)

            def transpose_h(source):
                for b in range(8):
                    for u in range(2):
                        for t in range(NT):
                            ins = pe_.transpose(ps[:, b, T * u + P * t:T * u + P * t + P], source(t, 2 * b + u), ident[:, :])
                    ins.then_inc(hT_ps, 1)

            def copied(j, blocks):
                pe_.wait_ge(hT_act, 8 * j + 2 * blocks)
                pe_.wait_ge(hT_dve, 8 * j + 2 * blocks)

            pe_.wait_ge(hs_act, 1)
            pe_.wait_ge(hs_dve, 1)
            pe_.wait_ge(prm_ready, 1)
            transpose_h(lambda t, k: hs_t[:, t, P * k:P * k + P])

            def chunk(c):
                pe_.wait_ge(loaded[c % RING], 16 * (c // RING + 1))
                return ring4(c % RING)

            for g in range(3):
                for kq in range(4):
                    if g == 0:
                        copied(0, max(2, kq + 1))
                    w = chunk(4 * g + kq)
                    for kk in range(4):
                        k = 4 * kq + kk
                        for t in range(NT):
                            ins = mm(ps[:, 2 + 2 * g + t, :], hT[:, k, P * t:P * t + P], w[:, kk, :],
                                     start=(k == 0), stop=(k == KD - 1))
                    ins.then_inc(chunks_used, 1)

            def block_of(c):
                if c >= 2:
                    pe_.wait_ge(block_copied, c - 1)
                g, cb = divmod(c, 4)
                for kq in range(4):
                    w = chunk(BLOCKS_FROM + 4 * g + kq)
                    for kk in range(4):
                        k = 4 * kq + kk
                        ins = mm(ps[:, c % 2, 0:T], w[:, kk, P * cb:P * cb + P], hT[:, k, :],
                                 start=(k == 0), stop=(k == KD - 1))
                    if cb == 3:
                        ins.then_inc(chunks_used, 1)
                if cb < 3:
                    ins.then_inc(block_ps, 1)

            def turn_qk(t):
                pe_.wait_ge(qk_ready, t + 1)
                pe_.wait_ge(qkv_ready, 4)
                if t:
                    pe_.wait_ge(qT_ready, t)
                for j in range(CB):
                    ins = pe_.transpose(ps[:, 4 + j // 4, P * (j % 4):P * (j % 4) + P],
                                        qk[:, t, 2 * j:2 * j + 2, :].rearrange("p h d -> p (h d)"), ident[:, :])
                ins.then_inc(qT_ps, 1)
                for kh in range(KV):
                    for half in range(2):
                        ins = mm(ps[64 * half:64 * half + 64, 6 + t, P * kh:P * kh + P], qk[:, t, HEADS + kh, :],
                                 ident[:, :], start=True, stop=True)
                ins.then_inc(kT_ps, 1)

            def scores(t):
                pe_.wait_ge(qT_ready, 2)
                pe_.wait_ge(kT_ready, 2)
                if t:
                    pe_.wait_ge(S_ready, t)
                for j in range(CB):
                    for q in range(2):
                        n = 2 * t + q
                        lo = max(0, CHUNK * (n - 1))
                        hi = CHUNK * (n + 1)
                        for two in range(2):
                            hh = 2 * j + two
                            at = P * (j % 4) + P - (hi - lo)
                            ins = mm(ps[64 * q:64 * q + 64, 4 + 2 * (j // 4) + two, at:at + hi - lo],
                                     qT[64 * two:64 * two + 64, j, CHUNK * n:CHUNK * n + CHUNK],
                                     kT[64 * two:64 * two + 64, hh // 4, lo:hi], start=True, stop=True)
                ins.then_inc(scores_ps, 1)

            def turn_probs(t):
                pe_.wait_ge(S_ready, 2)
                pe_.wait_ge(exp_ready, t + 1)
                if t:
                    pe_.wait_ge(PT_act, t)
                    pe_.wait_ge(PT_dve, t)
                for hh in range(HEADS):
                    ins = pe_.transpose(ps[:, 4 + hh // 4, P * (hh % 4):P * (hh % 4) + P], S[t][:, hh, :], ident[:, :])
                ins.then_inc(PT_ps, 1)

            def values(t):
                pe_.wait_ge(PT_act, t + 1)
                pe_.wait_ge(PT_dve, t + 1)
                if t:
                    pe_.wait_ge(yat_ready, t)
                for hh in range(HEADS):
                    for q in range(2):
                        vals = (vs if q == 0 else v)[:, t, hh // 4, :]
                        ins = mm(ps[64 * q:64 * q + 64, 2 + hh // 8, HD * (hh % 8):HD * (hh % 8) + HD],
                                 PT[:, hh, 64 * q:64 * q + 64], vals, start=True, stop=True)
                ins.then_inc(pv_ps, 1)

            block_of(0)
            block_of(1)
            block_of(2)
            turn_qk(0)
            block_of(3)
            turn_qk(1)
            block_of(4)
            scores(0)
            block_of(5)
            scores(1)
            block_of(6)
            block_of(7)
            block_of(8)
            turn_probs(0)
            block_of(9)
            values(0)
            block_of(10)
            turn_probs(1)
            block_of(11)
            values(1)
            block_of(12)
            pe_.wait_ge(yat_ready, 2)
            for cb in range(CB):
                for t in range(NT):
                    at = T * (cb % 2) + P * t
                    ins = pe_.transpose(ps[:, 4 + cb // 2, at:at + P],
                                        yat[:, t, 2 * cb:2 * cb + 2, :].rearrange("p h d -> p (h d)"), ident[:, :])
            ins.then_inc(yT_ps, 1)
            block_of(13)
            pe_.wait_ge(xc_ready, 2)
            pe_.wait_ge(bd_loaded, 64)
            pe_.wait_ge(yT_act, 4)
            pe_.wait_ge(yT_dve, 4)
            for cb in range(CB):
                if cb >= 4:
                    pe_.wait_ge(gates_ready, cb - 3)
                for w in range(2):
                    ins = mm(ps[:, 4 + cb % 4, T * w:T * w + T], bd[:, w, cb, :], xc[:, cb, :], start=True, stop=True)
                ins.then_inc(gates_ps, 1)
            block_of(14)
            block_of(15)

            for n in range(4):
                if n == 1:
                    pe_.wait_ge(gates_ready, CB)
                if n == 3:
                    pe_.wait_ge(hB_ready, 1)
                    pe_.wait_ge(ysum_ready, 1)
                    for t in range(NT):
                        ins = mm(ps[:, 2, t:t + 1], ysum[:, P * t:P * t + P], ones_c[:, 0:1], start=True, stop=True)
                    ins.then_inc(ssA_ps, 1)
                    pe_.wait_ge(block_copied, 2 * CB)
                for cq in range(2):
                    w = chunk(WOUT_B + 2 * n + cq)
                    for kk in range(4):
                        cc = 4 * cq + kk
                        for t in range(NT):
                            ins = mm(ps[:, B_BANKS[n] + t, :], yT[:, cc, P * t:P * t + P], w[:, kk, :],
                                     start=(cc == 0), stop=(cc == CB - 1))
                    ins.then_inc(chunks_used, 1)


            def w_out_A(t, n):
                for cq in range(2):
                    w = chunk(WOUT_A + 2 * n + cq)
                    for kk in range(4):
                        cc = 4 * cq + kk
                        if t == 0 and n == 0:
                            pe_.wait_ge(yg_ready, cc + 1)
                        ins = mm(ps[:, A_BANKS[t][n], :], gt[:, cc, P * t:P * t + P], w[:, kk, :],
                                 start=(cc == 0), stop=(cc == CB - 1))
                    if t == NT - 1:
                        ins.then_inc(chunks_used, 1)
                if t == 0:
                    ins.then_inc(A_ps, 1)

            def turn_xn(t):
                pe_.wait_ge(hs_act, 2 + t)
                pe_.wait_ge(hs_dve, 2 + t)
                for b in range(4):
                    for u in range(4):
                        ins = pe_.transpose(ps[:, XN_BANKS[b], P * u:P * u + P], hs[:, t, 4 * b + u, :], ident[:, :])
                    ins.then_inc(xnT_ps, 1)

            def logits(t):
                pe_.wait_ge(xnT_act, 8 * (t + 1))
                pe_.wait_ge(xnT_dve, 2 * (t + 1))
                for k in range(KD):
                    ins = mm(ps[:, 4 * (1 - t), 0:NL], hT[:, k, P * t:P * t + P], wr[:, k, :],
                             start=(k == 0), stop=(k == KD - 1))
                ins.then_inc(logits_ps, 1)

            def ple_unit(u):
                n, t = divmod(u, NT)
                for cc in range(2):
                    if u == 0:
                        chunk(PLE + cc)
                    ins = mm(ps[:, PLE_BANKS[u], :], pT[:, cc, P * t:P * t + P],
                             ring[:, (PLE + cc) % RING, 512 * n:512 * n + 512], start=(cc == 0), stop=(cc == 1))
                ins.then_inc(ple_ps, 1)

            for n in range(4):
                pe_.wait_ge(hB_ready, 1 if n == 0 else 2)
                if n == 3:
                    pe_.wait_ge(msA_ready, 1)
                w_out_A(0, n)
            for n in range(4):
                pe_.wait_ge(hB_ready, 3 if n < 2 else 4)
                if n == 2:
                    turn_xn(0)
                    pe_.wait_ge(ple_loaded, 32)
                    for cc in range(2):
                        for t in range(NT):
                            ins = pe_.transpose(ps[:, 1, T * cc + P * t:T * cc + P * t + P], pp[:, t, P * cc:P * cc + P], ident[:, :])
                    ins.then_inc(pT_ps, 1)
                if n == 3:
                    pe_.wait_ge(pT_ready, 1)
                w_out_A(1, n)
            pe_.wait_ge(wr_loaded, 32)
            pe_.wait_ge(h_ready, 6)
            logits(0)
            ple_unit(0)
            turn_xn(1)
            ple_unit(1)
            logits(1)
            for u in range(2, 5):
                ple_unit(u)
            pe_.wait_ge(chosen_ready, 1)
            pe_.wait_ge(route_consts, 4)
            mm(ps[:, 2, 0:NE], before, route[:, 7, 0, :], start=True, stop=True)
            mm(ps[:, 2, NE:2 * NE], ones, route[:, 7, 0, :], start=True, stop=False)
            mm(ps[:, 2, NE:2 * NE], before, route[:, 7, 1, :], start=False, stop=True)
            for t in range(NT):
                ins = mm(ps[0:1, 2, 2 * NE:3 * NE], ones[:, 0:1], route[:, 7, t, :], start=(t == 0), stop=(t == NT - 1))
            ins.then_inc(rank_ps, 1)
            pe_.wait_ge(pe_raw, 2)
            for u in range(5, 8):
                ple_unit(u)
            pe_.wait_ge(ple_ps, 8)
            pe_.nop().then_inc(chunks_used, 2)

            def gather(b, q):
                for k in range(4 * q, 4 * q + 4):
                    for t in range(NT):
                        ins = mm(ps[:, 1 + q % 2, P * (k % 4):P * (k % 4) + P], hs[:, t, k, :], SEL[:, b, t, :],
                                 start=(t == 0), stop=(t == NT - 1))
                ins.then_inc(gather_ps, 1)

            def scatter(b, u, count, banks=(6, 7)):
                t, n = divmod(u, 4)
                if u >= len(banks):
                    pe_.wait_ge(acc_done, count + (u + 1 - len(banks)))
                mm(ps[:, banks[u % len(banks)], :], G[:, b, t, :], Y[:, b, 512 * n:512 * n + 512], start=True, stop=True
                   ).then_inc(scatter_ps, 1)

            def pair_of(r, i, b, begins=False):
                pair = i * 2 + b
                quarters = r * GATHERS + pair * 4
                units = r * SCATTERS + pair * 8
                pe_.wait_ge(g_ready, r * (PAIRS + 1) + pair + 1)
                pe_.wait_ge(y_ready, (r * NE + pair * 2 + 1) * 4)
                for e in range(2):
                    n = r * NE + pair * 2 + e

                    def arrived(j):
                        if begins and e == 1 and j < AHEAD:
                            pe_.wait_ge(ahead_loaded[j], 16)
                            return hT_flat[:, CH * j:CH * j + CH]
                        ahead = 0 if begins and e == 0 else AHEAD
                        slot = slot_of(j, ahead)
                        pe_.wait_ge(loaded[slot], n * 16 + 16 * ((FRONT_CHUNKS - ahead + j) // RING + 1))
                        return ring[:, slot, :]

                    for kq in range(4):
                        if e == 0:
                            pe_.wait_ge(xg_ready, quarters + (kq + 1))
                        if begins and e == 0 and kq < 2:
                            gather(0, 2 + kq)
                        s1, s3 = arrived(2 * kq), arrived(2 * kq + 1)
                        for kk in range(4):
                            k = 4 * kq + kk
                            for half, s in ((0, s1), (1, s3)):
                                ins = mm(ps[64 * half:64 * half + 64, 0, :], XG[:, b, k, SLOTS * e:SLOTS * e + SLOTS],
                                         s[:, D_EXP * kk:D_EXP * kk + D_EXP], start=(k == 0), stop=(k == KD - 1))
                                if kk == 3:
                                    ins.then_inc(chunks_used, 1)
                        scatter(1 - b, 4 * e + kq, units)
                    if e == 0:
                        pe_.wait_ge(sel_ready, r * (PAIRS + 1) + pair + 2)
                    else:
                        pe_.wait_ge(xg_ready, quarters + 5)
                    gather(1 - b, 2 * e)
                    pe_.wait_ge(h13_ready, n + 1)
                    for k in range(4):
                        ins = pe_.transpose(ps[:, 5, P * k:P * k + P], H13[:, k, :], ident[:, :])
                    ins.then_inc(h13T_ps, 1)
                    if e == 1:
                        pe_.wait_ge(xg_ready, quarters + 6)
                    gather(1 - b, 2 * e + 1)
                    if e == 1:
                        pe_.wait_ge(selw_ready, r * PAIRS + pair + 1)
                        pe_.wait_ge(acc_done, units + 7)
                        for t in range(NT):
                            ins = pe_.transpose(ps[:, 6, P * t:P * t + P], SELW[:, t, :], ident[:, :])
                        ins.then_inc(g_ps, 1)
                        pe_.wait_ge(y_ready, (n + 1) * 4)
                    pe_.wait_ge(hdn_ready, n + 1)
                    for k in range(4):
                        s = arrived(8 + k)
                        for m in range(2):
                            for half in range(2):
                                at = 1024 * m + 512 * half
                                ins = mm(ps[64 * half:64 * half + 64, 3 + m, :], HDN[:, k, :], s[:, at:at + 512],
                                         start=(k == 0), stop=(k == 3))
                        ins.then_inc(chunks_used, 1)

            def expert_round(r, first=False):
                pe_.wait_ge(sel_ready, r * (PAIRS + 1) + 1)
                for q in range(2 if first else 4):
                    if q >= 2:
                        pe_.wait_ge(xg_ready, r * GATHERS + (q - 1))
                    gather(0, q)
                pe_.wait_ge(pe_raw, 8)
                if first:
                    for b in range(2):
                        pair_of(0, 0, b, begins=(b == 0))
                with pe_.Fori(1 if first else 0, PAIRS // 2) as i:
                    for b in range(2):
                        pair_of(r, i, b)
                pe_.wait_ge(g_ready, r * (PAIRS + 1) + (PAIRS + 1))
                pe_.wait_ge(xg_ready, r * GATHERS + GATHERS)
                for u in range(8):
                    if u < 4:
                        pe_.wait_ge(y_ready, r * (4 * NE) + (4 * NE + u + 1))
                    scatter(1, u, r * SCATTERS + PAIRS * 8, LAST_BANKS)

            expert_round(0, first=True)
            pe_.wait_ge(rounds_ready, 1)
            rounds = pe_.value_load(rounds_i[0:1, 0:1], min_val=1, max_val=ROUNDS)
            with pe_.If(rounds > 1):
                with pe_.Fori(1, rounds) as r:
                    expert_round(r)
                pe_.nop()
            with pe_.Else():
                pe_.nop()

            pe_.wait_ge(moe_done, 1)
            transpose_h(lambda t, k: h[:, t, P * k:P * k + P])

            def gate_columns(n, kq, tiles):
                c = 4 * n + kq
                slot = slot_of(c)
                copied(1, kq + 1 if n == 0 else 4)
                pe_.wait_ge(tail_loaded[slot], 16 * (c // RING + 1))
                for kk in range(4):
                    k = 4 * kq + kk
                    for t in tiles:
                        ins = mm(ps[:, 2 * n + t, :], hT[:, k, P * t:P * t + P], ring4(slot)[:, kk, :],
                                 start=(k == 0), stop=(k == KD - 1))
                return ins

            for n in range(3):
                for kq in range(4):
                    gate_columns(n, kq, range(NT)).then_inc(tail_used, 1)
            for kq in range(4):
                ins = gate_columns(3, kq, (0,))
            ins.then_inc(gate_ps, 1)
            for kq in range(4):
                gate_columns(3, kq, (1,)).then_inc(tail_used, 1)


NAMES = ["x", "p", "positions", "g_mix", "w_in", "conv_w", "conv_b", "w_a", "b_a", "w_i", "b_i", "lam", "g_q", "g_k",
         "sinks", "g_out_lru", "g_out_attn", "w_out", "g_moe", "w_rg", "b_rg", "w_re", "b_re", "w1", "w3", "w2",
         "w_ple", "g_ple", "g_pg", "w_pg", "b_pg"]


def kernel(**inputs):
    import numpy as _np
    import concourse.bacc as _bacc
    from concourse import mybir as _mybir
    from concourse.bass_utils import run_bass_kernel_spmd as _run

    nc = _bacc.Bacc("TRN2", target_bir_lowering=False, num_devices=1)
    arrays, args = {}, {}
    for name in NAMES:
        a = _np.ascontiguousarray(inputs[name])
        arrays[f"in_{name}"] = a
        args[name] = nc.dram_tensor(f"in_{name}", a.shape, _mybir.dt.from_np(a.dtype), kind="ExternalInput").ap()
    args["out"] = nc.dram_tensor("out_h", (1, T, D), _mybir.dt.float32, kind="ExternalOutput").ap()
    build(nc, **args)
    got = _run(nc, [arrays], core_ids=[0])
    return got.results[0]["out_h"]
```
